# Optimizing a Trainium2 kernel written in Bass

```python
import math
import jax
import jax.numpy as jnp
from jax import lax
import numpy as np

D_MODEL = 1024
BATCH = 1
SEQ = 256
DEPTH = 2

GRID_W = 64
CTX_LEN = 256
HEAD_DIM = 64
MIX_WIDTH = D_MODEL
RET_WIDTH = MIX_WIDTH // 4
SSD_WIDTH = MIX_WIDTH // 2
NA_WIDTH = MIX_WIDTH - RET_WIDTH - SSD_WIDTH
RET_HEADS = RET_WIDTH // HEAD_DIM
RET_DK = HEAD_DIM
SSD_HEADS = SSD_WIDTH // HEAD_DIM
SSD_HEADDIM = HEAD_DIM
SSD_GROUPS = 2
SSD_STATE = 64
SSD_CONV = 3
NA_HEADS = NA_WIDTH // HEAD_DIM
NA_WIN_ROWS = 8
NA_WIN_COLS = 16
NA_QBLOCK_COLS = 16
NA_KEY_COLS = NA_QBLOCK_COLS + NA_WIN_COLS
SCAN_CHUNK = 128
N_EXPERTS = 16
N_GROUPS = 4
EXPERTS_PER_GROUP = N_EXPERTS // N_GROUPS
TOP_K = 2
D_EXPERT = D_MODEL // 2
ROPE_BASE = 10000.0
EPS = 1e-6

SEGMENTS = (
    ("ret_q", RET_WIDTH), ("ret_k", RET_WIDTH), ("ret_v", RET_WIDTH), ("ret_g", RET_WIDTH),
    ("ssd_z", SSD_WIDTH), ("ssd_x", SSD_WIDTH), ("ssd_b", SSD_GROUPS * SSD_STATE),
    ("ssd_c", SSD_GROUPS * SSD_STATE), ("ssd_dt", 2 * SSD_HEADS),
    ("na_q", NA_WIDTH), ("na_k", NA_WIDTH), ("na_v", NA_WIDTH),
)
IN_COLS = 4 * RET_WIDTH + 2 * SSD_WIDTH + 2 * SSD_GROUPS * SSD_STATE + 2 * SSD_HEADS + 3 * NA_WIDTH
SSD_XBC = SSD_WIDTH + 2 * SSD_GROUPS * SSD_STATE
SSD_XB = SSD_WIDTH + SSD_GROUPS * SSD_STATE

kernel_name = "hybrid_prefix_retention_ssd_natten_moe"

def _offsets():
    off, start = {}, 0
    for name, width in SEGMENTS:
        off[name] = (start, start + width)
        start += width
    return off

def _segment_getter(h, w_in, full):
    off = _offsets()
    if full:
        u = h @ w_in
        return lambda a, b=None: u[..., off[a][0]:off[b or a][1]]
    return lambda a, b=None: h @ w_in[:, off[a][0]:off[b or a][1]]

def rmsnorm(t, w):
    t32 = t.astype(jnp.float32)
    y = t32 * lax.rsqrt(jnp.mean(t32 * t32, axis=-1, keepdims=True) + EPS) * w.astype(jnp.float32)
    return y.astype(t.dtype)

def modulate(h, shift, scale):
    return h * (1 + scale) + shift

def head_groupnorm(y):
    y = y.astype(jnp.float32)
    mu = jnp.mean(y, axis=-1, keepdims=True)
    var = jnp.mean(jnp.square(y - mu), axis=-1, keepdims=True)
    return (y - mu) * lax.rsqrt(var + EPS)

def axial_rope_tables(n_tokens):
    t = jnp.arange(n_tokens)
    pos = jnp.stack([t // GRID_W, t % GRID_W], axis=-1).astype(jnp.float32)
    n_freq = RET_DK // 4
    inv = 1.0 / (ROPE_BASE ** (jnp.arange(n_freq, dtype=jnp.float32) / n_freq))
    ang = pos[:, :, None] * inv
    return jnp.cos(ang), jnp.sin(ang)

def apply_axial_rope(t, cos, sin):
    b_, l_, h_, dk = t.shape
    tr = t.reshape(b_, l_, h_, 2, 2, dk // 4).astype(jnp.float32)
    x1, x2 = tr[..., 0, :], tr[..., 1, :]
    cs, sn = cos[None, :, None], sin[None, :, None]
    out = jnp.stack([x1 * cs - x2 * sn, x2 * cs + x1 * sn], axis=-2)
    return out.reshape(t.shape).astype(t.dtype)

def depthwise_conv(t, w, b):
    k = w.shape[0]
    y = lax.conv_general_dilated(
        t, w.astype(t.dtype)[:, None, :], window_strides=(1,), padding=[(k // 2, k // 2)],
        dimension_numbers=("NWC", "WIO", "NWC"), feature_group_count=t.shape[-1])
    return y + b.astype(t.dtype)

def chunk_scan(q, k, v, a, s0):
    bsz, seq, g, n = q.shape
    r, p = v.shape[3], v.shape[4]
    nc = seq // SCAN_CHUNK
    qc = q.reshape(bsz, nc, SCAN_CHUNK, g, n)
    kc = k.reshape(bsz, nc, SCAN_CHUNK, g, n)
    vc = v.reshape(bsz, nc, SCAN_CHUNK, g, r, p)
    acum = jnp.cumsum(a.astype(jnp.float32).reshape(bsz, nc, SCAN_CHUNK, g, r), axis=2)
    tril = jnp.tril(jnp.ones((SCAN_CHUNK, SCAN_CHUNK), dtype=bool))[None, None, :, :, None, None]
    seg = acum[:, :, :, None] - acum[:, :, None, :]
    decay = jnp.exp(jnp.where(tril, seg, -jnp.inf))
    scores = jnp.einsum("bclgn,bcsgn->bclsg", qc, kc)
    y_diag = jnp.einsum("bclsgr,bcsgrp->bclgrp", scores[..., None] * decay, vc)
    w_end = jnp.exp(acum[:, :, -1:] - acum)
    states = jnp.einsum("bcsgn,bcsgrp->bcgrpn", kc, vc * w_end[..., None])
    chunk_decay = jnp.exp(acum[:, :, -1])
    if s0 is None:
        s0 = jnp.zeros((bsz, g, r, p, n), jnp.float32)

    def step(h, inp):
        st, dc = inp
        return h * dc[..., None, None] + st, h

    s_final, h_prev = lax.scan(step, s0.astype(jnp.float32),
                               (jnp.moveaxis(states, 1, 0), jnp.moveaxis(chunk_decay, 1, 0)))
    h_prev = jnp.moveaxis(h_prev, 0, 1)
    y_off = jnp.einsum("bclgn,bcgrpn->bclgrp", qc, h_prev) * jnp.exp(acum)[..., None]
    return (y_diag + y_off).reshape(bsz, seq, g, r, p), s_final

def final_state(k, v, a):
    acum = jnp.cumsum(a.astype(jnp.float32), axis=1)
    w = jnp.exp(acum[:, -1:] - acum)
    return jnp.einsum("blgn,blgrp->bgrpn", k, v * w[..., None])

def _flip(t):
    return None if t is None else jnp.flip(t, axis=1)

def prefix_scan(q_c, k_c, v_c, a_c, q_l, k_l, v_l, a_l, need_ctx, reverse):
    if reverse:
        q_c, k_c, v_c, a_c = _flip(q_c), _flip(k_c), _flip(v_c), _flip(a_c)
        q_l, k_l, v_l, a_l = _flip(q_l), _flip(k_l), _flip(v_l), _flip(a_l)
    if need_ctx:
        y_c, s_c = chunk_scan(q_c, k_c, v_c, a_c, None)
    else:
        y_c, s_c = None, final_state(k_c, v_c, a_c)
    y_l, _ = chunk_scan(q_l, k_l, v_l, a_l, s_c)
    if reverse:
        y_c, y_l = _flip(y_c), _flip(y_l)
    return y_c, y_l

def retention_group(get_l, get_c, decay_f, decay_b, cos, sin, need_ctx):
    heads = lambda t: t.reshape(t.shape[0], t.shape[1], RET_HEADS, RET_DK)
    k_scale = RET_DK ** -0.5
    q_l = apply_axial_rope(heads(get_l("ret_q")), cos, sin)
    k_l = apply_axial_rope(heads(get_l("ret_k")), cos, sin) * k_scale
    v_l = heads(get_l("ret_v"))[:, :, :, None, :]
    k_c = heads(get_c("ret_k")) * k_scale
    v_c = heads(get_c("ret_v"))[:, :, :, None, :]
    q_c = heads(get_c("ret_q")) if need_ctx else None
    y_l, y_c = 0.0, 0.0
    for param, reverse in ((decay_f, False), (decay_b, True)):
        log_gamma = -jnp.exp(param.astype(jnp.float32))[:, None]
        a_l = jnp.broadcast_to(log_gamma, q_l.shape[:2] + log_gamma.shape)
        a_c = jnp.broadcast_to(log_gamma, k_c.shape[:2] + log_gamma.shape)
        yc, yl = prefix_scan(q_c, k_c, v_c, a_c, q_l, k_l, v_l, a_l, need_ctx, reverse)
        y_l = y_l + yl
        if need_ctx:
            y_c = y_c + yc

    def finish(y, g):
        y = head_groupnorm(y[:, :, :, 0, :]).reshape(g.shape)
        return (y * jax.nn.silu(g.astype(jnp.float32))).astype(g.dtype)

    out_l = finish(y_l, get_l("ret_g"))
    out_c = finish(y_c, get_c("ret_g")) if need_ctx else None
    return out_l, out_c

def ssd_group(get_l, get_c, conv_w, conv_b, dtb_f, dtb_b, alog_f, alog_b, d_skip, norm_w, need_ctx):
    def split_xbc(t):
        x = t[..., :SSD_WIDTH]
        b = t[..., SSD_WIDTH:SSD_XB]
        c = t[..., SSD_XB:] if t.shape[-1] == SSD_XBC else None
        return x, b, c

    x_l, b_l, c_l = split_xbc(jax.nn.silu(depthwise_conv(get_l("ssd_x", "ssd_c"), conv_w, conv_b)))
    if need_ctx:
        xbc_c = jax.nn.silu(depthwise_conv(get_c("ssd_x", "ssd_c"), conv_w, conv_b))
    else:
        xbc_c = jax.nn.silu(depthwise_conv(get_c("ssd_x", "ssd_b"), conv_w[:, :SSD_XB], conv_b[:SSD_XB]))
    x_c, b_c, c_c = split_xbc(xbc_c)
    dt_l, dt_c = get_l("ssd_dt"), get_c("ssd_dt")
    rep = SSD_HEADS // SSD_GROUPS
    grp = lambda t: None if t is None else t.reshape(t.shape[0], t.shape[1], SSD_GROUPS, SSD_STATE)
    y_l, y_c = 0.0, 0.0
    for d, (dtb, alog, reverse) in enumerate(((dtb_f, alog_f, False), (dtb_b, alog_b, True))):
        a_coef = -jnp.exp(alog.astype(jnp.float32))

        def prep(x, dt_raw):
            bsz, seq = x.shape[:2]
            dt = jax.nn.softplus(dt_raw[..., d * SSD_HEADS:(d + 1) * SSD_HEADS].astype(jnp.float32)
                                 + dtb.astype(jnp.float32))
            a = (dt * a_coef).reshape(bsz, seq, SSD_GROUPS, rep)
            v = x.reshape(bsz, seq, SSD_GROUPS, rep, SSD_HEADDIM) * dt.reshape(bsz, seq, SSD_GROUPS, rep)[..., None]
            return v, a

        v_l, a_l = prep(x_l, dt_l)
        v_c, a_c = prep(x_c, dt_c)
        yc, yl = prefix_scan(grp(c_c), grp(b_c), v_c, a_c, grp(c_l), grp(b_l), v_l, a_l, need_ctx, reverse)
        y_l = y_l + yl
        if need_ctx:
            y_c = y_c + yc

    def finish(y, x, z):
        bsz, seq = x.shape[:2]
        xh = x.reshape(bsz, seq, SSD_HEADS, SSD_HEADDIM).astype(jnp.float32)
        y = y.reshape(bsz, seq, SSD_HEADS, SSD_HEADDIM) + d_skip.astype(jnp.float32)[:, None] * xh
        y = y.reshape(bsz, seq, SSD_WIDTH) * jax.nn.silu(z.astype(jnp.float32))
        return rmsnorm(y, norm_w).astype(z.dtype)

    out_l = finish(y_l, x_l, get_l("ssd_z"))
    out_c = finish(y_c, x_c, get_c("ssd_z")) if need_ctx else None
    return out_l, out_c

def _na_column_tables():
    ncb = GRID_W // NA_QBLOCK_COLS
    c0 = np.arange(ncb) * NA_QBLOCK_COLS
    kc0 = np.clip(c0 - NA_WIN_COLS // 2, 0, GRID_W - NA_KEY_COLS)
    col_idx = kc0[:, None] + np.arange(NA_KEY_COLS)[None]
    qcol = c0[:, None] + np.arange(NA_QBLOCK_COLS)[None]
    cs = np.clip(qcol - NA_WIN_COLS // 2, 0, GRID_W - NA_WIN_COLS)[..., None]
    kcol = col_idx[:, None, :]
    mask = (kcol >= cs) & (kcol < cs + NA_WIN_COLS)
    dc = np.clip(kcol - qcol[..., None] + NA_WIN_COLS - 1, 0, 2 * NA_WIN_COLS - 2)
    return col_idx, dc, mask

def neighbourhood_attention(q, k, v, k_ctx, v_ctx, rpb, rows):
    bsz, seq, nh, d = q.shape
    wr = min(NA_WIN_ROWS, rows)
    col_idx, dc_idx, col_mask = _na_column_tables()
    ncb = col_idx.shape[0]
    scale = d ** -0.5
    qg = jnp.moveaxis(q.reshape(bsz, rows, ncb, NA_QBLOCK_COLS, nh, d), 1, 0)
    kg = k.reshape(bsz, rows, GRID_W, nh, d)[:, :, col_idx]
    vg = v.reshape(bsz, rows, GRID_W, nh, d)[:, :, col_idx]
    mask = jnp.asarray(col_mask)[:, :, None, :]
    n_lat_keys = wr * NA_KEY_COLS

    def one_row(args):
        q_r, r = args
        r0 = jnp.clip(r - wr // 2, 0, rows - wr)
        k_win = lax.dynamic_slice_in_dim(kg, r0, wr, axis=1)
        v_win = lax.dynamic_slice_in_dim(vg, r0, wr, axis=1)
        dr = r0 + jnp.arange(wr) - r + (NA_WIN_ROWS - 1)
        bias = rpb[:, dr[:, None, None, None], dc_idx[None]]
        bias = jnp.transpose(bias, (0, 2, 3, 1, 4)).astype(jnp.float32)
        s_lat = jnp.einsum("bjqhd,bijkhd->bhjqik", q_r, k_win).astype(jnp.float32) * scale + bias
        s_lat = jnp.where(mask, s_lat, -jnp.inf)
        s_ctx = jnp.einsum("bjqhd,bmhd->bhjqm", q_r, k_ctx).astype(jnp.float32) * scale
        s = jnp.concatenate([s_lat.reshape(bsz, nh, ncb, NA_QBLOCK_COLS, n_lat_keys), s_ctx], axis=-1)
        prob = jax.nn.softmax(s, axis=-1)
        p_lat = prob[..., :n_lat_keys].reshape(s_lat.shape).astype(v.dtype)
        p_ctx = prob[..., n_lat_keys:].astype(v.dtype)
        return (jnp.einsum("bhjqik,bijkhd->bjqhd", p_lat, v_win)
                + jnp.einsum("bhjqm,bmhd->bjqhd", p_ctx, v_ctx))

    o = lax.map(one_row, (qg, jnp.arange(rows)))
    return jnp.moveaxis(o, 0, 1).reshape(bsz, seq, nh * d)

def context_attention(q, k, v):
    s = jnp.einsum("bqhd,bkhd->bhqk", q, k).astype(jnp.float32) * q.shape[-1] ** -0.5
    prob = jax.nn.softmax(s, axis=-1).astype(v.dtype)
    o = jnp.einsum("bhqk,bkhd->bqhd", prob, v)
    return o.reshape(o.shape[0], o.shape[1], -1)

def na_group(get_l, get_c, q_norm, k_norm, rpb, rows, need_ctx):
    heads = lambda t: t.reshape(t.shape[0], t.shape[1], NA_HEADS, HEAD_DIM)
    q_l = rmsnorm(heads(get_l("na_q")), q_norm)
    k_l = rmsnorm(heads(get_l("na_k")), k_norm)
    v_l = heads(get_l("na_v"))
    k_c = rmsnorm(heads(get_c("na_k")), k_norm)
    v_c = heads(get_c("na_v"))
    out_l = neighbourhood_attention(q_l, k_l, v_l, k_c, v_c, rpb, rows)
    out_c = context_attention(rmsnorm(heads(get_c("na_q")), q_norm), k_c, v_c) if need_ctx else None
    return out_l, out_c

def moe_ffn(h, router_w, router_b, w_gate, w_up, w_down):
    shp = h.shape
    t = h.reshape(-1, shp[-1])
    aff = jax.nn.sigmoid((t @ router_w).astype(jnp.float32))
    sel = (aff + router_b.astype(jnp.float32)).reshape(-1, N_GROUPS, EXPERTS_PER_GROUP)
    group_score = jnp.sum(lax.top_k(sel, TOP_K)[0], axis=-1)
    best = jnp.argmax(group_score, axis=-1)
    in_group = (jnp.arange(N_GROUPS)[None, :] == best[:, None])[..., None]
    sel = jnp.where(in_group, sel, -jnp.inf).reshape(-1, N_EXPERTS)
    _, idx = lax.top_k(sel, TOP_K)
    w = jnp.take_along_axis(aff, idx, axis=-1)
    w = w / jnp.sum(w, axis=-1, keepdims=True)
    gates = jnp.sum(jax.nn.one_hot(idx, N_EXPERTS, dtype=jnp.float32) * w[..., None], axis=1).astype(h.dtype)
    out = jnp.zeros_like(t)
    for e in range(N_EXPERTS):
        he = jax.nn.silu(t @ w_gate[e]) * (t @ w_up[e])
        out = out + gates[:, e:e + 1] * (he @ w_down[e])
    return out.reshape(shp)

def setup_inputs(seed: int = 0) -> dict:
    key = jax.random.key(seed)
    ks = jax.random.split(key, 32)
    f32 = jnp.float32
    nrm = lambda k, shape, s: jax.random.normal(k, shape, f32) * s
    ret_base = jnp.log(-jnp.log(1.0 - 2.0 ** (-5.0 - jnp.arange(RET_HEADS, dtype=f32))))
    dt_f = jnp.exp(jax.random.uniform(ks[14], (DEPTH, SSD_HEADS), f32, math.log(1e-3), math.log(1e-1)))
    dt_b = jnp.exp(jax.random.uniform(ks[15], (DEPTH, SSD_HEADS), f32, math.log(1e-3), math.log(1e-1)))
    return {
        "x": nrm(ks[0], (BATCH, SEQ, D_MODEL), 1.0),
        "c": nrm(ks[1], (BATCH, D_MODEL), 1.0),
        "ctx": nrm(ks[2], (BATCH, CTX_LEN, D_MODEL), 1.0),
        "c_ctx": nrm(ks[3], (D_MODEL,), 1.0),
        "w_mod": nrm(ks[4], (DEPTH, D_MODEL, 6 * D_MODEL), 0.5 * D_MODEL ** -0.5),
        "b_mod": nrm(ks[5], (DEPTH, 6 * D_MODEL), 0.02),
        "norm_mix": 1.0 + nrm(ks[6], (DEPTH, D_MODEL), 0.02),
        "norm_ffn": 1.0 + nrm(ks[7], (DEPTH, D_MODEL), 0.02),
        "w_in": nrm(ks[8], (DEPTH, D_MODEL, IN_COLS), D_MODEL ** -0.5),
        "w_out": nrm(ks[9], (DEPTH, MIX_WIDTH, D_MODEL), MIX_WIDTH ** -0.5),
        "ret_decay_f": ret_base + nrm(ks[10], (DEPTH, RET_HEADS), 0.1),
        "ret_decay_b": ret_base + nrm(ks[11], (DEPTH, RET_HEADS), 0.1),
        "ssd_conv_w": nrm(ks[12], (DEPTH, SSD_CONV, SSD_XBC), SSD_CONV ** -0.5),
        "ssd_conv_b": nrm(ks[13], (DEPTH, SSD_XBC), 0.02),
        "ssd_dt_bias_f": dt_f + jnp.log(-jnp.expm1(-dt_f)),
        "ssd_dt_bias_b": dt_b + jnp.log(-jnp.expm1(-dt_b)),
        "ssd_a_log_f": jnp.log(jax.random.uniform(ks[16], (DEPTH, SSD_HEADS), f32, 1.0, 16.0)),
        "ssd_a_log_b": jnp.log(jax.random.uniform(ks[17], (DEPTH, SSD_HEADS), f32, 1.0, 16.0)),
        "ssd_d": 1.0 + nrm(ks[18], (DEPTH, SSD_HEADS), 0.1),
        "ssd_norm": 1.0 + nrm(ks[19], (DEPTH, SSD_WIDTH), 0.02),
        "na_q_norm": 1.0 + nrm(ks[20], (DEPTH, HEAD_DIM), 0.02),
        "na_k_norm": 1.0 + nrm(ks[21], (DEPTH, HEAD_DIM), 0.02),
        "na_rpb": nrm(ks[22], (DEPTH, NA_HEADS, 2 * NA_WIN_ROWS - 1, 2 * NA_WIN_COLS - 1), 0.1),
        "router_w": nrm(ks[23], (D_MODEL, N_EXPERTS), D_MODEL ** -0.5),
        "router_b": nrm(ks[24], (N_EXPERTS,), 0.01),
        "w_gate": nrm(ks[25], (DEPTH, N_EXPERTS, D_MODEL, D_EXPERT), D_MODEL ** -0.5),
        "w_up": nrm(ks[26], (DEPTH, N_EXPERTS, D_MODEL, D_EXPERT), D_MODEL ** -0.5),
        "w_down": nrm(ks[27], (DEPTH, N_EXPERTS, D_EXPERT, D_MODEL), D_EXPERT ** -0.5),
    }

def reference(x, c, ctx, c_ctx, w_mod, b_mod, norm_mix, norm_ffn, w_in, w_out, ret_decay_f, ret_decay_b,
              ssd_conv_w, ssd_conv_b, ssd_dt_bias_f, ssd_dt_bias_b, ssd_a_log_f, ssd_a_log_b, ssd_d, ssd_norm,
              na_q_norm, na_k_norm, na_rpb, router_w, router_b, w_gate, w_up, w_down):
    n_lat = x.shape[1]
    rows = n_lat // GRID_W
    cos, sin = axial_rope_tables(n_lat)
    s_lat = jax.nn.silu(c)
    s_ctx = jax.nn.silu(c_ctx)
    h_lat, h_ctx = x, ctx
    for layer in range(DEPTH):
        need_ctx = layer < DEPTH - 1
        mod_l = s_lat @ w_mod[layer] + b_mod[layer]
        sh_a, sc_a, g_a, sh_f, sc_f, g_f = [m[:, None, :] for m in jnp.split(mod_l, 6, axis=-1)]
        n_mod_c = 6 * D_MODEL if need_ctx else 2 * D_MODEL
        mod_c = s_ctx @ w_mod[layer][:, :n_mod_c] + b_mod[layer][:n_mod_c]
        mc = jnp.split(mod_c, n_mod_c // D_MODEL)

        a_l = modulate(rmsnorm(h_lat, norm_mix[layer]), sh_a, sc_a)
        a_c = modulate(rmsnorm(h_ctx, norm_mix[layer]), mc[0], mc[1])
        get_l = _segment_getter(a_l, w_in[layer], True)
        get_c = _segment_getter(a_c, w_in[layer], need_ctx)
        ret_l, ret_c = retention_group(get_l, get_c, ret_decay_f[layer], ret_decay_b[layer], cos, sin, need_ctx)
        ssd_l, ssd_c = ssd_group(get_l, get_c, ssd_conv_w[layer], ssd_conv_b[layer], ssd_dt_bias_f[layer],
                                 ssd_dt_bias_b[layer], ssd_a_log_f[layer], ssd_a_log_b[layer], ssd_d[layer],
                                 ssd_norm[layer], need_ctx)
        na_l, na_c = na_group(get_l, get_c, na_q_norm[layer], na_k_norm[layer], na_rpb[layer], rows, need_ctx)

        mix_l = jnp.concatenate([ret_l, ssd_l, na_l.astype(ret_l.dtype)], axis=-1)
        h_lat = h_lat + g_a * (mix_l @ w_out[layer])
        f_l = modulate(rmsnorm(h_lat, norm_ffn[layer]), sh_f, sc_f)
        h_lat = h_lat + g_f * moe_ffn(f_l, router_w, router_b, w_gate[layer], w_up[layer], w_down[layer])
        if need_ctx:
            mix_c = jnp.concatenate([ret_c, ssd_c, na_c.astype(ret_c.dtype)], axis=-1)
            h_ctx = h_ctx + mc[2] * (mix_c @ w_out[layer])
            f_c = modulate(rmsnorm(h_ctx, norm_ffn[layer]), mc[3], mc[4])
            h_ctx = h_ctx + mc[5] * moe_ffn(f_c, router_w, router_b, w_gate[layer], w_up[layer], w_down[layer])
    return h_lat


_drawn_inputs = setup_inputs


def setup_inputs(seed=0):
    import zlib

    import numpy as np

    out = dict(_drawn_inputs(seed))
    spreads = {}
    factors = {'ssd_conv_b': 2.709, 'na_q_norm': 8.0, 'na_k_norm': 8.0, 'na_rpb': 27.87}
    for name, (base, spread) in spreads.items():
        noise = np.random.default_rng([zlib.crc32(name.encode()), seed]).standard_normal(out[name].shape)
        drawn = base * np.exp(spread * noise) if base else spread * noise
        out[name] = jnp.asarray(drawn.astype(out[name].dtype))
    for name, factor in factors.items():
        out[name] = (out[name] * factor).astype(out[name].dtype)
    return out
```

```python
from contextlib import ExitStack
import math

import numpy as np
import concourse.bass as bass
from concourse import mybir

F32 = mybir.dt.float32
ALU = mybir.AluOpType
ACT = mybir.ActivationFunctionType
AX = mybir.AxisListType

P = 128
D = 1024
KD = D // P
DEPTH = 2
GRID = 64
CTX = 256
SEQ = 256
TOK = CTX + SEQ
NT = TOK // P
HD = 64
RET_H, SSD_H, NA_H = 4, 8, 4
NH = SSD_H + RET_H
STATE = 64
NE = 16
FE = 512
EPS = 1e-6
SCALE = HD ** -0.5
NEG = -1e30

IN_PIECES = (("bc_dt", 2048, 272), ("x", 1536, 512), ("ret_qk", 0, 512), ("ret_vg", 512, 512),
             ("z", 1024, 512), ("na_qk", 2320, 512), ("na_v", 2832, 256))
N_MOD = 12
N_OUT = 2
N_STATIC = N_MOD + len(IN_PIECES) + N_OUT
SLOT = 4096

C_ID, C_LE, C_GT, C_GE, C_LT, C_ONE, C_DRET, C_FLIP = (P * i for i in range(8))
C_MASK = 8 * P
C_COS = C_MASK + 64
C_SIN = C_COS + 128
C_TRI = C_SIN + 128
N_CONST = C_TRI + 16
L_BMOD, L_NMIX, L_NFFN, L_CW, L_CB = 0, 48, 56, 64, 82
N_COLP = 88
R_DTB, R_DEC, R_D, R_NQK, R_NORM = 0, 16, 40, 48, 560
N_ROWP = 1072


def shape_constants():
    c = np.zeros((P, N_CONST), np.float32)
    u = np.arange(P)[:, None]
    v = np.arange(P)[None, :]
    c[:, C_ID:C_ID + P] = u == v
    c[:, C_LE:C_LE + P] = u <= v
    c[:, C_GT:C_GT + P] = u > v
    c[:, C_GE:C_GE + P] = u >= v
    c[:, C_LT:C_LT + P] = u < v
    c[:, C_ONE:C_ONE + P] = 1.0
    c[:, C_DRET:C_DRET + P] = SCALE * (1.0 + (u == v))
    q = GRID - 1 - np.arange(P)[:, None] % GRID
    c[:, C_FLIP:C_FLIP + P] = (v // GRID == u // GRID) & (v % GRID == q)
    k = np.arange(GRID)[None, :]
    first = np.clip(q - 8, 0, GRID - 16)
    c[:, C_MASK:C_MASK + GRID] = np.where((k >= first) & (k < first + 16), 0.0, NEG)
    inv = (1.0 / (10000.0 ** (np.arange(16, dtype=np.float32) / 16))).astype(np.float32)
    for n in range(2):
        t = np.arange(P) + n * P
        for axis, pos in enumerate((t // GRID, t % GRID)):
            ang = pos[:, None].astype(np.float32) * inv
            for half in range(2):
                at = n * 64 + axis * 32 + half * 16
                c[:, C_COS + at:C_COS + at + 16] = np.cos(ang)
                c[:, C_SIN + at:C_SIN + at + 16] = np.sin(ang) * (1 if half else -1)
    i = np.arange(4)
    c[:, C_TRI:C_TRI + 16] = (i[None, :] < i[:, None]).reshape(1, 16)
    return c


def trunk(nc, ins, out):
    x, ctx_in = ins["x"], ins["ctx"]
    es = ExitStack()
    with es:
        sems = {}

        def S(name):
            if name not in sems:
                sems[name] = es.enter_context(nc.semaphore(name))
            return sems[name]

        def per_layer(name, l):
            T = len(tiles(l))
            jobs = in_jobs(l)
            a, d = emptied(jobs, len(jobs))
            table = {
                "mod_pe": N_MOD, "in_pe": len(jobs), "in_act": a, "in_dve": d, "out_pe": N_OUT * T, "res_dve": N_OUT * T,
                "a_sq": NT, "a_hn": NT, "a_tr": KD, "a_evac": KD, "f_sq": T, "f_hn": T, "f_tr": KD, "f_evac": KD,
                "conv_dve": 6, "conv_act": 6, "x_tr": 5, "x_evac": 5, "ret_tr": NT, "ret_evac": NT, "rope": 2,
                "na_sq": NT, "na_ss": NT, "na_norm": NT, "naT_tr": NT, "naT_evac": NT,
                "rf_dve": T + 1, "rb_pool": T + 1, "seg_pe": T + 1, "e_act": T + 1,
                "vw_dve": 6, "st_pe": 6, "h_dve": 6, "mix_tr": KD, "mixT": KD,
                "diag0": len(segs(l)), "row0": len(segs(l)), "diag1": len(segs(l)), "row1": len(segs(l)),
                "ld_colp": 16, "ld_rowp": 16, "ld_bias": 16 * 2 * NA_H,
            }
            table.update(dict.fromkeys(("sc_pe", "sl_dve", "mret_dve", "v_pool", "y_pe", "comb_dve", "dx_pool", "yz_dve",
                                        "yss_act", "gn_ms", "gn_rs", "na_out", "h_end"), T))
            table.update(dict.fromkeys(("mf_dve", "mb_pool", "diag_pe"), 2 * T))
            table.update(dict.fromkeys(("s_pe", "mx_dve", "p_act", "pt_pe", "pt_dve", "pv_pe"), NA_H * T))
            table.update(dict.fromkeys(("gu_pe", "hs_act", "hp_dve", "hT_pe", "hT_act", "dn_pe", "acc_dve"), NE * T))
            table.update(dict.fromkeys(("mod_evac", "modA", "a_ms", "a_rs", "f_ms", "f_rs", "pad_zero", "na_ms", "na_rs",
                                        "dt_abs", "dt_ln", "nA_act", "loga", "cum_pe", "ex_act", "bias_dve", "row0_pe",
                                        "row1_pe", "rt_pe", "rt_act", "acc_zero"), 1))
            return table[name]

        def upto(name, l, n):
            return n + sum(per_layer(name, m) for m in range(l))

        def sb(name, *shape):
            return es.enter_context(nc.sbuf_tensor(name, [P, *shape], F32))

        h = sb("h", NT, D)
        featT = sb("featT", KD, TOK)
        tokA = sb("tokA", NT, D)
        ring = sb("ring", 2, SLOT)
        const = sb("const", N_CONST)
        colp = sb("colp", N_COLP)
        condT = sb("condT", KD, 2)
        silT = sb("silT", KD, 2)
        mod = sb("mod", 48, 2)
        modA = sb("modA", 2, KD, 2)
        rw = sb("rw", KD, NE)
        rb = sb("rb", NE)
        stat = sb("stat", 64)
        stat2 = sb("stat2", 64)
        pw = sb("pw", 64)
        ARENA = 30780
        arena = sb("arena", ARENA)
        cursor = [0]

        def carve(*shape):
            n = int(np.prod(shape))
            at = cursor[0]
            cursor[0] += n
            assert cursor[0] <= ARENA
            v = arena[:, at:at + n]
            if len(shape) == 2:
                v = v.rearrange("p (a b) -> p a b", a=shape[0])
            elif len(shape) == 3:
                v = v.rearrange("p (a b c) -> p a b c", a=shape[0], b=shape[1])
            elif len(shape) == 4:
                v = v.rearrange("p (a b c d) -> p a b c d", a=shape[0], b=shape[1], c=shape[2])
            return v

        qk = carve(NT, 512)
        XV = carve(NT, NH * HD)
        at = cursor[0]
        nqk = carve(NT, 512)
        cursor[0] = at
        Mf = carve(2, 4, P)
        Mb = carve(2, 4, P)
        nav = carve(NT, 256)
        BCT = carve(2, TOK)
        Bt = carve(NT, P)
        retT = carve(4, TOK)
        naT = carve(4, TOK)
        at = cursor[0]
        xT = carve(4, TOK)
        cursor[0] = at
        rf = carve(SSD_H, P)
        rbk = carve(SSD_H, P)
        at = cursor[0]
        Hs = carve(2, NT, 384)
        cursor[0] = at
        xpad = carve(6, 2, CTX + 2)
        y = carve(NH, HD)
        y2 = carve(NH, HD)
        Pm = carve(2, 512)
        sq = Pm[:, 0, :]
        at_gate = cursor[0]
        E = carve(SSD_H, P)
        Eret = carve(RET_H, P)
        Mret = carve(RET_H, P)
        sU = carve(2, P)
        sL = carve(2, P)
        VW = carve(NH, HD)
        Vf = carve(SSD_H, HD)
        Vb = carve(SSD_H, HD)
        at = cursor[0]
        cursor[0] = at_gate
        diag = carve(2, D)
        grow = carve(2, D)
        assert cursor[0] <= at
        cursor[0] = at
        at = cursor[0]
        dx = carve(SSD_H, HD)
        cursor[0] = at
        PT = carve(2, 4, P)
        bias = carve(NA_H, 6, GRID)
        rowp = carve(N_ROWP)
        nA = carve(2, NH)
        dtr = carve(NT * 2, SSD_H)
        dta = carve(NT * 2, SSD_H)
        DTX = carve(NT * 2, NH)
        Aall = carve(NT * 2, NH)
        EX = carve(288)
        Wt = carve(2, NT, NH)
        Dec = carve(NT * 2, 6)
        rs = carve(NT, 8)
        nmx = carve(16)
        nsum = carve(16)
        nrec = carve(16)
        cursor[0] = 0
        slots = [ring[:, 0, :], ring[:, 1, :]] + [carve(SLOT) for _ in range(4)]
        hs = carve(2, FE)
        hp = carve(2, FE)
        hT = carve(2, 4, P)
        gates = carve(NT, NE)
        aff = carve(NT, NE)
        sel = carve(NT * 4, 4)
        g1, g2, g3, g4 = (carve(NT, 4) for _ in range(4))
        cmp1 = carve(NT * 4, 16)
        cmp2 = carve(NT * 4, 16)
        cnt = carve(NT * 4, 4)
        rsum = carve(NT)
        assert cursor[0] <= at_gate

        ps = es.enter_context(nc.psum_tensor("ps", [P, 8, 512], F32))
        ident = const[:, C_ID:C_ID + P]
        LE, GT, GE, LT, ONE = (const[:, c:c + P] for c in (C_LE, C_GT, C_GE, C_LT, C_ONE))

        def flat(bank, n):
            return ps[:, bank:bank + (n + 511) // 512, :].rearrange("p a b -> p (a b)")[:, 0:n]

        def heads(ap, n):
            return ap.rearrange("p (a b) -> p a b", a=n)

        def ssd(ap, n=1):
            return ap.rearrange("p (g c) -> p g c", g=2)[:, :, 0:4 * n]

        def ret(ap, n=1):
            return ap.rearrange("p (g c) -> p g c", g=2)[:, :, 4 * n:6 * n]

        def line(ap):
            return ap.rearrange("p a b -> p (a b)")

        def spread2(ap, n):
            return ap.unsqueeze(3).to_broadcast([P, 2, ap.shape[2], n])

        def triangle_rows(dst, a, m, tri):
            return (dst.rearrange("p (g h) c -> p g h c", g=2), spread2(a, P),
                    tri.unsqueeze(1).unsqueeze(1).to_broadcast([P, 2, m, P]))

        def spread(ap, n):
            return ap.unsqueeze(2).to_broadcast([P, ap.shape[1], n])

        def repeat(ap, n):
            return ap.unsqueeze(1).to_broadcast([P, n, ap.shape[1]])

        def tiles(l):
            return list(range(NT)) if l < DEPTH - 1 else [2, 3]

        def in_jobs(l):
            jobs = [("bc_dt", "f", 4, "A"), ("bc_dt", "f", 5, "A"), ("bc_dt", "dt", 0, "D")]
            jobs += [("x", "f", f, "A") for f in range(4)]
            jobs += [("ret_qk", "t", t, "D") for t in range(NT)]
            jobs += [("ret_vg", "t", t, "A") for t in range(NT)]
            jobs += [("z", "t", t, "A") for t in tiles(l)]
            jobs += [("na_qk", "t", t, "D") for t in range(NT)]
            jobs += [("na_v", "t", t, "D") for t in range(NT)]
            return jobs

        def emptied(jobs, upto):
            a = sum(j[3] == "A" for j in jobs[:upto])
            return a, upto - a

        def cols_needed(l, piece, t):
            full = l < DEPTH - 1 or t >= 2
            return {"ret_qk": (0 if full else 256, 512), "ret_vg": (0, 512 if full else 256),
                    "z": (0, 512), "na_qk": (0 if full else 256, 512), "na_v": (0, 256)}[piece]

        STATE_STEPS = ((0, 0), (1, 1), (0, 1), (1, 0), (0, 2), (1, 3))
        STATE_NEXT = {(0, 0): 1, (0, 1): 2, (0, 2): 3, (1, 1): 0, (1, 0): 3, (1, 3): 2}

        def dirs_of(t):
            return [d for d in (0, 1) if (d, t) not in ((0, 0), (1, 1))]

        def att_units(l):
            return [(t, hd) for t in tiles(l) for hd in range(NA_H)]

        def segs(l):
            return [0, 1] if l < DEPTH - 1 else [1]

        def dve_jobs_done(l, name, i):
            jobs = in_jobs(l)
            n = next(n for n, q in enumerate(jobs) if q[0] == name and q[2] == i and q[3] == "D")
            return emptied(jobs, n + 1)[1]

        def piece_uses(l):
            uses = [("mod_pe", l, n + 1) for n in range(N_MOD)]
            jobs = in_jobs(l)
            for name, _, _ in IN_PIECES:
                last = max(i for i, j in enumerate(jobs) if j[0] == name)
                uses.append(("in_pe", l, last + 1))
            nt = len(tiles(l))
            uses += [("out_pe", l, nt * (n + 1)) for n in range(N_OUT)]
            return uses

        def loads_before(l, slot):
            static = (N_STATIC + 1 - slot) // 2 if slot < 2 else 0
            return l * (static + NE // 2)

        def static_ready(eng, l, n):
            eng.wait_ge(S(f"slot{n % 2}"), 16 * (loads_before(l, n % 2) + n // 2 + 1))

        def static_loads(l, slot):
            return loads_before(l, slot) + ((N_STATIC + 1 - slot) // 2 if slot < 2 else 0)

        block = es.enter_context(nc.Block())

        @block.sync
        def _(sp):
            sp.dma_start(const[:, :], ins["consts"]).then_inc(S("ld_const"), 16)
            sp.dma_start(condT[:, :, :], ins["condT"]).then_inc(S("ld_cond"), 16)
            sp.dma_start(h[:, 0:2, :], ctx_in.rearrange("(t p) d -> p t d", p=P)).then_inc(S("ld_h0"), 16)
            sp.dma_start(h[:, 2:4, :], x.rearrange("(t p) d -> p t d", p=P)).then_inc(S("ld_h1"), 16)
            sp.dma_start(rw[:, :, :], ins["router_w"].rearrange("(k p) e -> p k e", p=P)).then_inc(S("ld_rw"), 16)
            rbt = ins["router_b"]
            sp.dma_start(rb[:, :], bass.AP(rbt.tensor, 0, [[0, P], [1, NE]])).then_inc(S("ld_rb"), 16)

            def source(l, n):
                if n < N_MOD:
                    return ins["w_mod"][l, :, 512 * n:512 * (n + 1)]
                if n < N_MOD + len(IN_PIECES):
                    _, c, w = IN_PIECES[n - N_MOD]
                    return ins["w_in"][l, :, c:c + w]
                c = 512 * (n - N_MOD - len(IN_PIECES))
                return ins["w_out"][l, :, c:c + 512]

            def load_static(l, n):
                src = source(l, n)
                w = src.shape[1]
                dst = slots[n % 2][:, 0:KD * w].rearrange("p (k c) -> p k c", k=KD)
                sp.dma_start(dst, src.rearrange("(k p) c -> p k c", p=P)).then_inc(S(f"slot{n % 2}"), 16)

            def small(l):
                sp.dma_start(colp[:, :], ins["colp"][l]).then_inc(S("ld_colp"), 16)
                rp = ins["rowp"]
                sp.dma_start(rowp, bass.AP(rp.tensor, l * N_ROWP, [[0, P], [1, N_ROWP]])).then_inc(S("ld_rowp"), 16)
                rpb = ins["na_rpb"]
                for half, dr0 in ((0, 5), (1, 4)):
                    for hd in range(NA_H):
                        base = ((l * NA_H + hd) * 15 + dr0) * 31 + 15 - (GRID - 1)
                        sp.dma_start(bias[64 * half:64 * half + 64, hd, :, :],
                                     bass.AP(rpb.tensor, base, [[1, 64], [31, 6], [1, 64]])
                                     ).then_inc(S("ld_bias"), 16)

            for l in range(DEPTH):
                uses = piece_uses(l)
                nt = len(tiles(l))
                if l > 0:
                    sp.wait_ge(S("dn_pe"), upto("dn_pe", l - 1, NE * len(tiles(l - 1))))
                    sp.wait_ge(S("acc_dve"), upto("acc_dve", l - 1, NE * len(tiles(l - 1))))
                    sp.wait_ge(S("f_evac"), upto("f_evac", l - 1, KD))
                small(l)
                for n in range(N_STATIC):
                    if n >= 2:
                        sp.wait_ge(S(uses[n - 2][0]), upto(*uses[n - 2]))
                    load_static(l, n)

                T = nt

                def load_expert(e, par, j):
                    slot = 3 * par + j
                    src = (ins["w_gate"], ins["w_up"], ins["w_down"])[j]
                    k = 8 if j < 2 else 4
                    dst = slots[slot].rearrange("p (k c) -> p k c", k=k)
                    if isinstance(e, int):
                        s = src[l, e]
                    else:
                        s = src[l, bass.ds(e, 1)].rearrange("o r c -> (o r) c")
                    sp.dma_start(dst, s.rearrange("(k p) c -> p k c", p=P)).then_inc(S(f"slot{slot}"), 16)

                sp.wait_ge(S(uses[N_STATIC - 2][0]), upto(*uses[N_STATIC - 2]))
                sp.wait_ge(S(uses[N_STATIC - 1][0]), upto(*uses[N_STATIC - 1]))
                load_expert(0, 0, 0)
                load_expert(0, 0, 1)
                sp.wait_ge(S("na_out"), upto("na_out", l, nt))
                for par, j in ((0, 2), (1, 0), (1, 1), (1, 2)):
                    load_expert(par, par, j)
                with sp.Fori(1, NE // 2) as i:
                    for par in range(2):
                        sp.wait_ge(S("gu_pe"), upto("gu_pe", l, (i * 2 + (par - 1)) * T))
                        load_expert(i * 2 + par, par, 0)
                        load_expert(i * 2 + par, par, 1)
                        sp.wait_ge(S("dn_pe"), upto("dn_pe", l, (i * 2 + (par - 1)) * T))
                        load_expert(i * 2 + par, par, 2)
            sp.wait_ge(S("h_end"), upto("h_end", DEPTH - 1, 2))
            sp.dma_start(out.rearrange("(t p) d -> p t d", p=P), h[:, 2:4, :]).then_inc(S("stored"), 16)
            sp.wait_ge(S("stored"), 16)

        @block.tensor
        def _(pe):
            mm = nc.tensor.matmul
            tr = nc.tensor.transpose
            pe.wait_ge(S("ld_const"), 16)

            def piece(n, w=512):
                return slots[n % 2][:, 0:KD * w].rearrange("p (k c) -> p k c", k=KD)

            def modulation(l):
                pe.wait_ge(S("sil"), 1)
                if l > 0:
                    pe.wait_ge(S("acc_dve"), upto("acc_dve", l - 1, NE * len(tiles(l - 1))))
                for n in range(N_MOD):
                    static_ready(pe, l, n)
                    for f in range(4):
                        c = 4 * n + f
                        for k in range(KD):
                            i = mm(ps[:, 0, 2 * c:2 * c + 2], piece(n)[:, k, P * f:P * f + P], silT[:, k, :],
                                   start=k == 0, stop=k == KD - 1)
                    i.then_inc(S("mod_pe"), 1)

            def norm_transpose(l, which, ts):
                pe.wait_ge(S(which + "_hn"), upto(which + "_hn", l, len(ts)))
                if which == "a":
                    pe.wait_ge(S("mod_evac"), upto("mod_evac", l, 1))
                for k in range(KD):
                    if k >= 4:
                        pe.wait_ge(S(which + "_evac"), upto(which + "_evac", l, k - 3))
                    for j, t in enumerate(ts):
                        i = tr(ps[:, 1 + k % 4, P * t:P * t + P], tokA[:, t, P * k:P * k + P], ident)
                    i.then_inc(S(which + "_tr"), 1)

            def project(l):
                jobs = in_jobs(l)
                pe.wait_ge(S("a_evac"), upto("a_evac", l, KD))
                for n, (name, kind, i, _) in enumerate(jobs):
                    p = [q[0] for q in IN_PIECES].index(name)
                    w = IN_PIECES[p][2]
                    W = piece(N_MOD + p, w)
                    if n == 0 or jobs[n - 1][0] != name:
                        static_ready(pe, l, N_MOD + p)
                    if n >= 4:
                        a, d = emptied(jobs, n - 3)
                        pe.wait_ge(S("in_act"), upto("in_act", l, a))
                        if d:
                            pe.wait_ge(S("in_dve"), upto("in_dve", l, d))
                    bank = ps[:, n % 4, :]
                    if kind == "f":
                        c = P * (i % 4)
                        lo = 0 if (l < DEPTH - 1 or i != 5) else CTX
                        for k in range(KD):
                            o = mm(bank[:, lo:TOK], W[:, k, c:c + P], featT[:, k, lo:TOK],
                                   start=k == 0, stop=k == KD - 1)
                    elif kind == "dt":
                        for t in range(NT):
                            for k in range(KD):
                                o = mm(bank[:, 16 * t:16 * t + 16], featT[:, k, P * t:P * t + P], W[:, k, 256:272],
                                       start=k == 0, stop=k == KD - 1)
                    else:
                        lo, hi = cols_needed(l, name, i)
                        for k in range(KD):
                            o = mm(bank[:, lo:hi], featT[:, k, P * i:P * i + P], W[:, k, lo:hi],
                                   start=k == 0, stop=k == KD - 1)
                    o.then_inc(S("in_pe"), 1)

            def turn_operands(l):
                jobs = in_jobs(l)
                a, d = emptied(jobs, len(jobs))
                pe.wait_ge(S("in_act"), upto("in_act", l, a))
                pe.wait_ge(S("in_dve"), upto("in_dve", l, d))
                for n, f in enumerate((4, 0, 1, 2, 3)):
                    pe.wait_ge(S("conv_act"), upto("conv_act", l, {4: 1, 5: 2}.get(f, f + 3)))
                    if n >= 2:
                        pe.wait_ge(S("x_evac"), upto("x_evac", l, n - 1))
                    src = BCT[:, 0, :] if f == 4 else xT[:, f, :]
                    for t in range(NT):
                        i = tr(ps[:, 4 + n % 2, P * t:P * t + P], src[:, P * t:P * t + P], ident)
                    i.then_inc(S("x_tr"), 1)
                for t in range(NT):
                    full = t in tiles(l)
                    if t >= 2:
                        pe.wait_ge(S("rope"), upto("rope", l, t - 1))
                        pe.wait_ge(S("ret_evac"), upto("ret_evac", l, t - 1))
                    for b in range(0 if full else 2, 4):
                        i = tr(ps[:, 6 + t % 2, P * b:P * b + P], qk[:, t, P * b:P * b + P], ident)
                    i.then_inc(S("ret_tr"), 1)
                for t in range(NT):
                    full = t in tiles(l)
                    pe.wait_ge(S("na_norm"), upto("na_norm", l, t + 1))
                    if t >= 2:
                        pe.wait_ge(S("naT_evac"), upto("naT_evac", l, t - 1))
                    for b in range(0 if full else 2, 4):
                        i = tr(ps[:, t % 2, P * b:P * b + P], nqk[:, t, P * b:P * b + P], ident)
                    i.then_inc(S("naT_tr"), 1)

            def decay_sums(l):
                pe.wait_ge(S("loga"), upto("loga", l, 1))
                f, b = Aall[:, 0:NT * 2:2, :], Aall[:, 1:NT * 2:2, :]
                pe.wait_ge(S("naT_evac"), upto("naT_evac", l, NT))
                for n, (tri, a) in enumerate(((LE, f), (GE, b), (GT, f), (LT, b))):
                    mm(ps[:, 2, 48 * n:48 * n + 48], tri, a, start=True, stop=True)
                mm(ps[:, 2, 192:288], ONE, Aall[:, :, :], start=True, stop=True).then_inc(S("cum_pe"), 1)

            def states(l):
                pe.wait_ge(S("x_evac"), upto("x_evac", l, 5))
                pe.wait_ge(S("ret_evac"), upto("ret_evac", l, NT))
                for n, (d, t) in enumerate(STATE_STEPS):
                    pe.wait_ge(S("vw_dve"), upto("vw_dve", l, n + 1))
                    if n >= 2:
                        pe.wait_ge(S("h_dve"), upto("h_dve", l, n - 1))
                    bank = ps[:, 3 + n % 2, :]
                    for g in range(2):
                        mm(bank[64 * g:64 * g + 64, 0:256], Bt[:, t, 64 * g:64 * g + 64],
                           VW[:, 6 * g:6 * g + 4, :], start=True, stop=True)
                    for r in range(RET_H):
                        i = mm(bank[64 * (r % 2):64 * (r % 2) + 64, 256 + 64 * (r // 2):320 + 64 * (r // 2)],
                               qk[:, t, 256 + 64 * r:320 + 64 * r], VW[:, 6 * (r % 2) + 4 + r // 2, :],
                               start=True, stop=True)
                    i.then_inc(S("st_pe"), 1)

            def scan_tile(l, n, t):
                pe.wait_ge(S("rf_dve"), upto("rf_dve", l, n + 2))
                pe.wait_ge(S("rb_pool"), upto("rb_pool", l, n + 2))
                if n > 0:
                    pe.wait_ge(S("mret_dve"), upto("mret_dve", l, n))
                else:
                    pe.wait_ge(S("e_act"), upto("e_act", l, 1))
                for hf in range(2):
                    mm(ps[:, 6 + hf, :], GT, rf[:, 4 * hf:4 * hf + 4, :], start=True, stop=False)
                    i = mm(ps[:, 6 + hf, :], LT, rbk[:, 4 * hf:4 * hf + 4, :], start=False, stop=True)
                i.then_inc(S("seg_pe"), 1)
                pe.wait_ge(S("e_act"), upto("e_act", l, n + 2))
                c = slice(P * t, P * t + P)
                for g in range(2):
                    s = slice(64 * g, 64 * g + 64)
                    mm(ps[:, 6 + g, 0:P], BCT[s, 0, c], BCT[s, 1, c], start=True, stop=True)
                for r in range(RET_H):
                    s = slice(64 * (r % 2), 64 * (r % 2) + 64)
                    o = P * (1 + r // 2)
                    i = mm(ps[:, 6 + r % 2, o:o + P], retT[s, 2 + r // 2, c], retT[s, r // 2, c],
                           start=True, stop=True)
                i.then_inc(S("sc_pe"), 1)
                if n > 0:
                    pe.wait_ge(S("comb_dve"), upto("comb_dve", l, n))
                for d in dirs_of(t):
                    b = 2 + 2 * d
                    pe.wait_ge(S("h_dve"), upto("h_dve", l, 6))
                    for g in range(2):
                        s = slice(64 * g, 64 * g + 64)
                        mm(ps[:, b + g, 0:256], BCT[s, 1, c], Hs[s, d, t, 0:256], start=True, stop=True)
                    for r in range(RET_H):
                        s = slice(64 * (r % 2), 64 * (r % 2) + 64)
                        mm(ps[:, b + r % 2, 256 + 64 * (r // 2):320 + 64 * (r // 2)], retT[s, r // 2, c],
                           Hs[s, d, t, 256 + 64 * (r // 2):320 + 64 * (r // 2)], start=True, stop=True)
                pe.wait_ge(S("v_pool"), upto("v_pool", l, n + 1))
                for g in range(2):
                    pe.wait_ge(S("mf_dve"), upto("mf_dve", l, 2 * n + g + 1))
                    pe.wait_ge(S("mb_pool"), upto("mb_pool", l, 2 * n + g + 1))
                    for j in range(4):
                        hd = 4 * g + j
                        o = ps[:, g, 64 * j:64 * j + 64]
                        mm(o, Mf[:, g, j, :], Vf[:, hd, :], start=True, stop=False)
                        i = mm(o, Mb[:, g, j, :], Vb[:, hd, :], start=False, stop=True)
                    i.then_inc(S("diag_pe"), 1)
                pe.wait_ge(S("mret_dve"), upto("mret_dve", l, n + 1))
                for r in range(RET_H):
                    g, o = r // 2, 256 + 64 * (r % 2)
                    i = mm(ps[:, g, o:o + 64], Mret[:, r, :], XV[:, t, 384 * g + o:384 * g + o + 64],
                           start=True, stop=True)
                i.then_inc(S("y_pe"), 1)

            def scan(l):
                pe.wait_ge(S("rf_dve"), upto("rf_dve", l, 1))
                pe.wait_ge(S("rb_pool"), upto("rb_pool", l, 1))
                mm(ps[:, 6, :], GT, rf[:, 0:4, :], start=True, stop=False)
                mm(ps[:, 6, :], LT, rbk[:, 0:4, :], start=False, stop=True).then_inc(S("seg_pe"), 1)
                states(l)
                for n, t in enumerate(tiles(l)):
                    scan_tile(l, n, t)

            def attention(l):
                un = att_units(l)
                pe.wait_ge(S("comb_dve"), upto("comb_dve", l, len(tiles(l))))

                def scores(n):
                    t, hd = un[n]
                    s = slice(64 * (hd % 2), 64 * (hd % 2) + 64)
                    keys = TOK if t >= 2 else CTX
                    if n >= 2:
                        pe.wait_ge(S("p_act"), upto("p_act", l, n - 1))
                    lat = t >= 2
                    i = mm(ps[:, n % 2, 0:keys], naT[s, hd // 2, P * t:P * t + P], naT[s, 2 + hd // 2, 0:keys],
                           start=True, stop=not lat)
                    if lat:
                        j = 2 - 2 * (t - 2)
                        pe.wait_ge(S("bias_dve"), upto("bias_dve", l, 1))
                        i = mm(ps[:, n % 2, CTX:TOK], const[:, C_FLIP:C_FLIP + P], bias[:, hd, j:j + 4, :], start=False, stop=True)
                    i.then_inc(S("s_pe"), 1)

                def turn(n):
                    t, hd = un[n]
                    nk = NT if t >= 2 else 2
                    pe.wait_ge(S("p_act"), upto("p_act", l, n + 1))
                    if n >= 2:
                        pe.wait_ge(S("pt_dve"), upto("pt_dve", l, n - 1))
                    for b in range(nk):
                        i = tr(ps[:, 2 + n % 2, P * b:P * b + P], Pm[:, n % 2, P * b:P * b + P], ident)
                    i.then_inc(S("pt_pe"), 1)

                def values(n):
                    t, hd = un[n]
                    nk = NT if t >= 2 else 2
                    pe.wait_ge(S("pt_dve"), upto("pt_dve", l, n + 1))
                    tile = n // NA_H
                    if n % NA_H == 0 and tile >= 2:
                        pe.wait_ge(S("na_out"), upto("na_out", l, tile - 1))
                    for b in range(nk):
                        i = mm(ps[:, 4 + tile % 2, 64 * hd:64 * hd + 64], PT[:, n % 2, b, :],
                               nav[:, b, 64 * hd:64 * hd + 64], start=b == 0, stop=b == nk - 1)
                    i.then_inc(S("pv_pe"), 1)

                N = len(un)
                scores(0)
                for n in range(N):
                    if n + 1 < N:
                        scores(n + 1)
                    if n >= 1:
                        values(n - 1)
                    turn(n)
                values(N - 1)

            def output(l):
                ts = tiles(l)
                pe.wait_ge(S("na_out"), upto("na_out", l, len(ts)))
                for k in range(KD):
                    if k >= 2:
                        pe.wait_ge(S("mixT"), upto("mixT", l, k - 1))
                    for t in ts:
                        i = tr(ps[:, 6 + k % 2, P * t:P * t + P], tokA[:, t, P * k:P * k + P], ident)
                    i.then_inc(S("mix_tr"), 1)
                gate_rows(l, 0)
                pe.wait_ge(S("mixT"), upto("mixT", l, KD))
                n = 0
                for half in range(N_OUT):
                    p = N_MOD + len(IN_PIECES) + half
                    static_ready(pe, l, p)
                    for t in ts:
                        if n >= 2:
                            pe.wait_ge(S("res_dve"), upto("res_dve", l, n - 1))
                        for k in range(KD):
                            i = mm(ps[:, 4 + n % 2, :], featT[:, k, P * t:P * t + P], piece(p)[:, k, :],
                                   start=k == 0, stop=k == KD - 1)
                        i.then_inc(S("out_pe"), 1)
                        n += 1

            def gate_rows(l, which):
                pe.wait_ge(S(f"diag{which}"), upto(f"diag{which}", l, len(segs(l))))
                if which == 1:
                    pe.wait_ge(S("rt_act"), upto("rt_act", l, 1))
                for seg in segs(l):
                    for hf in range(2):
                        i = mm(ps[:, 2 * seg + hf, :], ONE, diag[:, seg, 512 * hf:512 * hf + 512],
                               start=True, stop=True)
                i.then_inc(S(f"row{which}_pe"), 1)

            def router(l):
                ts = tiles(l)
                pe.wait_ge(S("f_evac"), upto("f_evac", l, KD))
                pe.wait_ge(S("ld_rw"), 16)
                for t in ts:
                    for k in range(KD):
                        i = mm(ps[:, 0, NE * t:NE * t + NE], featT[:, k, P * t:P * t + P], rw[:, k, :],
                               start=k == 0, stop=k == KD - 1)
                i.then_inc(S("rt_pe"), 1)

            def experts(l):
                ts = tiles(l)
                T = len(ts)
                pe.wait_ge(S("row1"), upto("row1", l, len(segs(l))))

                def gate_up(i, c):
                    par, j = divmod(c, T)
                    if j == 0:
                        for s in (3 * par, 3 * par + 1):
                            pe.wait_ge(S(f"slot{s}"), (i + 1) * 16 + 16 * static_loads(l, s))
                    if not (isinstance(i, int) and i == 0 and c < 2):
                        pe.wait_ge(S("hp_dve"), upto("hp_dve", l, i * (2 * T) + (c - 1)))
                    t = ts[j]
                    b = 2 * (c % 2)
                    for m in range(2):
                        W = slots[3 * par + m].rearrange("p (k c) -> p k c", k=KD)
                        for k in range(KD):
                            o = mm(ps[:, b + m, :], featT[:, k, P * t:P * t + P], W[:, k, :],
                                   start=k == 0, stop=k == KD - 1)
                    o.then_inc(S("gu_pe"), 1)

                def turn(i, c):
                    pe.wait_ge(S("hp_dve"), upto("hp_dve", l, i * (2 * T) + (c + 1)))
                    if not (isinstance(i, int) and i == 0 and c == 0):
                        pe.wait_ge(S("hT_act"), upto("hT_act", l, i * (2 * T) + c))
                    for b in range(4):
                        o = tr(ps[:, 4, P * b:P * b + P], hp[:, c % 2, P * b:P * b + P], ident)
                    o.then_inc(S("hT_pe"), 1)

                def down(i, c):
                    par, j = divmod(c, T)
                    pe.wait_ge(S("hT_act"), upto("hT_act", l, i * (2 * T) + (c + 1)))
                    if j == 0:
                        s = 3 * par + 2
                        pe.wait_ge(S(f"slot{s}"), (i + 1) * 16 + 16 * static_loads(l, s))
                    if not (isinstance(i, int) and i == 0 and c == 0):
                        pe.wait_ge(S("acc_dve"), upto("acc_dve", l, i * (2 * T) + c))
                    W = slots[3 * par + 2].rearrange("p (k c) -> p k c", k=4)
                    for hf in range(2):
                        for k in range(4):
                            o = mm(ps[:, 5 + hf, :], hT[:, c % 2, k, :], W[:, k, 512 * hf:512 * hf + 512],
                                   start=k == 0, stop=k == 3)
                    o.then_inc(S("dn_pe"), 1)

                def body(i, last):
                    for c in range(2 * T):
                        if c + 1 < 2 * T:
                            gate_up(i, c + 1)
                        elif not last:
                            gate_up(i + 1, 0)
                        turn(i, c)
                        down(i, c)

                gate_up(0, 0)
                body(0, False)
                with pe.Fori(1, NE // 2 - 1) as i:
                    body(i, False)
                body(NE // 2 - 1, True)

            for l in range(DEPTH):
                modulation(l)
                norm_transpose(l, "a", range(NT))
                project(l)
                turn_operands(l)
                decay_sums(l)
                scan(l)
                attention(l)
                output(l)
                norm_transpose(l, "f", tiles(l))
                router(l)
                gate_rows(l, 1)
                experts(l)

        @block.scalar
        def _(act):
            A = nc.scalar.activation
            chain = [0]

            def link(ins):
                chain[0] += 1
                ins.then_inc(S("act_chain"), 1)
                act.wait_ge(S("act_chain"), chain[0])

            act.wait_ge(S("ld_cond"), 16)
            A(silT[:, :, :], condT[:, :, :], ACT.Silu).then_inc(S("sil"), 1)

            def square_rows(l, which, ts):
                for t in ts:
                    A(tokA[:, t, :], h[:, t, :], ACT.Square, accum_out=stat[:, t:t + 1]).then_inc(S(which + "_sq"), 1)

            def norm_evac(l, which, ts):
                m = 0 if which == "a" else 1
                act.wait_ge(S("modA"), upto("modA", l, 1))
                for k in range(0, KD):
                    act.wait_ge(S(which + "_tr"), upto(which + "_tr", l, k + 1))
                    for n, seg in enumerate((segs(l) if which == 'f' else [0, 1])):
                        c = slice(CTX * seg, CTX * seg + CTX)
                        i = A(featT[:, k, c], ps[:, 1 + k % 4, c], ACT.Identity,
                              scale=modA[:, m, k, seg:seg + 1], bias=mod[:, 24 * m + k, seg:seg + 1])
                    i.then_inc(S(which + "_evac"), 1)

            def project(l):
                jobs = in_jobs(l)
                nconv = 0
                act.wait_ge(S("pad_zero"), upto("pad_zero", l, 1))
                for n, (name, kind, i, eng) in enumerate(jobs):
                    if eng != "A":
                        continue
                    act.wait_ge(S("in_pe"), upto("in_pe", l, n + 1))
                    bank = ps[:, n % 4, :]
                    if kind == "f":
                        if l < DEPTH - 1 or i != 5:
                            A(xpad[:, i, :, 1:CTX + 1], heads(bank, 2), ACT.Identity).then_inc(S("in_act"), 1)
                        else:
                            A(xpad[:, i, 1, 1:CTX + 1], bank[:, CTX:TOK], ACT.Identity).then_inc(S("in_act"), 1)
                    elif name == "ret_vg":
                        o = A(ret(XV[:, i, :], HD).rearrange("p g (j c) -> p j g c", j=2),
                              bank[:, 0:256].rearrange("p (j g c) -> p j g c", j=2, g=2), ACT.Identity)
                        if i in tiles(l):
                            o = A(tokA[:, i, 0:256], bank[:, 256:512], ACT.Silu)
                        o.then_inc(S("in_act"), 1)
                    else:
                        A(tokA[:, i, 256:768], bank, ACT.Silu).then_inc(S("in_act"), 1)
                for n, f in enumerate((4, 5, 0, 1, 2, 3)):
                    act.wait_ge(S("conv_dve"), upto("conv_dve", l, n + 1))
                    dst = xT[:, f, :] if f < 4 else BCT[:, f - 4, :]
                    if f == 5 and l == DEPTH - 1:
                        dst = dst[:, CTX:TOK]
                    A(dst, dst, ACT.Silu).then_inc(S("conv_act"), 1)

            def na_norm(l):
                for t in range(NT):
                    lo = 0 if t in tiles(l) else 256
                    act.wait_ge(S("in_dve"), upto("in_dve", l, dve_jobs_done(l, "na_qk", t)))
                    if t > 0:
                        act.wait_ge(S("na_ss"), upto("na_ss", l, t))
                    A(sq[:, lo:512], nqk[:, t, lo:512], ACT.Square).then_inc(S("na_sq"), 1)

            def turn_operands(l):
                for n, f in enumerate((4, 0, 1, 2, 3)):
                    act.wait_ge(S("x_tr"), upto("x_tr", l, n + 1))
                    src = heads(ps[:, 4 + n % 2, :], NT)
                    c = P * f + P * (f // 2)
                    dst = Bt[:, :, :] if f == 4 else XV[:, :, c:c + P]
                    A(dst, src, ACT.Identity).then_inc(S("x_evac"), 1)
                for t in range(NT):
                    lo = 0 if t in tiles(l) else 2
                    act.wait_ge(S("ret_tr"), upto("ret_tr", l, t + 1))
                    A(retT[:, lo:4, P * t:P * t + P], heads(ps[:, 6 + t % 2, :], 4)[:, lo:4, :],
                      ACT.Identity).then_inc(S("ret_evac"), 1)
                for t in range(NT):
                    lo = 0 if t in tiles(l) else 2
                    act.wait_ge(S("naT_tr"), upto("naT_tr", l, t + 1))
                    A(naT[:, lo:4, P * t:P * t + P], heads(ps[:, t % 2, :], 4)[:, lo:4, :],
                      ACT.Identity).then_inc(S("naT_evac"), 1)

            def softplus(l):
                act.wait_ge(S("ld_rowp"), upto("ld_rowp", l, 16))
                A(nA[:, :, :], heads(rowp[:, R_DEC:R_DEC + 24], 2), ACT.Exp).then_inc(S("nA_act"), 1)
                act.wait_ge(S("dt_abs"), upto("dt_abs", l, 1))
                link(A(dta[:, :, :], dta[:, :, :], ACT.Exp, scale=-1.0))
                A(dta[:, :, :], dta[:, :, :], ACT.Ln, bias=1.0).then_inc(S("dt_ln"), 1)

            def scan(l):
                act.wait_ge(S("cum_pe"), upto("cum_pe", l, 1))
                A(EX, ps[:, 2, 0:288], ACT.Exp).then_inc(S("ex_act"), 1)
                act.wait_ge(S("seg_pe"), upto("seg_pe", l, 1))
                A(Eret[:, :, :], heads(ps[:, 6, :], 4), ACT.Exp).then_inc(S("e_act"), 1)

                def decays(n):
                    act.wait_ge(S("seg_pe"), upto("seg_pe", l, n + 2))
                    if n > 0:
                        act.wait_ge(S("mf_dve"), upto("mf_dve", l, 2 * n))
                        act.wait_ge(S("mb_pool"), upto("mb_pool", l, 2 * n))
                    A(E[:, :, :], heads(flat(6, 1024), SSD_H), ACT.Exp).then_inc(S("e_act"), 1)

                ts = tiles(l)
                decays(0)
                for n in range(len(ts)):
                    if n + 1 < len(ts):
                        decays(n + 1)
                    act.wait_ge(S("yz_dve"), upto("yz_dve", l, n + 1))
                    A(heads(sq, 2), ssd(line(y2), HD), ACT.Square,
                      accum_out=stat[:, 8 + n:9 + n]).then_inc(S("yss_act"), 1)

            def attention(l):
                for n, (t, hd) in enumerate(att_units(l)):
                    keys = TOK if t >= 2 else CTX
                    act.wait_ge(S("mx_dve"), upto("mx_dve", l, n + 1))
                    if n >= 2:
                        act.wait_ge(S("pt_pe"), upto("pt_pe", l, n - 1))
                    A(Pm[:, n % 2, 0:keys], ps[:, n % 2, 0:keys], ACT.Exp, bias=nmx[:, n:n + 1],
                      accum_out=nsum[:, n:n + 1]).then_inc(S("p_act"), 1)

            def mixT(l):
                ts = tiles(l)
                lo, hi = P * ts[0], P * ts[-1] + P
                for k in range(KD):
                    act.wait_ge(S("mix_tr"), upto("mix_tr", l, k + 1))
                    A(featT[:, k, lo:hi], ps[:, 6 + k % 2, lo:hi], ACT.Identity).then_inc(S("mixT"), 1)

            def gate_rows(l, which):
                act.wait_ge(S(f"row{which}_pe"), upto(f"row{which}_pe", l, 1))
                for seg in segs(l):
                    A(grow[:, seg, :], flat(2 * seg, 1024), ACT.Identity).then_inc(S(f"row{which}"), 1)

            def affinities(l):
                ts = tiles(l)
                act.wait_ge(S("rt_pe"), upto("rt_pe", l, 1))
                A(aff[:, ts[0]:NT, :], heads(ps[:, 0, NE * ts[0]:NE * NT], len(ts)),
                  ACT.Sigmoid).then_inc(S("rt_act"), 1)

            def experts(l):
                T = len(tiles(l))

                def silu(i, c):
                    act.wait_ge(S("gu_pe"), upto("gu_pe", l, i * (2 * T) + (c + 1)))
                    if not (isinstance(i, int) and i == 0 and c < 2):
                        act.wait_ge(S("hp_dve"), upto("hp_dve", l, i * (2 * T) + (c - 1)))
                    A(hs[:, c % 2, :], ps[:, 2 * (c % 2), :], ACT.Silu).then_inc(S("hs_act"), 1)

                def evac(i, c):
                    act.wait_ge(S("hT_pe"), upto("hT_pe", l, i * (2 * T) + (c + 1)))
                    if not (isinstance(i, int) and i == 0 and c < 2):
                        act.wait_ge(S("dn_pe"), upto("dn_pe", l, i * (2 * T) + (c - 1)))
                    A(hT[:, c % 2, :, :], heads(ps[:, 4, :], 4), ACT.Identity).then_inc(S("hT_act"), 1)

                def body(i, last):
                    for c in range(2 * T):
                        if c + 1 < 2 * T:
                            silu(i, c + 1)
                        elif not last:
                            silu(i + 1, 0)
                        evac(i, c)

                silu(0, 0)
                body(0, False)
                with act.Fori(1, NE // 2 - 1) as i:
                    body(i, False)
                body(NE // 2 - 1, True)

            for l in range(DEPTH):
                if l == 0:
                    act.wait_ge(S("ld_h0"), 16)
                    act.wait_ge(S("ld_h1"), 16)
                else:
                    act.wait_ge(S("h_end"), upto("h_end", l - 1, NT))
                square_rows(l, "a", range(NT))
                norm_evac(l, "a", range(NT))
                project(l)
                na_norm(l)
                softplus(l)
                turn_operands(l)
                scan(l)
                attention(l)
                mixT(l)
                gate_rows(l, 0)
                act.wait_ge(S("res_dve"), upto("res_dve", l, 2 * len(tiles(l))))
                square_rows(l, "f", tiles(l))
                norm_evac(l, "f", tiles(l))
                affinities(l)
                gate_rows(l, 1)
                experts(l)

        @block.vector
        def _(dve):
            V = nc.vector
            chain = [0]

            def link(ins):
                chain[0] += 1
                ins.then_inc(S("dve_chain"), 1)
                dve.wait_ge(S("dve_chain"), chain[0])

            def after(ins, name, l, n):
                ins.then_inc(S(name), 1)
                dve.wait_ge(S(name), upto(name, l, n))

            def modulation(l):
                dve.wait_ge(S("ld_colp"), upto("ld_colp", l, 16))
                dve.wait_ge(S("mod_pe"), upto("mod_pe", l, N_MOD))
                after(V.tensor_tensor(mod[:, :, :], heads(ps[:, 0, 0:96], 48),
                                      spread(colp[:, L_BMOD:L_BMOD + 48], 2), ALU.add), "mod_evac", l, 1)
                for m, c in ((0, L_NMIX), (1, L_NFFN)):
                    i = V.scalar_tensor_tensor(modA[:, m, :, :], mod[:, 24 * m + 8:24 * m + 16, :], 1.0,
                                               spread(colp[:, c:c + 8], 2), ALU.add, ALU.mult)
                i.then_inc(S("modA"), 1)

            def norm_rows(l, which, ts):
                n = len(ts)
                a = slice(ts[0], ts[0] + n)
                dve.wait_ge(S(which + "_sq"), upto(which + "_sq", l, n))
                V.tensor_scalar(stat2[:, a], stat[:, a], 1.0 / D, EPS, ALU.mult, ALU.add
                                ).then_inc(S(which + "_ms"), 1)
                dve.wait_ge(S(which + "_rs"), upto(which + "_rs", l, 1))
                for t in ts:
                    V.tensor_scalar(tokA[:, t, :], h[:, t, :], stat2[:, t:t + 1], None, ALU.mult
                                    ).then_inc(S(which + "_hn"), 1)

            def project(l):
                jobs = in_jobs(l)
                for n, (name, kind, i, eng) in enumerate(jobs):
                    if eng != "D":
                        continue
                    dve.wait_ge(S("in_pe"), upto("in_pe", l, n + 1))
                    bank = ps[:, n % 4, :]
                    if kind == "dt":
                        dve.wait_ge(S("ld_rowp"), upto("ld_rowp", l, 16))
                        V.tensor_tensor(dtr.rearrange("p (t d) h -> p t (d h)", t=NT), heads(bank[:, 0:64], NT),
                                        repeat(rowp[:, R_DTB:R_DTB + 16], NT), ALU.add).then_inc(S("in_dve"), 1)
                        dve.wait_ge(S("in_dve"), upto("in_dve", l, 1))
                        V.scalar_tensor_tensor(dta[:, :, :], dtr[:, :, :], -1.0, dtr[:, :, :], ALU.mult, ALU.max
                                               ).then_inc(S("dt_abs"), 1)
                        convolve(l)
                        continue
                    lo, hi = cols_needed(l, name, i)
                    dst = {"ret_qk": qk, "na_qk": nqk, "na_v": nav}[name]
                    V.tensor_copy(dst[:, i, lo:hi], bank[:, lo:hi]).then_inc(S("in_dve"), 1)

            def convolve(l):
                for n, f in enumerate((4, 5, 0, 1, 2, 3)):
                    dve.wait_ge(S("in_act"), upto("in_act", l, n + 1))
                    full = l < DEPTH - 1 or f != 5
                    dst = heads(xT[:, f, :] if f < 4 else BCT[:, f - 4, :], 2)
                    sg = slice(0, 2) if full else slice(1, 2)
                    w = [colp[:, L_CW + 3 * f + j:L_CW + 3 * f + j + 1] for j in range(3)]
                    src = [xpad[:, f, sg, j:j + CTX] for j in range(3)]
                    link(V.tensor_scalar(dst[:, sg, :], src[0], w[0], colp[:, L_CB + f:L_CB + f + 1],
                                         ALU.mult, ALU.add))
                    link(V.scalar_tensor_tensor(dst[:, sg, :], src[1], w[1], dst[:, sg, :], ALU.mult, ALU.add))
                    V.scalar_tensor_tensor(dst[:, sg, :], src[2], w[2], dst[:, sg, :], ALU.mult, ALU.add
                                           ).then_inc(S("conv_dve"), 1)

            def na_norm(l):
                ts = tiles(l)
                for t in range(NT):
                    lo = 0 if t in ts else 4
                    dve.wait_ge(S("na_sq"), upto("na_sq", l, t + 1))
                    V.tensor_reduce(rs[:, t, lo:8], heads(sq, 8)[:, lo:8, :], AX.X, ALU.add
                                    ).then_inc(S("na_ss"), 1)
                dve.wait_ge(S("na_ss"), upto("na_ss", l, NT))
                V.tensor_scalar(rs[:, :, 4:8], rs[:, :, 4:8], 1.0 / HD, EPS, ALU.mult, ALU.add)
                V.tensor_scalar(rs[:, ts[0]:NT, 0:4], rs[:, ts[0]:NT, 0:4], 1.0, HD * EPS, ALU.mult, ALU.add
                                ).then_inc(S("na_ms"), 1)
                dve.wait_ge(S("na_rs"), upto("na_rs", l, 1))
                for t in range(NT):
                    lo = 0 if t in ts else 4
                    v = heads(nqk[:, t, :], 8)[:, lo:8, :]
                    link(V.tensor_tensor(v, v, spread(rs[:, t, lo:8], HD), ALU.mult))
                    V.tensor_tensor(v, v, heads(rowp[:, R_NQK:R_NQK + 512], 8)[:, lo:8, :], ALU.mult
                                    ).then_inc(S("na_norm"), 1)

            def log_decays(l):
                dve.wait_ge(S("nA_act"), upto("nA_act", l, 1))
                link(V.memset(DTX[:, :, :], SCALE))
                n6 = nA.rearrange("p d (g h) -> p (d g) h", g=2)
                V.tensor_scalar(n6[:, :, 0:4], n6[:, :, 0:4], -1.0, None, ALU.mult)
                link(V.tensor_scalar(n6[:, :, 4:6], n6[:, :, 4:6], -1.0 / SCALE, None, ALU.mult))
                dve.wait_ge(S("dt_ln"), upto("dt_ln", l, 1))
                by6 = DTX.rearrange("p a (g h) -> p (a g) h", g=2)[:, :, 0:4]
                by4 = [v.rearrange("p a (g h) -> p (a g) h", g=2) for v in (dtr, dta)]
                link(V.scalar_tensor_tensor(by6, by4[0], 0.0, by4[1], ALU.max, ALU.add))
                V.tensor_tensor(Aall.rearrange("p (t d) h -> p t (d h)", t=NT),
                                DTX.rearrange("p (t d) h -> p t (d h)", t=NT),
                                repeat(nA.rearrange("p d h -> p (d h)"), NT), ALU.mult).then_inc(S("loga"), 1)
                dve.wait_ge(S("loga"), upto("loga", l, 1))

            def ret_triangle(l):
                dve.wait_ge(S("x_evac"), upto("x_evac", l, 5))
                V.tensor_tensor(*triangle_rows(rf[:, 0:RET_H, :], ret(Aall[:, 0, :]), 2, LE), ALU.mult
                                ).then_inc(S("rf_dve"), 1)

            def triangle(l, n):
                t = tiles(l)[n]
                dve.wait_ge(S("seg_pe"), upto("seg_pe", l, n + 1))
                V.tensor_tensor(*triangle_rows(rf, ssd(Aall[:, 2 * t, :]), 4, LE), ALU.mult
                                ).then_inc(S("rf_dve"), 1)

            def chunk_weights(l):
                dve.wait_ge(S("ex_act"), upto("ex_act", l, 1))
                for d in range(2):
                    V.tensor_tensor(Wt[:, d, :, :], heads(EX[:, 96 + 48 * d:144 + 48 * d], NT),
                                    DTX[:, d:2 * NT:2, :], ALU.mult)
                T = heads(EX[:, 192:288], 2 * NT)
                V.tensor_copy(Dec[0:64, :, :], T[0:64, :, 0:6])
                link(V.tensor_copy(Dec[64:128, :, :], T[64:128, :, 6:12]))
                dve.wait_ge(S("e_act"), upto("e_act", l, 1))
                link(V.tensor_tensor(Eret[:, :, :], Eret[:, :, :], repeat(const[:, C_DRET:C_DRET + P], RET_H), ALU.mult))

            def states(l):
                def weigh(n):
                    d, t = STATE_STEPS[n]
                    if n > 0:
                        dve.wait_ge(S("st_pe"), upto("st_pe", l, n))
                    V.tensor_tensor(VW[:, :, :], heads(XV[:, t, :], NH), spread(Wt[:, d, t, :], HD), ALU.mult
                                    ).then_inc(S("vw_dve"), 1)

                weigh(0)
                for n, (d, t) in enumerate(STATE_STEPS):
                    if n + 1 < len(STATE_STEPS):
                        weigh(n + 1)
                    else:
                        dve.wait_ge(S("st_pe"), upto("st_pe", l, n + 1))
                    bank = ps[:, 3 + n % 2, 0:384]
                    new = Hs[:, d, STATE_NEXT[d, t], :]
                    if n < 2:
                        V.tensor_copy(new, bank).then_inc(S("h_dve"), 1)
                    else:
                        if n == 2:
                            dve.wait_ge(S("h_dve"), upto("h_dve", l, 2))
                        else:
                            dve.wait_ge(S("h_dve"), upto("h_dve", l, n - 1))
                        link(V.tensor_tensor(heads(new, 6), heads(Hs[:, d, t, :], 6),
                                             spread(Dec[:, 2 * t + d, :], HD), ALU.mult))
                        V.tensor_tensor(new, new, bank, ALU.add).then_inc(S("h_dve"), 1)

            def scan_head(l, n):
                dve.wait_ge(S("sc_pe"), upto("sc_pe", l, n + 1))
                if n > 0:
                    dve.wait_ge(S("mb_pool"), upto("mb_pool", l, 2 * n))
                    dve.wait_ge(S("mf_dve"), upto("mf_dve", l, 2 * n))
                s = ps[:, 6:8, 0:P]
                V.tensor_tensor(sL[:, :, :], s, repeat(GE, 2), ALU.mult).then_inc(S("sl_dve"), 1)
                link(V.tensor_tensor(sU[:, :, :], s, repeat(LE, 2), ALU.mult))
                if n > 0:
                    dve.wait_ge(S("y_pe"), upto("y_pe", l, n))
                two = lambda v: v.rearrange("p (g h) c -> p g (h c)", g=2)
                V.tensor_tensor(two(Mret), two(Eret), ps[:, 6:8, P:3 * P], ALU.mult
                                ).then_inc(S("mret_dve"), 1)
                dve.wait_ge(S("e_act"), upto("e_act", l, n + 2))
                for g in range(2):
                    if n > 0:
                        dve.wait_ge(S("diag_pe"), upto("diag_pe", l, 2 * n - 1 + g))
                    V.tensor_tensor(Mf[:, g, :, :], E[:, 4 * g:4 * g + 4, :], repeat(sU[:, g, :], 4), ALU.mult
                                    ).then_inc(S("mf_dve"), 1)
                if n + 1 < len(tiles(l)):
                    triangle(l, n + 1)

            def scan_tail(l, n):
                t = tiles(l)[n]
                dve.wait_ge(S("y_pe"), upto("y_pe", l, n + 1))
                ds = dirs_of(t)
                places = lambda v: v.rearrange("p (g h) c -> p g h c", g=2)
                bank2 = lambda b: ps[:, b:b + 2, 0:384].rearrange("p g (h c) -> p g h c", h=6)
                for k, d in enumerate(ds):
                    at = 48 * d + NH * t
                    link(V.tensor_tensor(places(y if k == 0 else y2), bank2(2 + 2 * d),
                                         spread2(heads(EX[:, at:at + NH], 2), HD), ALU.mult))
                after(V.tensor_tensor(places(y), places(y), bank2(0), ALU.add), "comb_dve", l, n + 1)
                if len(ds) == 2:
                    link(V.tensor_tensor(y[:, :, :], y[:, :, :], y2[:, :, :], ALU.add))
                ys, y2s = ssd(line(y), HD), ssd(line(y2), HD)
                dve.wait_ge(S("dx_pool"), upto("dx_pool", l, n + 1))
                link(V.tensor_tensor(ys, ys, heads(line(dx), 2), ALU.add))
                V.tensor_tensor(y2s, ys, heads(tokA[:, t, 256:768], 2), ALU.mult).then_inc(S("yz_dve"), 1)
                four = lambda v: v.rearrange("p g (h c) -> p g h c", h=2)
                yr, sqr = four(ret(line(y), HD)), four(ret(line(y2), HD))
                mu, var = heads(stat2[:, 8:12], 2), heads(stat2[:, 16:20], 2)
                link(V.tensor_reduce(mu, yr, AX.X, ALU.add))
                link(V.tensor_scalar(mu, mu, -1.0 / HD, None, ALU.mult))
                link(V.tensor_tensor(yr, yr, spread2(mu, HD), ALU.add))
                link(V.tensor_tensor(sqr, yr, yr, ALU.mult))
                link(V.tensor_reduce(var, sqr, AX.X, ALU.add))
                V.tensor_scalar(var, var, 1.0 / HD, EPS, ALU.mult, ALU.add)
                dve.wait_ge(S("yss_act"), upto("yss_act", l, n + 1))
                V.tensor_scalar(stat2[:, 20:21], stat[:, 8 + n:9 + n], 1.0 / (SSD_H * HD), EPS, ALU.mult, ALU.add
                                ).then_inc(S("gn_ms"), 1)
                dve.wait_ge(S("gn_rs"), upto("gn_rs", l, n + 1))
                V.scalar_tensor_tensor(heads(tokA[:, t, 256:768], 2), y2s, stat2[:, 20:21],
                                       heads(rowp[:, R_NORM:R_NORM + 512], 2), ALU.mult, ALU.mult)
                link(V.tensor_tensor(yr, yr, spread2(var, HD), ALU.mult))
                g = tokA[:, t, 0:256].rearrange("p (j g c) -> p g j c", j=2, g=2)
                link(V.tensor_tensor(g, yr, g, ALU.mult))

            def scan(l):
                ret_triangle(l)
                chunk_weights(l)
                triangle(l, 0)
                states(l)
                scan_head(l, 0)
                for n in range(len(tiles(l))):
                    if n + 1 < len(tiles(l)):
                        scan_head(l, n + 1)
                    scan_tail(l, n)

            def attention(l):
                dve.wait_ge(S("ld_bias"), upto("ld_bias", l, 16 * 2 * NA_H))
                b = bias.rearrange("p a b c -> p (a b) c")
                V.tensor_tensor(b, b, repeat(const[:, C_MASK:C_MASK + GRID], NA_H * 6), ALU.add
                                ).then_inc(S("bias_dve"), 1)
                un = att_units(l)

                def maximum(n):
                    keys = TOK if un[n][0] >= 2 else CTX
                    dve.wait_ge(S("s_pe"), upto("s_pe", l, n + 1))
                    V.tensor_reduce(nmx[:, n:n + 1], ps[:, n % 2, 0:keys], AX.X, ALU.max, negate=True
                                    ).then_inc(S("mx_dve"), 1)

                def turned(n):
                    nk = NT if un[n][0] >= 2 else 2
                    dve.wait_ge(S("pt_pe"), upto("pt_pe", l, n + 1))
                    if n >= 2:
                        dve.wait_ge(S("pv_pe"), upto("pv_pe", l, n - 1))
                    V.tensor_copy(PT[:, n % 2, 0:nk, :], heads(ps[:, 2 + n % 2, :], NT)[:, 0:nk, :]
                                  ).then_inc(S("pt_dve"), 1)

                def normalise(tile):
                    t = tiles(l)[tile]
                    c = slice(NA_H * tile, NA_H * tile + NA_H)
                    dve.wait_ge(S("pv_pe"), upto("pv_pe", l, NA_H * (tile + 1)))
                    link(V.reciprocal(nrec[:, c], nsum[:, c]))
                    o = V.tensor_tensor(heads(tokA[:, t, 768:1024], NA_H), heads(ps[:, 4 + tile % 2, 0:256], NA_H),
                                        spread(nrec[:, c], HD), ALU.mult)
                    o.then_inc(S("na_out"), 1)

                N = len(un)
                maximum(0)
                for n in range(N):
                    if n + 1 < N:
                        maximum(n + 1)
                    if n >= 1 and n % NA_H == 0:
                        normalise(n // NA_H - 1)
                    turned(n)
                normalise(N // NA_H - 1)

            def gate_diag(l, which):
                if which == 1:
                    dve.wait_ge(S("res_dve"), upto("res_dve", l, 2 * len(tiles(l))))
                for seg in segs(l):
                    c = 24 * which + 16
                    V.tensor_tensor(heads(diag[:, seg, :], KD), repeat(ident, KD),
                                    spread(mod[:, c:c + 8, seg], P), ALU.mult).then_inc(S(f"diag{which}"), 1)

            def residual(l):
                dve.wait_ge(S("row0"), upto("row0", l, len(segs(l))))
                ts = tiles(l)
                n = 0
                for half in range(N_OUT):
                    c = slice(512 * half, 512 * half + 512)
                    for t in ts:
                        dve.wait_ge(S("out_pe"), upto("out_pe", l, n + 1))
                        link(V.tensor_tensor(Pm[:, n % 2, :], grow[:, t // 2, c], ps[:, 4 + n % 2, :], ALU.mult))
                        V.tensor_tensor(h[:, t, c], h[:, t, c], Pm[:, n % 2, :], ALU.add).then_inc(S("res_dve"), 1)
                        n += 1

            def route(l):
                ts = tiles(l)
                T = len(ts)
                t0 = ts[0]
                dve.wait_ge(S("ld_rb"), 16)
                dve.wait_ge(S("rt_act"), upto("rt_act", l, 1))
                se = sel.rearrange("p (t g) e -> p t (g e)", t=NT)[:, t0:NT, :]
                af = aff[:, t0:NT, :]
                link(V.tensor_tensor(se, af, repeat(rb[:, :], T), ALU.add))
                s4 = sel[:, 4 * t0:4 * NT, :]
                fl = lambda v: v.rearrange("p t g -> p (t g)")[:, 4 * t0:4 * NT]
                a, b, c, d = fl(g1), fl(g2), fl(g3), fl(g4)
                e = [s4[:, :, j] for j in range(4)]
                link(V.tensor_tensor(a, e[0], e[1], ALU.add))
                link(V.tensor_tensor(b, e[2], e[3], ALU.add))
                link(V.tensor_tensor(a, a, b, ALU.max))
                link(V.tensor_tensor(b, e[0], e[1], ALU.max))
                link(V.tensor_tensor(c, e[2], e[3], ALU.max))
                link(V.tensor_tensor(b, b, c, ALU.add))
                link(V.tensor_tensor(a, a, b, ALU.max))

                def rank(v, n, out):
                    other = v.unsqueeze(2).to_broadcast([P, n, 4, 4])
                    own = v.unsqueeze(3).to_broadcast([P, n, 4, 4])
                    x1 = cmp1[:, 0:n, :].rearrange("p n (i j) -> p n i j", i=4)
                    x2 = cmp2[:, 0:n, :].rearrange("p n (i j) -> p n i j", i=4)
                    link(V.tensor_tensor(x1, other, own, ALU.is_gt))
                    link(V.tensor_tensor(x2, other, own, ALU.is_equal))
                    link(V.tensor_tensor(cmp2[:, 0:n, :], cmp2[:, 0:n, :],
                                         repeat(const[:, C_TRI:C_TRI + 16], n), ALU.mult))
                    link(V.tensor_tensor(cmp1[:, 0:n, :], cmp1[:, 0:n, :], cmp2[:, 0:n, :], ALU.add))
                    link(V.tensor_reduce(out, x1, AX.X, ALU.add))

                rank(g1[:, t0:NT, :], T, g4[:, t0:NT, :])
                link(V.tensor_scalar(d, d, 0.5, None, ALU.is_lt))
                rank(s4, 4 * T, cnt[:, 0:4 * T, :])
                cn = cnt[:, 0:4 * T, :]
                link(V.tensor_scalar(cn, cn, 1.5, None, ALU.is_lt))
                link(V.tensor_tensor(cn, cn, spread(d, 4), ALU.mult))
                ga = gates[:, t0:NT, :]
                link(V.tensor_tensor(ga, af, cn.rearrange("p (t g) e -> p t (g e)", t=T), ALU.mult))
                link(V.tensor_reduce(rsum[:, t0:NT], ga, AX.X, ALU.add))
                link(V.reciprocal(rsum[:, t0:NT], rsum[:, t0:NT]))
                link(V.tensor_tensor(ga, ga, spread(rsum[:, t0:NT], NE), ALU.mult))

            def experts(l):
                ts = tiles(l)
                T = len(ts)
                dve.wait_ge(S("acc_zero"), upto("acc_zero", l, 1))

                def product(i, c):
                    dve.wait_ge(S("hs_act"), upto("hs_act", l, i * (2 * T) + (c + 1)))
                    if not (isinstance(i, int) and i == 0 and c < 2):
                        dve.wait_ge(S("hT_pe"), upto("hT_pe", l, i * (2 * T) + (c - 1)))
                    V.tensor_tensor(hp[:, c % 2, :], hs[:, c % 2, :], ps[:, 2 * (c % 2) + 1, :], ALU.mult
                                    ).then_inc(S("hp_dve"), 1)

                def accumulate(i, c):
                    par, j = divmod(c, T)
                    t = ts[j]
                    dve.wait_ge(S("dn_pe"), upto("dn_pe", l, i * (2 * T) + (c + 1)))
                    if not (isinstance(i, int) and i == 0 and c == 0):
                        dve.wait_ge(S("acc_dve"), upto("acc_dve", l, i * (2 * T) + c))
                    gate = gates[:, t, bass.ds(i * 2 + par, 1)]
                    V.scalar_tensor_tensor(tokA[:, t, :], flat(5, 1024), gate, tokA[:, t, :], ALU.mult, ALU.add
                                           ).then_inc(S("acc_dve"), 1)

                def body(i, last):
                    for c in range(2 * T):
                        if c + 1 < 2 * T:
                            product(i, c + 1)
                        elif not last:
                            product(i + 1, 0)
                        accumulate(i, c)

                product(0, 0)
                body(0, False)
                with dve.Fori(1, NE // 2 - 1) as i:
                    body(i, False)
                body(NE // 2 - 1, True)
                dve.wait_ge(S("row1"), upto("row1", l, len(segs(l))))
                dve.wait_ge(S("acc_dve"), upto("acc_dve", l, NE * T))
                for t in ts:
                    link(V.tensor_tensor(tokA[:, t, :], tokA[:, t, :], grow[:, t // 2, :], ALU.mult))
                    V.tensor_tensor(h[:, t, :], h[:, t, :], tokA[:, t, :], ALU.add).then_inc(S("h_end"), 1)

            dve.wait_ge(S("ld_const"), 16)
            for l in range(DEPTH):
                modulation(l)
                norm_rows(l, "a", range(NT))
                project(l)
                na_norm(l)
                log_decays(l)
                scan(l)
                attention(l)
                gate_diag(l, 0)
                residual(l)
                norm_rows(l, "f", tiles(l))
                route(l)
                gate_diag(l, 1)
                experts(l)

        @block.gpsimd
        def _(pool):
            G = nc.gpsimd
            chain = [0]

            def link(ins):
                chain[0] += 1
                ins.then_inc(S("pool_chain"), 1)
                pool.wait_ge(S("pool_chain"), chain[0])

            def rsqrt(v, n):
                return G.tensor_tensor(v, v, pw[:, 0:n], ALU.pow)

            def rope(l):
                for n, t in enumerate((2, 3)):
                    pool.wait_ge(S("in_dve"), upto("in_dve", l, dve_jobs_done(l, "ret_qk", t)))
                    v = heads(qk[:, t, :], 8)
                    a = heads(y.rearrange("p a b -> p (a b)")[:, 0:512], 8)
                    b = heads(y2.rearrange("p a b -> p (a b)")[:, 0:512], 8)
                    cos = const[:, C_COS + 64 * n:C_COS + 64 * n + 64]
                    sin = heads(const[:, C_SIN + 64 * n:C_SIN + 64 * n + 64], 2)
                    link(G.tensor_tensor(a, v, repeat(cos, 8), ALU.mult))
                    for half in range(2):
                        o, s = slice(16 * half, 16 * half + 16), slice(16 - 16 * half, 32 - 16 * half)
                        parts = lambda w, c: w.rearrange("p a (b c) -> p a b c", b=2)[:, :, :, c]
                        link(G.tensor_tensor(parts(b, o), parts(v, s),
                                             sin[:, :, o].unsqueeze(1).to_broadcast([P, 8, 2, 16]), ALU.mult))
                    G.tensor_tensor(v, a, b, ALU.add).then_inc(S("rope"), 1)
                    pool.wait_ge(S("rope"), upto("rope", l, n + 1))

            def triangle(l, n):
                if n < 0:
                    pool.wait_ge(S("loga"), upto("loga", l, 1))
                    pool.wait_ge(S("x_evac"), upto("x_evac", l, 5))
                    G.tensor_tensor(*triangle_rows(rbk[:, 0:RET_H, :], ret(Aall[:, 1, :]), 2, GE), ALU.mult
                                    ).then_inc(S("rb_pool"), 1)
                    return
                t = tiles(l)[n]
                pool.wait_ge(S("seg_pe"), upto("seg_pe", l, n + 1))
                G.tensor_tensor(*triangle_rows(rbk, ssd(Aall[:, 2 * t + 1, :]), 4, GE), ALU.mult
                                ).then_inc(S("rb_pool"), 1)

            def scan_head(l, n):
                t = tiles(l)[n]
                if n > 0:
                    pool.wait_ge(S("diag_pe"), upto("diag_pe", l, 2 * n))
                v = ssd(XV[:, t, :], HD).rearrange("p g (h c) -> p g h c", h=4)
                by_group = lambda w: w.rearrange("p (g h) c -> p g h c", g=2)
                G.tensor_tensor(by_group(Vf), v, spread2(ssd(DTX[:, 2 * t, :]), HD), ALU.mult)
                G.tensor_tensor(by_group(Vb), v, spread2(ssd(DTX[:, 2 * t + 1, :]), HD), ALU.mult
                                ).then_inc(S("v_pool"), 1)
                pool.wait_ge(S("sl_dve"), upto("sl_dve", l, n + 1))
                pool.wait_ge(S("e_act"), upto("e_act", l, n + 2))
                for g in range(2):
                    G.tensor_tensor(Mb[:, g, :, :], E[:, 4 * g:4 * g + 4, :], repeat(sL[:, g, :], 4), ALU.mult
                                    ).then_inc(S("mb_pool"), 1)
                if n + 1 < len(tiles(l)):
                    triangle(l, n + 1)

            def scan_tail(l, n):
                t = tiles(l)[n]
                if n > 0:
                    pool.wait_ge(S("yz_dve"), upto("yz_dve", l, n))
                G.tensor_tensor(dx.rearrange("p (g h) c -> p g h c", g=2),
                                ssd(XV[:, t, :], HD).rearrange("p g (h c) -> p g h c", h=4),
                                spread2(heads(rowp[:, R_D:R_D + SSD_H], 2), HD), ALU.mult).then_inc(S("dx_pool"), 1)
                pool.wait_ge(S("gn_ms"), upto("gn_ms", l, n + 1))
                rsqrt(stat2[:, 16:21], 5).then_inc(S("gn_rs"), 1)

            link(G.memset(pw[:, :], -0.5))
            pool.wait_ge(S("ld_const"), 16)
            for l in range(DEPTH):
                ts = tiles(l)
                if l > 0:
                    pool.wait_ge(S("dn_pe"), upto("dn_pe", l - 1, NE * len(tiles(l - 1))))
                for c in (0, CTX + 1):
                    i = G.memset(xpad[:, :, :, c:c + 1], 0.0)
                i.then_inc(S("pad_zero"), 1)
                pool.wait_ge(S("a_ms"), upto("a_ms", l, 1))
                rsqrt(stat2[:, 0:NT], NT).then_inc(S("a_rs"), 1)
                rope(l)
                pool.wait_ge(S("na_ms"), upto("na_ms", l, 1))
                G.tensor_tensor(rs[:, :, 4:8], rs[:, :, 4:8], pw[:, 0:16].rearrange("p (a b) -> p a b", a=NT), ALU.pow)
                G.tensor_tensor(rs[:, ts[0]:NT, 0:4], rs[:, ts[0]:NT, 0:4],
                                pw[:, 0:4 * len(ts)].rearrange("p (a b) -> p a b", b=4), ALU.pow
                                ).then_inc(S("na_rs"), 1)
                triangle(l, -1)
                triangle(l, 0)
                pool.wait_ge(S("ld_rowp"), upto("ld_rowp", l, 16))
                scan_head(l, 0)
                for n in range(len(ts)):
                    if n + 1 < len(ts):
                        scan_head(l, n + 1)
                    scan_tail(l, n)
                pool.wait_ge(S("f_ms"), upto("f_ms", l, 1))
                rsqrt(stat2[:, ts[0]:NT], len(ts)).then_inc(S("f_rs"), 1)
                pool.wait_ge(S("f_tr"), upto("f_tr", l, KD))
                G.memset(tokA[:, ts[0]:NT, :], 0.0).then_inc(S("acc_zero"), 1)


_RAW = ["x", "ctx", "w_mod", "w_in", "w_out", "na_rpb", "router_w", "router_b", "w_gate", "w_up", "w_down"]


def _layout(i):
    a = {k: np.ascontiguousarray(np.asarray(i[k])) for k in _RAW}
    a["x"], a["ctx"] = a["x"][0], a["ctx"][0]
    a["consts"] = shape_constants()
    col = lambda v: v.reshape(v.shape[0], -1, P).transpose(0, 2, 1)
    c = np.stack([np.asarray(i["c"])[0], np.asarray(i["c_ctx"])])[::-1]
    a["condT"] = np.ascontiguousarray(c.reshape(2, KD, P).transpose(2, 1, 0))
    cw = np.asarray(i["ssd_conv_w"])
    cw = cw.reshape(DEPTH, 3, 6, P).transpose(0, 3, 2, 1).reshape(DEPTH, P, 18)
    a["colp"] = np.ascontiguousarray(np.concatenate(
        [col(np.asarray(i["b_mod"])), col(np.asarray(i["norm_mix"])), col(np.asarray(i["norm_ffn"])), cw,
         col(np.asarray(i["ssd_conv_b"]))], axis=2))
    g = lambda k: np.asarray(i[k])
    qn = np.broadcast_to(g("na_q_norm")[:, None], (DEPTH, NA_H, HD)).reshape(DEPTH, -1)
    kn = np.broadcast_to(g("na_k_norm")[:, None], (DEPTH, NA_H, HD)).reshape(DEPTH, -1)

    def placed(d):
        s, r = g("ssd_a_log_" + d), g("ret_decay_" + d)
        return np.concatenate([s[:, 0:4], r[:, 0::2], s[:, 4:8], r[:, 1::2]], axis=1)

    a["rowp"] = np.ascontiguousarray(np.concatenate(
        [g("ssd_dt_bias_f"), g("ssd_dt_bias_b"), placed("f"), placed("b"), g("ssd_d"), qn, kn, g("ssd_norm")], axis=1))
    return a


def kernel(**inputs):
    import concourse.bacc as _bacc
    from concourse.bass_utils import run_bass_kernel_spmd as _run

    nc = _bacc.Bacc("TRN2", target_bir_lowering=False, num_devices=1)
    arrays = {f"in_{k}": v for k, v in _layout(inputs).items()}
    ins = {k[3:]: nc.dram_tensor(k, v.shape, mybir.dt.from_np(v.dtype), kind="ExternalInput").ap()
           for k, v in arrays.items()}
    out = nc.dram_tensor("out_0", (SEQ, D), F32, kind="ExternalOutput").ap()
    trunk(nc, ins, out)
    r = _run(nc, [arrays], core_ids=[0])
    return r.results[0]["out_0"].reshape(1, SEQ, D)
```

```python
from contextlib import ExitStack
import math

import numpy as np
import concourse.bass as bass
from concourse import mybir

F32 = mybir.dt.float32
U32 = mybir.dt.uint32
I32 = mybir.dt.int32
ALU = mybir.AluOpType
ACT = mybir.ActivationFunctionType
AX = mybir.AxisListType

P = 128
D = 1024
KD = D // P
DEPTH = 2
GRID = 64
CTX = 256
SEQ = 256
TOK = CTX + SEQ
NT = TOK // P
HD = 64
RET_H, SSD_H, NA_H = 4, 8, 4
NH = SSD_H + RET_H
STATE = 64
NE = 16
FE = 512
EPS = 1e-6
SCALE = HD ** -0.5
NEG = -1e30

IN_PIECES = (("bc_dt", 2048, 272), ("x", 1536, 512), ("ret_qk", 0, 512), ("ret_vg", 512, 512),
             ("z", 1024, 512), ("na_qk", 2320, 512), ("na_v", 2832, 256))
CAP = P
NO_ROW = NE * CAP
N_MOD = 12
N_OUT = 2
SLOT = 4096

C_ID, C_LE, C_GT, C_GE, C_LT, C_ONE, C_DRET, C_FLIP = (P * i for i in range(8))
C_MASK = 8 * P
C_COS = C_MASK + 64
C_SIN = C_COS + 128
C_TRI = C_SIN + 128
C_IOTA = C_TRI + 16
C_TOK = C_IOTA + P
C_EXP = C_TOK + 4
N_CONST = C_EXP + NE
L_BMOD, L_NMIX, L_NFFN, L_CW, L_CB = 0, 48, 56, 64, 82
N_COLP = 88
R_DTB, R_DEC, R_D, R_NQK, R_NORM = 0, 16, 40, 48, 560
N_ROWP = 1072


def shape_constants():
    c = np.zeros((P, N_CONST), np.float32)
    u = np.arange(P)[:, None]
    v = np.arange(P)[None, :]
    c[:, C_ID:C_ID + P] = u == v
    c[:, C_LE:C_LE + P] = u <= v
    c[:, C_GT:C_GT + P] = u > v
    c[:, C_GE:C_GE + P] = u >= v
    c[:, C_LT:C_LT + P] = u < v
    c[:, C_ONE:C_ONE + P] = 1.0
    c[:, C_DRET:C_DRET + P] = SCALE * (1.0 + (u == v))
    q = GRID - 1 - np.arange(P)[:, None] % GRID
    c[:, C_FLIP:C_FLIP + P] = (v // GRID == u // GRID) & (v % GRID == q)
    k = np.arange(GRID)[None, :]
    first = np.clip(q - 8, 0, GRID - 16)
    c[:, C_MASK:C_MASK + GRID] = np.where((k >= first) & (k < first + 16), 0.0, NEG)
    inv = (1.0 / (10000.0 ** (np.arange(16, dtype=np.float32) / 16))).astype(np.float32)
    for n in range(2):
        t = np.arange(P) + n * P
        for axis, pos in enumerate((t // GRID, t % GRID)):
            ang = pos[:, None].astype(np.float32) * inv
            for half in range(2):
                at = n * 64 + axis * 32 + half * 16
                c[:, C_COS + at:C_COS + at + 16] = np.cos(ang)
                c[:, C_SIN + at:C_SIN + at + 16] = np.sin(ang) * (1 if half else -1)
    i = np.arange(4)
    c[:, C_TRI:C_TRI + 16] = (i[None, :] < i[:, None]).reshape(1, 16)
    c[:, C_IOTA:C_IOTA + P] = v
    c[:, C_TOK:C_TOK + 4] = u + P * i[None, :]
    c[:, C_EXP:C_EXP + NE] = CAP * np.arange(NE)
    return c


def trunk(nc, ins, out):
    x, ctx_in = ins["x"], ins["ctx"]
    es = ExitStack()
    with es:
        sems = {}

        def S(name):
            if name not in sems:
                sems[name] = es.enter_context(nc.semaphore(name))
            return sems[name]

        def per_layer(name, l):
            T = len(tiles(l))
            jobs = in_jobs(l)
            a, d = emptied(jobs, len(jobs))
            table = {
                "mod_pe": mod_units(l), "mod_row": mod_units(l), "in_pe": len(jobs), "in_act": a, "in_dve": d, "out_pe": N_OUT * T, "res_dve": N_OUT * T,
                "a_sq": NT, "a_hn": NT, "a_tr": KD, "a_evac": KD, "f_sq": T, "f_hn": T, "f_tr": KD, "f_evac": KD,
                "conv_dve": 6, "conv_act": 6, "x_tr": 5, "x_evac": 5, "ret_tr": NT, "ret_evac": NT, "rope": 2,
                "na_sq": NT, "na_ss": NT, "na_norm": NT, "naT_tr": NT, "naT_evac": NT,
                "rf_dve": T + 1, "rb_pool": T + 1, "seg_pe": T + 1, "e_act": T + 1,
                "vw_dve": 6, "st_pe": 6, "h_dve": 6, "mix_tr": KD, "mixT": KD,
                "diag0": len(segs(l)), "row0": len(segs(l)), "diag1": len(segs(l)), "row1": len(segs(l)),
                "ld_rowp": 16, "ld_bias": 16 * 2 * NA_H,
            }
            table.update(dict.fromkeys(("sc_pe", "sl_dve", "mret_dve", "v_pool", "y_pe", "comb_dve", "dx_pool", "yz_dve",
                                        "yss_act", "gn_ms", "gn_rs", "na_out", "h_end"), T))
            table.update(dict.fromkeys(("mf_dve", "mb_pool", "diag_pe"), 2 * T))
            table.update(dict.fromkeys(("s_pe", "mx_dve", "p_act", "pt_pe", "pt_dve", "pv_pe"), NA_H * T))
            table.update({"turn_pe": KD, "turn_act": KD, "f_stored": 16, "chosen_dve": 1, "pos_pe": 1, "rounds_dve": 1,
                          "route_dve": 1})
            table.update(dict.fromkeys(("mod_turned", "mod_evac", "modA", "a_ms", "a_rs", "f_ms", "f_rs", "pad_zero", "na_ms", "na_rs",
                                        "dt_abs", "dt_ln", "nA_act", "loga", "cum_pe", "ex_act", "bias_dve", "row0_pe",
                                        "row1_pe", "rt_pe", "rt_act", "acc_zero"), 1))
            return table[name]

        def upto(name, l, n):
            return n + sum(per_layer(name, m) for m in range(l))

        def sb(name, *shape):
            return es.enter_context(nc.sbuf_tensor(name, [P, *shape], F32))

        h = sb("h", NT, D)
        featT = sb("featT", KD, TOK)
        tokA = sb("tokA", NT, D)
        ring = sb("ring", 2, SLOT)
        const = sb("const", N_CONST)
        colp = sb("colp", DEPTH, N_COLP)
        condT = sb("condT", KD, 2)
        silT = sb("silT", KD, 2)
        mod = sb("mod", DEPTH, 48, 2)
        modA = sb("modA", DEPTH, 2, KD, 2)
        rw = sb("rw", KD, NE)
        rb = sb("rb", NE)
        stat = sb("stat", 64)
        stat2 = sb("stat2", 64)
        pw = sb("pw", 64)
        zero8 = sb("zero8", KD)
        slot_i = es.enter_context(nc.sbuf_tensor("slot_i", [P, 2], U32))
        rounds = es.enter_context(nc.sbuf_tensor("rounds", [P, DEPTH], I32))
        ARENA = 30368
        arena = sb("arena", ARENA)
        cursor = [0]

        def carve(*shape):
            n = int(np.prod(shape))
            at = cursor[0]
            cursor[0] += n
            assert cursor[0] <= ARENA
            v = arena[:, at:at + n]
            if len(shape) == 2:
                v = v.rearrange("p (a b) -> p a b", a=shape[0])
            elif len(shape) == 3:
                v = v.rearrange("p (a b c) -> p a b c", a=shape[0], b=shape[1])
            elif len(shape) == 4:
                v = v.rearrange("p (a b c d) -> p a b c d", a=shape[0], b=shape[1], c=shape[2])
            return v

        qk = carve(NT, 512)
        XV = carve(NT, NH * HD)
        at = cursor[0]
        nqk = carve(NT, 512)
        cursor[0] = at
        Mf = carve(2, 4, P)
        Mb = carve(2, 4, P)
        nav = carve(NT, 256)
        BCT = carve(2, TOK)
        Bt = carve(NT, P)
        retT = carve(4, TOK)
        naT = carve(4, TOK)
        at = cursor[0]
        xT = carve(4, TOK)
        cursor[0] = at
        rf = carve(SSD_H, P)
        rbk = carve(SSD_H, P)
        at = cursor[0]
        Hs = carve(2, NT, 384)
        cursor[0] = at
        xpad = carve(6, 2, CTX + 2)
        y = carve(NH, HD)
        y2 = carve(NH, HD)
        Pm = carve(2, 512)
        sq = Pm[:, 0, :]
        at_gate = cursor[0]
        E = carve(SSD_H, P)
        Eret = carve(RET_H, P)
        Mret = carve(RET_H, P)
        sU = carve(2, P)
        sL = carve(2, P)
        VW = carve(NH, HD)
        Vf = carve(SSD_H, HD)
        Vb = carve(SSD_H, HD)
        at = cursor[0]
        cursor[0] = at_gate
        diag = carve(2, D)
        grow = carve(2, D)
        assert cursor[0] <= at
        cursor[0] = at
        at = cursor[0]
        dx = carve(SSD_H, HD)
        cursor[0] = at
        PT = carve(2, 4, P)
        bias = carve(NA_H, 6, GRID)
        rowp = carve(N_ROWP)
        nA = carve(2, NH)
        dtr = carve(NT * 2, SSD_H)
        dta = carve(NT * 2, SSD_H)
        DTX = carve(NT * 2, NH)
        Aall = carve(NT * 2, NH)
        EX = carve(288)
        Wt = carve(2, NT, NH)
        Dec = carve(NT * 2, 6)
        rs = carve(NT, 8)
        nmx = carve(16)
        nsum = carve(16)
        nrec = carve(16)
        mixer_end = cursor[0]
        cursor[0] = 0
        slots = [ring[:, 0, :], ring[:, 1, :]] + [carve(SLOT) for _ in range(4)]
        hs = carve(FE)
        hp = carve(FE)
        hT = carve(4, P)
        onehot = carve(2, NT, P)
        Xg = carve(1, D)
        assert cursor[0] <= at_gate
        cursor[0] = at_gate + 4 * D
        XT = carve(2, KD, P)
        Yb = carve(2, D)
        gates = carve(NT, NE)
        aff = carve(NT, NE)
        sel = carve(NT * 4, 4)
        g1, g2, g3, g4 = (carve(NT, 4) for _ in range(4))
        cmp1 = XT[:, 0, 0:2, :].rearrange("p a (b c) -> p (a b) c", c=16)
        cmp2 = XT[:, 0, 2:4, :].rearrange("p a (b c) -> p (a b) c", c=16)
        chosen = carve(NT * 4, 4)
        rsum = carve(NT)
        place = carve(NT, NE)
        pick = carve(NT, NE)
        tmp16 = carve(NT, NE)
        pos2 = carve(2, NT)
        first2 = carve(2, NT)
        gate2 = carve(2, NT)
        row2 = carve(2, NT)
        inround = carve(2, NT)
        row_i = carve(2, NT).bitcast(U32)
        count = carve(NE)
        few = carve(4)
        gathered = [Xg[:, 0, :], diag[:, 0, :]]
        back = gathered + [Yb[:, 0, :], Yb[:, 1, :]]

        ps = es.enter_context(nc.psum_tensor("ps", [P, 8, 512], F32))
        ident = const[:, C_ID:C_ID + P]
        LE, GT, GE, LT, ONE = (const[:, c:c + P] for c in (C_LE, C_GT, C_GE, C_LT, C_ONE))

        def flat(bank, n):
            return ps[:, bank:bank + (n + 511) // 512, :].rearrange("p a b -> p (a b)")[:, 0:n]

        def scan_out(k, g, place, n=1):
            half = NH * HD // 2
            bank, c = divmod((half * g if k == 0 else 2 * half * (1 + g) + half * (k - 1)) + HD * place, 512)
            assert c + HD * n <= 512
            return ps[:, bank, c:c + HD * n]

        def scan_outs(k):
            all_ = flat(0, 3 * NH * HD)
            if k == 0:
                return all_[:, 0:NH * HD].rearrange("p (g h c) -> p g h c", g=2, h=6)
            return all_[:, NH * HD:].rearrange("p (g k h c) -> p g k h c", g=2, k=2, h=6)[:, :, k - 1, :, :]

        def heads(ap, n):
            return ap.rearrange("p (a b) -> p a b", a=n)

        def ssd(ap, n=1):
            return ap.rearrange("p (g c) -> p g c", g=2)[:, :, 0:4 * n]

        def ret(ap, n=1):
            return ap.rearrange("p (g c) -> p g c", g=2)[:, :, 4 * n:6 * n]

        def line(ap):
            return ap.rearrange("p a b -> p (a b)")

        def spread2(ap, n):
            return ap.unsqueeze(3).to_broadcast([P, 2, ap.shape[2], n])

        def triangle_rows(dst, a, m, tri):
            return (dst.rearrange("p (g h) c -> p g h c", g=2), spread2(a, P),
                    tri.unsqueeze(1).unsqueeze(1).to_broadcast([P, 2, m, P]))

        def spread(ap, n):
            return ap.unsqueeze(2).to_broadcast([P, ap.shape[1], n])

        def repeat(ap, n):
            return ap.unsqueeze(1).to_broadcast([P, n, ap.shape[1]])

        def tiles(l):
            return list(range(NT)) if l < DEPTH - 1 else [2, 3]

        def in_jobs(l):
            jobs = [("bc_dt", "f", 4, "A"), ("bc_dt", "f", 5, "A"), ("bc_dt", "dt", 0, "D")]
            jobs += [("x", "f", f, "A") for f in range(4)]
            jobs += [("ret_qk", "t", t, "D") for t in range(NT)]
            jobs += [("ret_vg", "t", t, "A") for t in range(NT)]
            jobs += [("z", "t", t, "A") for t in tiles(l)]
            jobs += [("na_qk", "t", t, "D") for t in range(NT)]
            jobs += [("na_v", "t", t, "D") for t in range(NT)]
            return jobs

        def emptied(jobs, upto):
            a = sum(j[3] == "A" for j in jobs[:upto])
            return a, upto - a

        def cols_needed(l, piece, t):
            full = l < DEPTH - 1 or t >= 2
            return {"ret_qk": (0 if full else 256, 512), "ret_vg": (0, 512 if full else 256),
                    "z": (0, 512), "na_qk": (0 if full else 256, 512), "na_v": (0, 256)}[piece]

        STATE_STEPS = ((0, 0), (1, 1), (0, 1), (1, 0), (0, 2), (1, 3))
        STATE_NEXT = {(0, 0): 1, (0, 1): 2, (0, 2): 3, (1, 1): 0, (1, 0): 3, (1, 3): 2}

        def dirs_of(t):
            return [d for d in (0, 1) if (d, t) not in ((0, 0), (1, 1))]

        def att_units(l):
            return [(t, hd) for t in tiles(l) for hd in range(NA_H)]

        def segs(l):
            return [0, 1] if l < DEPTH - 1 else [1]

        def dve_jobs_done(l, name, i):
            jobs = in_jobs(l)
            n = next(n for n, q in enumerate(jobs) if q[0] == name and q[2] == i and q[3] == "D")
            return emptied(jobs, n + 1)[1]

        def mod_width(l):
            return 512 if l == 0 else P

        def mod_units(l):
            return N_MOD * 512 // mod_width(l)

        def mod_row(l, u):
            return ps[0:2, u % 2, :] if l == 0 else ps[0:2, 5, 0:P]

        def mod_lag(l):
            return 2 if l == 0 else 1

        def mod_copy(l, u):
            at = 512 * (u % 4)
            return featT.rearrange("p k c -> p (k c)")[0:2, at:at + mod_width(l)]

        def mod_columns(l):
            return ps[:, 4, 0:96] if l == 0 else ps[:, 5, 384:480]

        def mod_at(l, step, n, point=0):
            if l >= DEPTH:
                return range(0)
            ns, na = len(STATE_STEPS) - 2, len(att_units(l - 1))
            per_point = 2
            first_att = ns + per_point * 3 * len(tiles(l - 1))
            if step == "state":
                return range(n - 2, n - 1) if n >= 2 else range(0)
            if step == "tile":
                at = ns + per_point * (3 * n + point)
                return range(at, at + per_point)
            left = mod_units(l) - first_att
            return range(first_att + left * n // na, first_att + left * (n + 1) // na)

        def static_pieces():
            p = []
            for l in range(DEPTH):
                if l == 0:
                    p += [("mod", 0, n) for n in range(N_MOD)]
                p += [("in", l, n) for n in range(len(IN_PIECES))]
                if l + 1 < DEPTH:
                    p += [("mod", l + 1, n) for n in range(N_MOD)]
                p += [("out", l, n) for n in range(N_OUT)]
            return p

        def slot_of(piece):
            g = static_pieces().index(piece)
            return (2, 3, 4, 0, 1)[g % 5] if g < N_MOD else g % 2

        def landed(piece):
            ps_ = static_pieces()
            return 16 * sum(slot_of(q) == slot_of(piece) for q in ps_[:ps_.index(piece) + 1])

        def use_of(piece):
            kind, l, n = piece
            if kind == "mod":
                return "mod_pe", l, (n + 1) * 512 // mod_width(l)
            if kind == "in":
                return "in_pe", l, 1 + max(i for i, j in enumerate(in_jobs(l)) if j[0] == IN_PIECES[n][0])
            return "out_pe", l, len(tiles(l)) * (n + 1)

        def before(piece):
            ps_ = static_pieces()
            same = [q for q in ps_[:ps_.index(piece)] if slot_of(q) == slot_of(piece)]
            return same[-1] if same else None

        def X(name, l):
            return S(f"{name}_{l}")

        def job(r, i, c=0):
            return r * NE + (i * 2 + c)

        def load_rounds(eng, l):
            eng.wait_ge(S("rounds_dve"), upto("rounds_dve", l, 1))
            first = 0
            for m in range(l):
                first = first + eng.value_load(rounds[0:1, m:m + 1], min_val=1, max_val=len(tiles(m)))
            return first, eng.value_load(rounds[0:1, l:l + 1], min_val=1, max_val=len(tiles(l)))

        rows_in = [nc.dram_tensor(f"ffn_rows{l}", (P * len(tiles(l)), D), F32, kind="Internal").ap() for l in range(DEPTH)]
        rows_out = [nc.dram_tensor(f"expert_rows{l}", (NO_ROW + 1, D), F32, kind="Internal").ap() for l in range(DEPTH)]

        block = es.enter_context(nc.Block())

        @block.sync
        def _(sp):
            sp.dma_start(const[:, :], ins["consts"]).then_inc(S("ld_const"), 16)
            sp.dma_start(condT[:, :, :], ins["condT"]).then_inc(S("ld_cond"), 16)
            sp.dma_start(h[:, 0:2, :], ctx_in.rearrange("(t p) d -> p t d", p=P)).then_inc(S("ld_h0"), 16)
            sp.dma_start(h[:, 2:4, :], x.rearrange("(t p) d -> p t d", p=P)).then_inc(S("ld_h1"), 16)
            sp.dma_start(rw[:, :, :], ins["router_w"].rearrange("(k p) e -> p k e", p=P)).then_inc(S("ld_rw"), 16)
            rbt = ins["router_b"]
            sp.dma_start(rb[:, :], bass.AP(rbt.tensor, 0, [[0, P], [1, NE]])).then_inc(S("ld_rb"), 16)

            for l in range(DEPTH):
                sp.dma_start(colp[:, l, :], ins["colp"][l]).then_inc(S("ld_colp"), 16)

            def load_static(piece):
                kind, l, n = piece
                if kind == "mod":
                    src = ins["w_mod"][l, :, 512 * n:512 * (n + 1)]
                elif kind == "in":
                    _, c, w = IN_PIECES[n]
                    src = ins["w_in"][l, :, c:c + w]
                else:
                    src = ins["w_out"][l, :, 512 * n:512 * (n + 1)]
                k = slot_of(piece)
                dst = slots[k][:, 0:KD * src.shape[1]].rearrange("p (k c) -> p k c", k=KD)
                sp.dma_start(dst, src.rearrange("(k p) c -> p k c", p=P)).then_inc(S(f"piece{k}"), 16)

            def small(l):
                rp = ins["rowp"]
                sp.dma_start(rowp, bass.AP(rp.tensor, l * N_ROWP, [[0, P], [1, N_ROWP]])).then_inc(S("ld_rowp"), 16)
                rpb = ins["na_rpb"]
                for half, dr0 in ((0, 5), (1, 4)):
                    for hd in range(NA_H):
                        base = ((l * NA_H + hd) * 15 + dr0) * 31 + 15 - (GRID - 1)
                        sp.dma_start(bias[64 * half:64 * half + 64, hd, :, :],
                                     bass.AP(rpb.tensor, base, [[1, 64], [31, 6], [1, 64]])
                                     ).then_inc(S("ld_bias"), 16)

            for l in range(DEPTH):
                nt = len(tiles(l))
                mine = [q for q in static_pieces() if l == (max(q[1] - 1, 0) if q[0] == "mod" else q[1])]
                if l > 0:
                    sp.wait_ge(S("up_pe"), (first + R) * NE)
                for m, piece in enumerate(mine):
                    if l > 0 and m == 2:
                        sp.wait_ge(S("h_end"), upto("h_end", l - 1, len(tiles(l - 1))))
                        small(l)
                    if before(piece) is not None and not (l > 0 and m < 2):
                        name, ll, value = use_of(before(piece))
                        sp.wait_ge(S(name), upto(name, ll, value))
                    load_static(piece)
                    if l == 0 and m == 4:
                        small(l)

                def load_expert(e, c, j):
                    slot = 3 * c + j
                    src = (ins["w_gate"], ins["w_up"], ins["w_down"])[j]
                    k = 8 if j < 2 else 4
                    dst = slots[slot].rearrange("p (k c) -> p k c", k=k)
                    w = src[l, e] if isinstance(e, int) else src[l, bass.ds(e, 1)].rearrange("o r c -> (o r) c")
                    sp.dma_start(dst, w.rearrange("(k p) c -> p k c", p=P)).then_inc(S(f"slot{slot}"), 16)

                for n in range(N_OUT):
                    name, ll, value = use_of(("out", l, n))
                    sp.wait_ge(S(name), upto(name, ll, value))
                load_expert(0, 0, 0)
                load_expert(0, 0, 1)
                sp.wait_ge(S("na_out"), upto("na_out", l, nt))
                for c, j in ((0, 2), (1, 0), (1, 1), (1, 2)):
                    load_expert(c, c, j)
                sp.wait_ge(S("turn_act"), upto("turn_act", l, KD))
                sp.dma_start(rows_in[l].rearrange("(t p) d -> p t d", p=P), tokA[:, tiles(l)[0]:NT, :]
                             ).then_inc(S("f_stored"), 16)
                sp.wait_ge(S("zero_pool"), 1)
                sp.dma_start(rows_out[l][NO_ROW:NO_ROW + 1, :].rearrange("o (p c) -> (o p) c", p=P), zero8[:, :]
                             ).then_inc(X("no_row", l), 16)
                first, R = load_rounds(sp, l)
                with sp.Fori(first * (NE // 2) + 1, (first + R) * (NE // 2)) as i:
                    for c in range(2):
                        sp.wait_ge(S("up_pe"), job(0, i, c - 1))
                        load_expert((i % (NE // 2)) * 2 + c, c, 0)
                        load_expert((i % (NE // 2)) * 2 + c, c, 1)
                        sp.wait_ge(S("dn_pe"), job(0, i, c - 1))
                        load_expert((i % (NE // 2)) * 2 + c, c, 2)
            sp.wait_ge(S("h_end"), upto("h_end", DEPTH - 1, 2))
            for l in range(DEPTH):
                sp.wait_ge(X("no_row", l), 16)
            sp.dma_start(out.rearrange("(t p) d -> p t d", p=P), h[:, 2:4, :]).then_inc(S("stored"), 16)
            sp.wait_ge(S("stored"), 16)

        @block.tensor
        def _(pe):
            mm = nc.tensor.matmul
            tr = nc.tensor.transpose
            pe.wait_ge(S("ld_const"), 16)

            def piece(q, w=512):
                return slots[slot_of(q)][:, 0:KD * w].rearrange("p (k c) -> p k c", k=KD)

            def turn_mod(l, u):
                w = mod_width(l)
                for f in range(w // P):
                    c = 2 * (u * w // P + f)
                    i = tr(mod_columns(l)[:, c:c + 2], mod_copy(l, u)[:, P * f:P * f + P], ident[0:2, 0:2])
                return i

            def mod_unit(l, u):
                n, c = divmod(u * mod_width(l), 512)
                if c == 0:
                    pe.wait_ge(S(f"piece{slot_of(('mod', l, n))}"), landed(("mod", l, n)))
                if u >= mod_lag(l):
                    pe.wait_ge(S("mod_row"), upto("mod_row", l, u - mod_lag(l) + 1))
                    turn_mod(l, u - mod_lag(l))
                for k in range(KD):
                    i = mm(mod_row(l, u), silT[:, k, :], piece(("mod", l, n))[:, k, c:c + mod_width(l)],
                           start=k == 0, stop=k == KD - 1)
                i.then_inc(S("mod_pe"), 1)

            def mod_end(l):
                n = mod_units(l)
                pe.wait_ge(S("mod_row"), upto("mod_row", l, n))
                for u in range(n - mod_lag(l), n):
                    i = turn_mod(l, u)
                i.then_inc(S("mod_turned"), 1)

            def modulation(l):
                pe.wait_ge(S("sil"), 1)
                for u in range(mod_units(l)):
                    mod_unit(l, u)
                mod_end(l)

            def norm_transpose(l, which, ts):
                pe.wait_ge(S(which + "_hn"), upto(which + "_hn", l, len(ts)))
                if which == "a":
                    pe.wait_ge(S("mod_evac"), upto("mod_evac", l, 1))
                for k in range(KD):
                    if k >= 4:
                        pe.wait_ge(S(which + "_evac"), upto(which + "_evac", l, k - 3))
                    for j, t in enumerate(ts):
                        i = tr(ps[:, 1 + k % 4, P * t:P * t + P], tokA[:, t, P * k:P * k + P], ident)
                    i.then_inc(S(which + "_tr"), 1)

            def project(l):
                jobs = in_jobs(l)
                pe.wait_ge(S("a_evac"), upto("a_evac", l, KD))
                for n, (name, kind, i, _) in enumerate(jobs):
                    p = [q[0] for q in IN_PIECES].index(name)
                    w = IN_PIECES[p][2]
                    W = piece(("in", l, p), w)
                    if n == 0 or jobs[n - 1][0] != name:
                        pe.wait_ge(S(f"piece{slot_of(('in', l, p))}"), landed(("in", l, p)))
                    if n >= 4:
                        a, d = emptied(jobs, n - 3)
                        pe.wait_ge(S("in_act"), upto("in_act", l, a))
                        if d:
                            pe.wait_ge(S("in_dve"), upto("in_dve", l, d))
                    bank = ps[:, n % 4, :]
                    if kind == "f":
                        c = P * (i % 4)
                        lo = 0 if (l < DEPTH - 1 or i != 5) else CTX
                        for k in range(KD):
                            o = mm(bank[:, lo:TOK], W[:, k, c:c + P], featT[:, k, lo:TOK],
                                   start=k == 0, stop=k == KD - 1)
                    elif kind == "dt":
                        for t in range(NT):
                            for k in range(KD):
                                o = mm(bank[:, 16 * t:16 * t + 16], featT[:, k, P * t:P * t + P], W[:, k, 256:272],
                                       start=k == 0, stop=k == KD - 1)
                    else:
                        lo, hi = cols_needed(l, name, i)
                        for k in range(KD):
                            o = mm(bank[:, lo:hi], featT[:, k, P * i:P * i + P], W[:, k, lo:hi],
                                   start=k == 0, stop=k == KD - 1)
                    o.then_inc(S("in_pe"), 1)

            def turn_operands(l):
                jobs = in_jobs(l)
                a, d = emptied(jobs, len(jobs))
                pe.wait_ge(S("in_act"), upto("in_act", l, a))
                pe.wait_ge(S("in_dve"), upto("in_dve", l, d))
                for n, f in enumerate((4, 0, 1, 2, 3)):
                    pe.wait_ge(S("conv_act"), upto("conv_act", l, {4: 1, 5: 2}.get(f, f + 3)))
                    if n >= 2:
                        pe.wait_ge(S("x_evac"), upto("x_evac", l, n - 1))
                    src = BCT[:, 0, :] if f == 4 else xT[:, f, :]
                    for t in range(NT):
                        i = tr(ps[:, 4 + n % 2, P * t:P * t + P], src[:, P * t:P * t + P], ident)
                    i.then_inc(S("x_tr"), 1)
                for t in range(NT):
                    full = t in tiles(l)
                    if t >= 2:
                        pe.wait_ge(S("rope"), upto("rope", l, t - 1))
                        pe.wait_ge(S("ret_evac"), upto("ret_evac", l, t - 1))
                    for b in range(0 if full else 2, 4):
                        i = tr(ps[:, 6 + t % 2, P * b:P * b + P], qk[:, t, P * b:P * b + P], ident)
                    i.then_inc(S("ret_tr"), 1)
                for t in range(NT):
                    full = t in tiles(l)
                    pe.wait_ge(S("na_norm"), upto("na_norm", l, t + 1))
                    if t >= 2:
                        pe.wait_ge(S("naT_evac"), upto("naT_evac", l, t - 1))
                    for b in range(0 if full else 2, 4):
                        i = tr(ps[:, t % 2, P * b:P * b + P], nqk[:, t, P * b:P * b + P], ident)
                    i.then_inc(S("naT_tr"), 1)

            def decay_sums(l):
                pe.wait_ge(S("loga"), upto("loga", l, 1))
                f, b = Aall[:, 0:NT * 2:2, :], Aall[:, 1:NT * 2:2, :]
                pe.wait_ge(S("naT_evac"), upto("naT_evac", l, NT))
                for n, (tri, a) in enumerate(((LE, f), (GE, b), (GT, f), (LT, b))):
                    mm(ps[:, 2, 48 * n:48 * n + 48], tri, a, start=True, stop=True)
                mm(ps[:, 2, 192:288], ONE, Aall[:, :, :], start=True, stop=True).then_inc(S("cum_pe"), 1)

            def states(l):
                pe.wait_ge(S("x_evac"), upto("x_evac", l, 5))
                pe.wait_ge(S("ret_evac"), upto("ret_evac", l, NT))
                for n, (d, t) in enumerate(STATE_STEPS):
                    pe.wait_ge(S("vw_dve"), upto("vw_dve", l, n + 1))
                    if n >= 2:
                        pe.wait_ge(S("h_dve"), upto("h_dve", l, n - 1))
                    bank = ps[:, 3 + n % 2, :]
                    for g in range(2):
                        mm(bank[64 * g:64 * g + 64, 0:256], Bt[:, t, 64 * g:64 * g + 64],
                           VW[:, 6 * g:6 * g + 4, :], start=True, stop=True)
                    for r in range(RET_H):
                        i = mm(bank[64 * (r % 2):64 * (r % 2) + 64, 256 + 64 * (r // 2):320 + 64 * (r // 2)],
                               qk[:, t, 256 + 64 * r:320 + 64 * r], VW[:, 6 * (r % 2) + 4 + r // 2, :],
                               start=True, stop=True)
                    i.then_inc(S("st_pe"), 1)
                    for u in mod_at(l + 1, "state", n):
                        mod_unit(l + 1, u)

            def scan_tile(l, n, t):
                pe.wait_ge(S("rf_dve"), upto("rf_dve", l, n + 2))
                pe.wait_ge(S("rb_pool"), upto("rb_pool", l, n + 2))
                if n > 0:
                    pe.wait_ge(S("mret_dve"), upto("mret_dve", l, n))
                else:
                    pe.wait_ge(S("e_act"), upto("e_act", l, 1))
                for hf in range(2):
                    mm(ps[:, 6 + hf, :], GT, rf[:, 4 * hf:4 * hf + 4, :], start=True, stop=False)
                    i = mm(ps[:, 6 + hf, :], LT, rbk[:, 4 * hf:4 * hf + 4, :], start=False, stop=True)
                i.then_inc(S("seg_pe"), 1)
                for u in mod_at(l + 1, "tile", n, 0):
                    mod_unit(l + 1, u)
                pe.wait_ge(S("e_act"), upto("e_act", l, n + 2))
                c = slice(P * t, P * t + P)
                for g in range(2):
                    s = slice(64 * g, 64 * g + 64)
                    mm(ps[:, 6 + g, 0:P], BCT[s, 0, c], BCT[s, 1, c], start=True, stop=True)
                for r in range(RET_H):
                    s = slice(64 * (r % 2), 64 * (r % 2) + 64)
                    o = P * (1 + r // 2)
                    i = mm(ps[:, 6 + r % 2, o:o + P], retT[s, 2 + r // 2, c], retT[s, r // 2, c],
                           start=True, stop=True)
                i.then_inc(S("sc_pe"), 1)
                if n > 0:
                    pe.wait_ge(S("comb_dve"), upto("comb_dve", l, n))
                for d in dirs_of(t):
                    pe.wait_ge(S("h_dve"), upto("h_dve", l, 6))
                    for g in range(2):
                        s = slice(64 * g, 64 * g + 64)
                        for place in (0, 2):
                            mm(scan_out(1 + d, g, place, 2), BCT[s, 1, c], Hs[s, d, t, HD * place:HD * (place + 2)],
                               start=True, stop=True)
                    for r in range(RET_H):
                        s = slice(64 * (r % 2), 64 * (r % 2) + 64)
                        mm(scan_out(1 + d, r % 2, 4 + r // 2), retT[s, r // 2, c],
                           Hs[s, d, t, 256 + 64 * (r // 2):320 + 64 * (r // 2)], start=True, stop=True)
                for u in mod_at(l + 1, "tile", n, 1):
                    mod_unit(l + 1, u)
                pe.wait_ge(S("v_pool"), upto("v_pool", l, n + 1))
                for g in range(2):
                    pe.wait_ge(S("mf_dve"), upto("mf_dve", l, 2 * n + g + 1))
                    pe.wait_ge(S("mb_pool"), upto("mb_pool", l, 2 * n + g + 1))
                    for j in range(4):
                        hd = 4 * g + j
                        o = scan_out(0, g, j)
                        mm(o, Mf[:, g, j, :], Vf[:, hd, :], start=True, stop=False)
                        i = mm(o, Mb[:, g, j, :], Vb[:, hd, :], start=False, stop=True)
                    i.then_inc(S("diag_pe"), 1)
                pe.wait_ge(S("mret_dve"), upto("mret_dve", l, n + 1))
                for r in range(RET_H):
                    g, o = r // 2, 256 + 64 * (r % 2)
                    i = mm(scan_out(0, g, 4 + r % 2), Mret[:, r, :], XV[:, t, 384 * g + o:384 * g + o + 64],
                           start=True, stop=True)
                i.then_inc(S("y_pe"), 1)
                for u in mod_at(l + 1, "tile", n, 2):
                    mod_unit(l + 1, u)

            def scan(l):
                pe.wait_ge(S("rf_dve"), upto("rf_dve", l, 1))
                pe.wait_ge(S("rb_pool"), upto("rb_pool", l, 1))
                mm(ps[:, 6, :], GT, rf[:, 0:4, :], start=True, stop=False)
                mm(ps[:, 6, :], LT, rbk[:, 0:4, :], start=False, stop=True).then_inc(S("seg_pe"), 1)
                states(l)
                for n, t in enumerate(tiles(l)):
                    scan_tile(l, n, t)

            def attention(l):
                un = att_units(l)
                pe.wait_ge(S("comb_dve"), upto("comb_dve", l, len(tiles(l))))

                def scores(n):
                    t, hd = un[n]
                    s = slice(64 * (hd % 2), 64 * (hd % 2) + 64)
                    keys = TOK if t >= 2 else CTX
                    if n >= 2:
                        pe.wait_ge(S("p_act"), upto("p_act", l, n - 1))
                    lat = t >= 2
                    i = mm(ps[:, n % 2, 0:keys], naT[s, hd // 2, P * t:P * t + P], naT[s, 2 + hd // 2, 0:keys],
                           start=True, stop=not lat)
                    if lat:
                        j = 2 - 2 * (t - 2)
                        pe.wait_ge(S("bias_dve"), upto("bias_dve", l, 1))
                        i = mm(ps[:, n % 2, CTX:TOK], const[:, C_FLIP:C_FLIP + P], bias[:, hd, j:j + 4, :], start=False, stop=True)
                    i.then_inc(S("s_pe"), 1)

                def turn(n):
                    t, hd = un[n]
                    nk = NT if t >= 2 else 2
                    pe.wait_ge(S("p_act"), upto("p_act", l, n + 1))
                    if n >= 2:
                        pe.wait_ge(S("pt_dve"), upto("pt_dve", l, n - 1))
                    for b in range(nk):
                        i = tr(ps[:, 2 + n % 2, P * b:P * b + P], Pm[:, n % 2, P * b:P * b + P], ident)
                    i.then_inc(S("pt_pe"), 1)

                def values(n):
                    t, hd = un[n]
                    nk = NT if t >= 2 else 2
                    pe.wait_ge(S("pt_dve"), upto("pt_dve", l, n + 1))
                    tile = n // NA_H
                    if n % NA_H == 0 and tile >= 2:
                        pe.wait_ge(S("na_out"), upto("na_out", l, tile - 1))
                    for b in range(nk):
                        i = mm(ps[:, 4 + 2 * (tile % 2), 64 * hd:64 * hd + 64], PT[:, n % 2, b, :],
                               nav[:, b, 64 * hd:64 * hd + 64], start=b == 0, stop=b == nk - 1)
                    i.then_inc(S("pv_pe"), 1)

                N = len(un)
                scores(0)
                for n in range(N):
                    if n + 1 < N:
                        scores(n + 1)
                    if n >= 1:
                        values(n - 1)
                    for u in mod_at(l + 1, "unit", n):
                        mod_unit(l + 1, u)
                    turn(n)
                values(N - 1)
                if l + 1 < DEPTH:
                    mod_end(l + 1)

            def output(l):
                ts = tiles(l)
                pe.wait_ge(S("na_out"), upto("na_out", l, len(ts)))
                for k in range(KD):
                    if k >= 2:
                        pe.wait_ge(S("mixT"), upto("mixT", l, k - 1))
                    for t in ts:
                        i = tr(ps[:, 6 + k % 2, P * t:P * t + P], tokA[:, t, P * k:P * k + P], ident)
                    i.then_inc(S("mix_tr"), 1)
                gate_rows(l, 0)
                pe.wait_ge(S("mixT"), upto("mixT", l, KD))
                if l + 1 < DEPTH:
                    pe.wait_ge(S("mod_evac"), upto("mod_evac", l + 1, 1))
                n = 0
                for half in range(N_OUT):
                    p = ("out", l, half)
                    pe.wait_ge(S(f"piece{slot_of(p)}"), landed(p))
                    for t in ts:
                        if n >= 2:
                            pe.wait_ge(S("res_dve"), upto("res_dve", l, n - 1))
                        for k in range(KD):
                            i = mm(ps[:, 4 + n % 2, :], featT[:, k, P * t:P * t + P], piece(p)[:, k, :],
                                   start=k == 0, stop=k == KD - 1)
                        i.then_inc(S("out_pe"), 1)
                        n += 1

            def gate_rows(l, which):
                pe.wait_ge(S(f"diag{which}"), upto(f"diag{which}", l, len(segs(l))))
                if which == 1:
                    pe.wait_ge(S("rt_act"), upto("rt_act", l, 1))
                    pe.wait_ge(S("rounds_dve"), upto("rounds_dve", l, 1))
                for seg in segs(l):
                    for hf in range(2):
                        i = mm(ps[:, 2 * seg + hf, :], ONE, diag[:, seg, 512 * hf:512 * hf + 512],
                               start=True, stop=True)
                i.then_inc(S(f"row{which}_pe"), 1)

            def router(l):
                ts = tiles(l)
                pe.wait_ge(S("f_evac"), upto("f_evac", l, KD))
                pe.wait_ge(S("ld_rw"), 16)
                for t in ts:
                    for k in range(KD):
                        i = mm(ps[:, 0, NE * t:NE * t + NE], featT[:, k, P * t:P * t + P], rw[:, k, :],
                               start=k == 0, stop=k == KD - 1)
                i.then_inc(S("rt_pe"), 1)

            def turn_back(l):
                for k in range(KD):
                    if k >= 4:
                        pe.wait_ge(S("turn_act"), upto("turn_act", l, k - 3))
                    for t in tiles(l):
                        i = tr(ps[:, 4 + k % 4, P * t:P * t + P], featT[:, k, P * t:P * t + P], ident)
                    i.then_inc(S("turn_pe"), 1)

            def places(l):
                ts = tiles(l)
                pe.wait_ge(S("chosen_dve"), upto("chosen_dve", l, 1))
                of = lambda t: chosen[:, 4 * (t - ts[0]):4 * (t - ts[0]) + 4, :]
                for t in ts:
                    for u in range(ts[0], t + 1):
                        mm(ps[:, 1, NE * t:NE * t + NE], ONE if u < t else LT, of(u), start=u == ts[0], stop=u == t)
                for t in ts:
                    i = mm(ps[:, 2, 0:NE], ONE, of(t), start=t == ts[0], stop=t == ts[-1])
                i.then_inc(S("pos_pe"), 1)

            def experts(l):
                ts = tiles(l)
                T = len(ts)
                first, R = load_rounds(pe, l)

                def who(r, i, c):
                    pe.wait_ge(S("onehot_dve"), job(r, i, c) + 1)
                    if not (isinstance(i, int) and 2 * i + c == 0):
                        pe.wait_ge(S("who_dve"), job(r, i, c))
                    for n in range(T):
                        o = mm(ps[:, 7, 0:1], onehot[:, c % 2, n, :], const[:, C_TOK + n:C_TOK + n + 1],
                               start=n == 0, stop=n == T - 1)
                    o.then_inc(S("who_pe"), 1)

                def turn_x(r, i, c):
                    pe.wait_ge(S(f"gathered{c % 2}"), (r * (NE // 2) + (i + c // 2) + 1) * 16)
                    if not (isinstance(i, int) and 2 * i + c == 0):
                        pe.wait_ge(S("xT_act"), job(r, i, c))
                    for k in range(KD):
                        o = tr(ps[:, 5 + k // 4, P * (k % 4):P * (k % 4) + P], gathered[c % 2][:, P * k:P * k + P], ident)
                    o.then_inc(S("xT_pe"), 1)

                def gate_up(r, i, c):
                    pe.wait_ge(S("xT_act"), job(r, i, c) + 1)
                    if not (isinstance(i, int) and 2 * i + c == 0):
                        pe.wait_ge(S("hp_dve"), job(r, i, c))
                    for m, name in ((0, "gate_pe"), (1, "up_pe")):
                        pe.wait_ge(S(f"slot{3 * c + m}"), (r * (NE // 2) + i + 1) * 16)
                        W = slots[3 * c + m].rearrange("p (k c) -> p k c", k=KD)
                        for k in range(KD):
                            o = mm(ps[:, m, :], XT[:, c, k, :], W[:, k, :], start=k == 0, stop=k == KD - 1)
                        o.then_inc(S(name), 1)

                def turn_h(r, i, c):
                    pe.wait_ge(S("hp_dve"), job(r, i, c) + 1)
                    if not (isinstance(i, int) and 2 * i + c == 0):
                        pe.wait_ge(S("hT_act"), job(r, i, c))
                    for b in range(4):
                        o = tr(ps[:, 2, P * b:P * b + P], hp[:, P * b:P * b + P], ident)
                    o.then_inc(S("hT_pe"), 1)

                def down(r, i, c):
                    pe.wait_ge(S("hT_act"), job(r, i, c) + 1)
                    pe.wait_ge(S(f"slot{3 * c + 2}"), (r * (NE // 2) + i + 1) * 16)
                    if not (isinstance(i, int) and 2 * i + c == 0):
                        pe.wait_ge(S("y_dve"), job(r, i, c))
                    W = slots[3 * c + 2].rearrange("p (k c) -> p k c", k=4)
                    for hf in range(2):
                        for k in range(4):
                            o = mm(ps[:, 3 + hf, :], hT[:, k, :], W[:, k, 512 * hf:512 * hf + 512],
                                   start=k == 0, stop=k == 3)
                    o.then_inc(S("dn_pe"), 1)

                def pair(r, i, last):
                    for c in range(2):
                        gate_up(r, i, c)
                        if not last:
                            who(r, i, c + 2)
                        turn_h(r, i, c)
                        if not (last and c == 1):
                            turn_x(r, i, c + 1)
                        down(r, i, c)

                pe.wait_ge(S("row1"), upto("row1", l, len(segs(l))))
                with pe.Fori(0, R) as n_round:
                    r = n_round + first
                    pe.wait_ge(S("round_dve"), r + 1)
                    who(r, 0, 0)
                    who(r, 0, 1)
                    turn_x(r, 0, 0)
                    pair(r, 0, False)
                    with pe.Fori(1, NE // 2 - 1) as i:
                        pair(r, i, False)
                    pair(r, NE // 2 - 1, True)

            modulation(0)
            for l in range(DEPTH):
                norm_transpose(l, "a", range(NT))
                project(l)
                turn_operands(l)
                decay_sums(l)
                scan(l)
                attention(l)
                output(l)
                norm_transpose(l, "f", tiles(l))
                router(l)
                turn_back(l)
                places(l)
                gate_rows(l, 1)
                experts(l)

        @block.scalar
        def _(act):
            A = nc.scalar.activation
            chain = [0]

            def link(ins):
                chain[0] += 1
                ins.then_inc(S("act_chain"), 1)
                act.wait_ge(S("act_chain"), chain[0])

            act.wait_ge(S("ld_cond"), 16)
            A(silT[:, :, :], condT[:, :, :], ACT.Silu).then_inc(S("sil"), 1)

            def mod_rows(l, units):
                for u in units:
                    act.wait_ge(S("mod_pe"), upto("mod_pe", l, u + 1))
                    A(mod_copy(l, u), mod_row(l, u), ACT.Identity).then_inc(S("mod_row"), 1)

            def square_rows(l, which, ts):
                for t in ts:
                    A(tokA[:, t, :], h[:, t, :], ACT.Square, accum_out=stat[:, t:t + 1]).then_inc(S(which + "_sq"), 1)

            def norm_evac(l, which, ts):
                m = 0 if which == "a" else 1
                act.wait_ge(S("modA"), upto("modA", l, 1))
                for k in range(0, KD):
                    act.wait_ge(S(which + "_tr"), upto(which + "_tr", l, k + 1))
                    for n, seg in enumerate((segs(l) if which == 'f' else [0, 1])):
                        c = slice(CTX * seg, CTX * seg + CTX)
                        i = A(featT[:, k, c], ps[:, 1 + k % 4, c], ACT.Identity,
                              scale=modA[:, l, m, k, seg:seg + 1], bias=mod[:, l, 24 * m + k, seg:seg + 1])
                    i.then_inc(S(which + "_evac"), 1)

            def project(l):
                jobs = in_jobs(l)
                nconv = 0
                act.wait_ge(S("pad_zero"), upto("pad_zero", l, 1))
                for n, (name, kind, i, eng) in enumerate(jobs):
                    if eng != "A":
                        continue
                    act.wait_ge(S("in_pe"), upto("in_pe", l, n + 1))
                    bank = ps[:, n % 4, :]
                    if kind == "f":
                        if l < DEPTH - 1 or i != 5:
                            A(xpad[:, i, :, 1:CTX + 1], heads(bank, 2), ACT.Identity).then_inc(S("in_act"), 1)
                        else:
                            A(xpad[:, i, 1, 1:CTX + 1], bank[:, CTX:TOK], ACT.Identity).then_inc(S("in_act"), 1)
                    elif name == "ret_vg":
                        o = A(ret(XV[:, i, :], HD).rearrange("p g (j c) -> p j g c", j=2),
                              bank[:, 0:256].rearrange("p (j g c) -> p j g c", j=2, g=2), ACT.Identity)
                        if i in tiles(l):
                            o = A(tokA[:, i, 0:256], bank[:, 256:512], ACT.Silu)
                        o.then_inc(S("in_act"), 1)
                    else:
                        A(tokA[:, i, 256:768], bank, ACT.Silu).then_inc(S("in_act"), 1)
                for n, f in enumerate((4, 5, 0, 1, 2, 3)):
                    act.wait_ge(S("conv_dve"), upto("conv_dve", l, n + 1))
                    dst = xT[:, f, :] if f < 4 else BCT[:, f - 4, :]
                    if f == 5 and l == DEPTH - 1:
                        dst = dst[:, CTX:TOK]
                    A(dst, dst, ACT.Silu).then_inc(S("conv_act"), 1)

            def na_norm(l):
                for t in range(NT):
                    lo = 0 if t in tiles(l) else 256
                    act.wait_ge(S("in_dve"), upto("in_dve", l, dve_jobs_done(l, "na_qk", t)))
                    if t > 0:
                        act.wait_ge(S("na_ss"), upto("na_ss", l, t))
                    A(sq[:, lo:512], nqk[:, t, lo:512], ACT.Square).then_inc(S("na_sq"), 1)

            def turn_operands(l):
                for n, f in enumerate((4, 0, 1, 2, 3)):
                    act.wait_ge(S("x_tr"), upto("x_tr", l, n + 1))
                    src = heads(ps[:, 4 + n % 2, :], NT)
                    c = P * f + P * (f // 2)
                    dst = Bt[:, :, :] if f == 4 else XV[:, :, c:c + P]
                    A(dst, src, ACT.Identity).then_inc(S("x_evac"), 1)
                for t in range(NT):
                    lo = 0 if t in tiles(l) else 2
                    act.wait_ge(S("ret_tr"), upto("ret_tr", l, t + 1))
                    A(retT[:, lo:4, P * t:P * t + P], heads(ps[:, 6 + t % 2, :], 4)[:, lo:4, :],
                      ACT.Identity).then_inc(S("ret_evac"), 1)
                for t in range(NT):
                    lo = 0 if t in tiles(l) else 2
                    act.wait_ge(S("naT_tr"), upto("naT_tr", l, t + 1))
                    A(naT[:, lo:4, P * t:P * t + P], heads(ps[:, t % 2, :], 4)[:, lo:4, :],
                      ACT.Identity).then_inc(S("naT_evac"), 1)

            def softplus(l):
                act.wait_ge(S("ld_rowp"), upto("ld_rowp", l, 16))
                A(nA[:, :, :], heads(rowp[:, R_DEC:R_DEC + 24], 2), ACT.Exp).then_inc(S("nA_act"), 1)
                act.wait_ge(S("dt_abs"), upto("dt_abs", l, 1))
                link(A(dta[:, :, :], dta[:, :, :], ACT.Exp, scale=-1.0))
                A(dta[:, :, :], dta[:, :, :], ACT.Ln, bias=1.0).then_inc(S("dt_ln"), 1)

            def scan(l):
                act.wait_ge(S("cum_pe"), upto("cum_pe", l, 1))
                A(EX, ps[:, 2, 0:288], ACT.Exp).then_inc(S("ex_act"), 1)
                act.wait_ge(S("seg_pe"), upto("seg_pe", l, 1))
                A(Eret[:, :, :], heads(ps[:, 6, :], 4), ACT.Exp).then_inc(S("e_act"), 1)
                for n in range(len(STATE_STEPS)):
                    mod_rows(l + 1, mod_at(l + 1, "state", n))

                def decays(n):
                    act.wait_ge(S("seg_pe"), upto("seg_pe", l, n + 2))
                    if n > 0:
                        act.wait_ge(S("mf_dve"), upto("mf_dve", l, 2 * n))
                        act.wait_ge(S("mb_pool"), upto("mb_pool", l, 2 * n))
                    A(E[:, :, :], heads(flat(6, 1024), SSD_H), ACT.Exp).then_inc(S("e_act"), 1)

                ts = tiles(l)
                decays(0)
                for point in range(3):
                    mod_rows(l + 1, mod_at(l + 1, "tile", 0, point))
                for n in range(len(ts)):
                    if n + 1 < len(ts):
                        decays(n + 1)
                        mod_rows(l + 1, mod_at(l + 1, "tile", n + 1, 0))
                    act.wait_ge(S("yz_dve"), upto("yz_dve", l, n + 1))
                    A(heads(sq, 2), ssd(line(y2), HD), ACT.Square,
                      accum_out=stat[:, 8 + n:9 + n]).then_inc(S("yss_act"), 1)
                    if n + 1 < len(ts):
                        for point in (1, 2):
                            mod_rows(l + 1, mod_at(l + 1, "tile", n + 1, point))

            def attention(l):
                for n, (t, hd) in enumerate(att_units(l)):
                    keys = TOK if t >= 2 else CTX
                    act.wait_ge(S("mx_dve"), upto("mx_dve", l, n + 1))
                    if n >= 2:
                        act.wait_ge(S("pt_pe"), upto("pt_pe", l, n - 1))
                    A(Pm[:, n % 2, 0:keys], ps[:, n % 2, 0:keys], ACT.Exp, bias=nmx[:, n:n + 1],
                      accum_out=nsum[:, n:n + 1]).then_inc(S("p_act"), 1)
                    mod_rows(l + 1, mod_at(l + 1, "unit", n))

            def mixT(l):
                ts = tiles(l)
                lo, hi = P * ts[0], P * ts[-1] + P
                for k in range(KD):
                    act.wait_ge(S("mix_tr"), upto("mix_tr", l, k + 1))
                    A(featT[:, k, lo:hi], ps[:, 6 + k % 2, lo:hi], ACT.Identity).then_inc(S("mixT"), 1)

            def gate_rows(l, which):
                act.wait_ge(S(f"row{which}_pe"), upto(f"row{which}_pe", l, 1))
                for seg in segs(l):
                    A(grow[:, seg, :], flat(2 * seg, 1024), ACT.Identity).then_inc(S(f"row{which}"), 1)

            def affinities(l):
                ts = tiles(l)
                act.wait_ge(S("rt_pe"), upto("rt_pe", l, 1))
                A(aff[:, ts[0]:NT, :], heads(ps[:, 0, NE * ts[0]:NE * NT], len(ts)),
                  ACT.Sigmoid).then_inc(S("rt_act"), 1)

            def turn_back(l):
                ts = tiles(l)
                act.wait_ge(S("f_tr"), upto("f_tr", l, KD))
                for k in range(KD):
                    act.wait_ge(S("turn_pe"), upto("turn_pe", l, k + 1))
                    A(tokA[:, ts[0]:NT, P * k:P * k + P], heads(ps[:, 4 + k % 4, :], NT)[:, ts[0]:NT, :],
                      ACT.Identity).then_inc(S("turn_act"), 1)

            def experts(l):
                first, R = load_rounds(act, l)

                def turned_x(r, i, c):
                    act.wait_ge(S("xT_pe"), job(r, i, c) + 1)
                    if not (isinstance(i, int) and 2 * i + c < 2):
                        act.wait_ge(S("up_pe"), job(r, i, c) - 1)
                    A(XT[:, c % 2, :, :], heads(flat(5, 1024), KD), ACT.Identity).then_inc(S("xT_act"), 1)

                def silu(r, i, c):
                    act.wait_ge(S("gate_pe"), job(r, i, c) + 1)
                    if not (isinstance(i, int) and 2 * i + c == 0):
                        act.wait_ge(S("hp_dve"), job(r, i, c))
                    A(hs, ps[:, 0, :], ACT.Silu).then_inc(S("hs_act"), 1)

                def turned_h(r, i, c):
                    act.wait_ge(S("hT_pe"), job(r, i, c) + 1)
                    if not (isinstance(i, int) and 2 * i + c == 0):
                        act.wait_ge(S("dn_pe"), job(r, i, c))
                    A(hT[:, :, :], heads(ps[:, 2, :], 4), ACT.Identity).then_inc(S("hT_act"), 1)

                def store(r, i, c):
                    act.wait_ge(S("y_dve"), job(r, i, c) + 1)
                    e = i * 2 + c
                    dst = (rows_out[l][CAP * e:CAP * e + CAP, :] if isinstance(e, int)
                           else rows_out[l][bass.ds(e * CAP, CAP), :])
                    act.dma_start(dst, Yb[:, c % 2, :]).then_inc(S(f"stored{c % 2}"), 16)

                def pair(r, i, first, last):
                    for c in range(2):
                        silu(r, i, c)
                        turned_h(r, i, c)
                        if not (last and c == 1):
                            turned_x(r, i, c + 1)
                        if not (first and c == 0):
                            store(r, i, c - 1)

                with act.Fori(0, R) as n_round:
                    r = n_round + first
                    act.wait_ge(S("round_dve"), r + 1)
                    turned_x(r, 0, 0)
                    pair(r, 0, True, False)
                    with act.Fori(1, NE // 2 - 1) as i:
                        pair(r, i, False, False)
                    pair(r, NE // 2 - 1, False, True)
                    store(r, NE // 2 - 1, 1)

            for l in range(DEPTH):
                if l == 0:
                    act.wait_ge(S("ld_h0"), 16)
                    act.wait_ge(S("ld_h1"), 16)
                else:
                    act.wait_ge(S("h_end"), upto("h_end", l - 1, NT))
                square_rows(l, "a", range(NT))
                if l == 0:
                    mod_rows(0, range(mod_units(0)))
                norm_evac(l, "a", range(NT))
                project(l)
                na_norm(l)
                softplus(l)
                turn_operands(l)
                scan(l)
                attention(l)
                mixT(l)
                gate_rows(l, 0)
                act.wait_ge(S("res_dve"), upto("res_dve", l, 2 * len(tiles(l))))
                square_rows(l, "f", tiles(l))
                norm_evac(l, "f", tiles(l))
                affinities(l)
                turn_back(l)
                gate_rows(l, 1)
                experts(l)

        @block.vector
        def _(dve):
            V = nc.vector
            chain = [0]

            def link(ins):
                chain[0] += 1
                ins.then_inc(S("dve_chain"), 1)
                dve.wait_ge(S("dve_chain"), chain[0])

            def after(ins, name, l, n):
                ins.then_inc(S(name), 1)
                dve.wait_ge(S(name), upto(name, l, n))

            def modulation(l):
                dve.wait_ge(S("ld_colp"), 16 * DEPTH)
                dve.wait_ge(S("mod_turned"), upto("mod_turned", l, 1))
                after(V.tensor_tensor(mod[:, l, :, :], heads(mod_columns(l), 48),
                                      spread(colp[:, l, L_BMOD:L_BMOD + 48], 2), ALU.add), "mod_evac", l, 1)
                for m, c in ((0, L_NMIX), (1, L_NFFN)):
                    i = V.scalar_tensor_tensor(modA[:, l, m, :, :], mod[:, l, 24 * m + 8:24 * m + 16, :], 1.0,
                                               spread(colp[:, l, c:c + 8], 2), ALU.add, ALU.mult)
                i.then_inc(S("modA"), 1)

            def norm_rows(l, which, ts):
                n = len(ts)
                a = slice(ts[0], ts[0] + n)
                dve.wait_ge(S(which + "_sq"), upto(which + "_sq", l, n))
                V.tensor_scalar(stat2[:, a], stat[:, a], 1.0 / D, EPS, ALU.mult, ALU.add
                                ).then_inc(S(which + "_ms"), 1)
                dve.wait_ge(S(which + "_rs"), upto(which + "_rs", l, 1))
                for t in ts:
                    V.tensor_scalar(tokA[:, t, :], h[:, t, :], stat2[:, t:t + 1], None, ALU.mult
                                    ).then_inc(S(which + "_hn"), 1)

            def project(l):
                jobs = in_jobs(l)
                for n, (name, kind, i, eng) in enumerate(jobs):
                    if eng != "D":
                        continue
                    dve.wait_ge(S("in_pe"), upto("in_pe", l, n + 1))
                    bank = ps[:, n % 4, :]
                    if kind == "dt":
                        dve.wait_ge(S("ld_rowp"), upto("ld_rowp", l, 16))
                        V.tensor_tensor(dtr.rearrange("p (t d) h -> p t (d h)", t=NT), heads(bank[:, 0:64], NT),
                                        repeat(rowp[:, R_DTB:R_DTB + 16], NT), ALU.add).then_inc(S("in_dve"), 1)
                        dve.wait_ge(S("in_dve"), upto("in_dve", l, 1))
                        V.scalar_tensor_tensor(dta[:, :, :], dtr[:, :, :], -1.0, dtr[:, :, :], ALU.mult, ALU.max
                                               ).then_inc(S("dt_abs"), 1)
                        convolve(l)
                        continue
                    lo, hi = cols_needed(l, name, i)
                    dst = {"ret_qk": qk, "na_qk": nqk, "na_v": nav}[name]
                    V.tensor_copy(dst[:, i, lo:hi], bank[:, lo:hi]).then_inc(S("in_dve"), 1)

            def convolve(l):
                for n, f in enumerate((4, 5, 0, 1, 2, 3)):
                    dve.wait_ge(S("in_act"), upto("in_act", l, n + 1))
                    full = l < DEPTH - 1 or f != 5
                    dst = heads(xT[:, f, :] if f < 4 else BCT[:, f - 4, :], 2)
                    sg = slice(0, 2) if full else slice(1, 2)
                    w = [colp[:, l, L_CW + 3 * f + j:L_CW + 3 * f + j + 1] for j in range(3)]
                    src = [xpad[:, f, sg, j:j + CTX] for j in range(3)]
                    link(V.tensor_scalar(dst[:, sg, :], src[0], w[0], colp[:, l, L_CB + f:L_CB + f + 1],
                                         ALU.mult, ALU.add))
                    link(V.scalar_tensor_tensor(dst[:, sg, :], src[1], w[1], dst[:, sg, :], ALU.mult, ALU.add))
                    V.scalar_tensor_tensor(dst[:, sg, :], src[2], w[2], dst[:, sg, :], ALU.mult, ALU.add
                                           ).then_inc(S("conv_dve"), 1)

            def na_norm(l):
                ts = tiles(l)
                for t in range(NT):
                    lo = 0 if t in ts else 4
                    dve.wait_ge(S("na_sq"), upto("na_sq", l, t + 1))
                    V.tensor_reduce(rs[:, t, lo:8], heads(sq, 8)[:, lo:8, :], AX.X, ALU.add
                                    ).then_inc(S("na_ss"), 1)
                dve.wait_ge(S("na_ss"), upto("na_ss", l, NT))
                V.tensor_scalar(rs[:, :, 4:8], rs[:, :, 4:8], 1.0 / HD, EPS, ALU.mult, ALU.add)
                V.tensor_scalar(rs[:, ts[0]:NT, 0:4], rs[:, ts[0]:NT, 0:4], 1.0, HD * EPS, ALU.mult, ALU.add
                                ).then_inc(S("na_ms"), 1)
                dve.wait_ge(S("na_rs"), upto("na_rs", l, 1))
                for t in range(NT):
                    lo = 0 if t in ts else 4
                    v = heads(nqk[:, t, :], 8)[:, lo:8, :]
                    link(V.tensor_tensor(v, v, spread(rs[:, t, lo:8], HD), ALU.mult))
                    V.tensor_tensor(v, v, heads(rowp[:, R_NQK:R_NQK + 512], 8)[:, lo:8, :], ALU.mult
                                    ).then_inc(S("na_norm"), 1)

            def log_decays(l):
                dve.wait_ge(S("nA_act"), upto("nA_act", l, 1))
                link(V.memset(DTX[:, :, :], SCALE))
                n6 = nA.rearrange("p d (g h) -> p (d g) h", g=2)
                V.tensor_scalar(n6[:, :, 0:4], n6[:, :, 0:4], -1.0, None, ALU.mult)
                link(V.tensor_scalar(n6[:, :, 4:6], n6[:, :, 4:6], -1.0 / SCALE, None, ALU.mult))
                dve.wait_ge(S("dt_ln"), upto("dt_ln", l, 1))
                by6 = DTX.rearrange("p a (g h) -> p (a g) h", g=2)[:, :, 0:4]
                by4 = [v.rearrange("p a (g h) -> p (a g) h", g=2) for v in (dtr, dta)]
                link(V.scalar_tensor_tensor(by6, by4[0], 0.0, by4[1], ALU.max, ALU.add))
                V.tensor_tensor(Aall.rearrange("p (t d) h -> p t (d h)", t=NT),
                                DTX.rearrange("p (t d) h -> p t (d h)", t=NT),
                                repeat(nA.rearrange("p d h -> p (d h)"), NT), ALU.mult).then_inc(S("loga"), 1)
                dve.wait_ge(S("loga"), upto("loga", l, 1))

            def ret_triangle(l):
                dve.wait_ge(S("x_evac"), upto("x_evac", l, 5))
                V.tensor_tensor(*triangle_rows(rf[:, 0:RET_H, :], ret(Aall[:, 0, :]), 2, LE), ALU.mult
                                ).then_inc(S("rf_dve"), 1)

            def triangle(l, n):
                t = tiles(l)[n]
                dve.wait_ge(S("seg_pe"), upto("seg_pe", l, n + 1))
                V.tensor_tensor(*triangle_rows(rf, ssd(Aall[:, 2 * t, :]), 4, LE), ALU.mult
                                ).then_inc(S("rf_dve"), 1)

            def chunk_weights(l):
                dve.wait_ge(S("ex_act"), upto("ex_act", l, 1))
                for d in range(2):
                    V.tensor_tensor(Wt[:, d, :, :], heads(EX[:, 96 + 48 * d:144 + 48 * d], NT),
                                    DTX[:, d:2 * NT:2, :], ALU.mult)
                T = heads(EX[:, 192:288], 2 * NT)
                V.tensor_copy(Dec[0:64, :, :], T[0:64, :, 0:6])
                link(V.tensor_copy(Dec[64:128, :, :], T[64:128, :, 6:12]))
                dve.wait_ge(S("e_act"), upto("e_act", l, 1))
                link(V.tensor_tensor(Eret[:, :, :], Eret[:, :, :], repeat(const[:, C_DRET:C_DRET + P], RET_H), ALU.mult))

            def states(l):
                def weigh(n):
                    d, t = STATE_STEPS[n]
                    if n > 0:
                        dve.wait_ge(S("st_pe"), upto("st_pe", l, n))
                    V.tensor_tensor(VW[:, :, :], heads(XV[:, t, :], NH), spread(Wt[:, d, t, :], HD), ALU.mult
                                    ).then_inc(S("vw_dve"), 1)

                weigh(0)
                for n, (d, t) in enumerate(STATE_STEPS):
                    if n + 1 < len(STATE_STEPS):
                        weigh(n + 1)
                    else:
                        dve.wait_ge(S("st_pe"), upto("st_pe", l, n + 1))
                    bank = ps[:, 3 + n % 2, 0:384]
                    new = Hs[:, d, STATE_NEXT[d, t], :]
                    if n < 2:
                        V.tensor_copy(new, bank).then_inc(S("h_dve"), 1)
                    else:
                        if n == 2:
                            dve.wait_ge(S("h_dve"), upto("h_dve", l, 2))
                        else:
                            dve.wait_ge(S("h_dve"), upto("h_dve", l, n - 1))
                        link(V.tensor_tensor(heads(new, 6), heads(Hs[:, d, t, :], 6),
                                             spread(Dec[:, 2 * t + d, :], HD), ALU.mult))
                        V.tensor_tensor(new, new, bank, ALU.add).then_inc(S("h_dve"), 1)

            def scan_head(l, n):
                dve.wait_ge(S("sc_pe"), upto("sc_pe", l, n + 1))
                if n > 0:
                    dve.wait_ge(S("mb_pool"), upto("mb_pool", l, 2 * n))
                    dve.wait_ge(S("mf_dve"), upto("mf_dve", l, 2 * n))
                s = ps[:, 6:8, 0:P]
                V.tensor_tensor(sL[:, :, :], s, repeat(GE, 2), ALU.mult).then_inc(S("sl_dve"), 1)
                link(V.tensor_tensor(sU[:, :, :], s, repeat(LE, 2), ALU.mult))
                if n > 0:
                    dve.wait_ge(S("y_pe"), upto("y_pe", l, n))
                two = lambda v: v.rearrange("p (g h) c -> p g (h c)", g=2)
                V.tensor_tensor(two(Mret), two(Eret), ps[:, 6:8, P:3 * P], ALU.mult
                                ).then_inc(S("mret_dve"), 1)
                dve.wait_ge(S("e_act"), upto("e_act", l, n + 2))
                for g in range(2):
                    if n > 0:
                        dve.wait_ge(S("diag_pe"), upto("diag_pe", l, 2 * n - 1 + g))
                    V.tensor_tensor(Mf[:, g, :, :], E[:, 4 * g:4 * g + 4, :], repeat(sU[:, g, :], 4), ALU.mult
                                    ).then_inc(S("mf_dve"), 1)
                if n + 1 < len(tiles(l)):
                    triangle(l, n + 1)

            def scan_tail(l, n):
                t = tiles(l)[n]
                dve.wait_ge(S("y_pe"), upto("y_pe", l, n + 1))
                ds = dirs_of(t)
                places = lambda v: v.rearrange("p (g h) c -> p g h c", g=2)
                for k, d in enumerate(ds):
                    at = 48 * d + NH * t
                    link(V.tensor_tensor(places(y if k == 0 else y2), scan_outs(1 + d),
                                         spread2(heads(EX[:, at:at + NH], 2), HD), ALU.mult))
                after(V.tensor_tensor(places(y), places(y), scan_outs(0), ALU.add), "comb_dve", l, n + 1)
                if len(ds) == 2:
                    link(V.tensor_tensor(y[:, :, :], y[:, :, :], y2[:, :, :], ALU.add))
                ys, y2s = ssd(line(y), HD), ssd(line(y2), HD)
                dve.wait_ge(S("dx_pool"), upto("dx_pool", l, n + 1))
                link(V.tensor_tensor(ys, ys, heads(line(dx), 2), ALU.add))
                V.tensor_tensor(y2s, ys, heads(tokA[:, t, 256:768], 2), ALU.mult).then_inc(S("yz_dve"), 1)
                four = lambda v: v.rearrange("p g (h c) -> p g h c", h=2)
                yr, sqr = four(ret(line(y), HD)), four(ret(line(y2), HD))
                mu, var = heads(stat2[:, 8:12], 2), heads(stat2[:, 16:20], 2)
                link(V.tensor_reduce(mu, yr, AX.X, ALU.add))
                link(V.tensor_scalar(mu, mu, -1.0 / HD, None, ALU.mult))
                link(V.tensor_tensor(yr, yr, spread2(mu, HD), ALU.add))
                link(V.tensor_tensor(sqr, yr, yr, ALU.mult))
                link(V.tensor_reduce(var, sqr, AX.X, ALU.add))
                V.tensor_scalar(var, var, 1.0 / HD, EPS, ALU.mult, ALU.add)
                dve.wait_ge(S("yss_act"), upto("yss_act", l, n + 1))
                V.tensor_scalar(stat2[:, 20:21], stat[:, 8 + n:9 + n], 1.0 / (SSD_H * HD), EPS, ALU.mult, ALU.add
                                ).then_inc(S("gn_ms"), 1)
                dve.wait_ge(S("gn_rs"), upto("gn_rs", l, n + 1))
                V.scalar_tensor_tensor(heads(tokA[:, t, 256:768], 2), y2s, stat2[:, 20:21],
                                       heads(rowp[:, R_NORM:R_NORM + 512], 2), ALU.mult, ALU.mult)
                link(V.tensor_tensor(yr, yr, spread2(var, HD), ALU.mult))
                g = tokA[:, t, 0:256].rearrange("p (j g c) -> p g j c", j=2, g=2)
                link(V.tensor_tensor(g, yr, g, ALU.mult))

            def scan(l):
                ret_triangle(l)
                chunk_weights(l)
                triangle(l, 0)
                states(l)
                scan_head(l, 0)
                for n in range(len(tiles(l))):
                    if n + 1 < len(tiles(l)):
                        scan_head(l, n + 1)
                    scan_tail(l, n)

            def attention(l):
                dve.wait_ge(S("ld_bias"), upto("ld_bias", l, 16 * 2 * NA_H))
                b = bias.rearrange("p a b c -> p (a b) c")
                V.tensor_tensor(b, b, repeat(const[:, C_MASK:C_MASK + GRID], NA_H * 6), ALU.add
                                ).then_inc(S("bias_dve"), 1)
                un = att_units(l)

                def maximum(n):
                    keys = TOK if un[n][0] >= 2 else CTX
                    dve.wait_ge(S("s_pe"), upto("s_pe", l, n + 1))
                    V.tensor_reduce(nmx[:, n:n + 1], ps[:, n % 2, 0:keys], AX.X, ALU.max, negate=True
                                    ).then_inc(S("mx_dve"), 1)

                def turned(n):
                    nk = NT if un[n][0] >= 2 else 2
                    dve.wait_ge(S("pt_pe"), upto("pt_pe", l, n + 1))
                    if n >= 2:
                        dve.wait_ge(S("pv_pe"), upto("pv_pe", l, n - 1))
                    V.tensor_copy(PT[:, n % 2, 0:nk, :], heads(ps[:, 2 + n % 2, :], NT)[:, 0:nk, :]
                                  ).then_inc(S("pt_dve"), 1)

                def normalise(tile):
                    t = tiles(l)[tile]
                    c = slice(NA_H * tile, NA_H * tile + NA_H)
                    dve.wait_ge(S("pv_pe"), upto("pv_pe", l, NA_H * (tile + 1)))
                    link(V.reciprocal(nrec[:, c], nsum[:, c]))
                    o = V.tensor_tensor(heads(tokA[:, t, 768:1024], NA_H), heads(ps[:, 4 + 2 * (tile % 2), 0:256], NA_H),
                                        spread(nrec[:, c], HD), ALU.mult)
                    o.then_inc(S("na_out"), 1)

                N = len(un)
                maximum(0)
                for n in range(N):
                    if n + 1 < N:
                        maximum(n + 1)
                    if n >= 1 and n % NA_H == 0:
                        normalise(n // NA_H - 1)
                    turned(n)
                normalise(N // NA_H - 1)

            def gate_diag(l, which):
                if which == 1:
                    dve.wait_ge(S("res_dve"), upto("res_dve", l, 2 * len(tiles(l))))
                for seg in segs(l):
                    c = 24 * which + 16
                    V.tensor_tensor(heads(diag[:, seg, :], KD), repeat(ident, KD),
                                    spread(mod[:, l, c:c + 8, seg], P), ALU.mult).then_inc(S(f"diag{which}"), 1)

            def residual(l):
                dve.wait_ge(S("row0"), upto("row0", l, len(segs(l))))
                ts = tiles(l)
                n = 0
                for half in range(N_OUT):
                    c = slice(512 * half, 512 * half + 512)
                    for t in ts:
                        dve.wait_ge(S("out_pe"), upto("out_pe", l, n + 1))
                        link(V.tensor_tensor(Pm[:, n % 2, :], grow[:, t // 2, c], ps[:, 4 + n % 2, :], ALU.mult))
                        V.tensor_tensor(h[:, t, c], h[:, t, c], Pm[:, n % 2, :], ALU.add).then_inc(S("res_dve"), 1)
                        n += 1

            def route(l):
                ts = tiles(l)
                T = len(ts)
                t0 = ts[0]
                dve.wait_ge(S("ld_rb"), 16)
                dve.wait_ge(S("rt_act"), upto("rt_act", l, 1))
                se = sel.rearrange("p (t g) e -> p t (g e)", t=NT)[:, t0:NT, :]
                af = aff[:, t0:NT, :]
                link(V.tensor_tensor(se, af, repeat(rb[:, :], T), ALU.add))
                s4 = sel[:, 4 * t0:4 * NT, :]
                fl = lambda v: v.rearrange("p t g -> p (t g)")[:, 4 * t0:4 * NT]
                a, b, c, d = fl(g1), fl(g2), fl(g3), fl(g4)
                e = [s4[:, :, j] for j in range(4)]
                link(V.tensor_tensor(a, e[0], e[1], ALU.add))
                link(V.tensor_tensor(b, e[2], e[3], ALU.add))
                link(V.tensor_tensor(a, a, b, ALU.max))
                link(V.tensor_tensor(b, e[0], e[1], ALU.max))
                link(V.tensor_tensor(c, e[2], e[3], ALU.max))
                link(V.tensor_tensor(b, b, c, ALU.add))
                link(V.tensor_tensor(a, a, b, ALU.max))

                def rank(v, n, out):
                    other = v.unsqueeze(2).to_broadcast([P, n, 4, 4])
                    own = v.unsqueeze(3).to_broadcast([P, n, 4, 4])
                    x1 = cmp1[:, 0:n, :].rearrange("p n (i j) -> p n i j", i=4)
                    x2 = cmp2[:, 0:n, :].rearrange("p n (i j) -> p n i j", i=4)
                    link(V.tensor_tensor(x1, other, own, ALU.is_gt))
                    link(V.tensor_tensor(x2, other, own, ALU.is_equal))
                    link(V.tensor_tensor(cmp2[:, 0:n, :], cmp2[:, 0:n, :],
                                         repeat(const[:, C_TRI:C_TRI + 16], n), ALU.mult))
                    link(V.tensor_tensor(cmp1[:, 0:n, :], cmp1[:, 0:n, :], cmp2[:, 0:n, :], ALU.add))
                    link(V.tensor_reduce(out, x1, AX.X, ALU.add))

                rank(g1[:, t0:NT, :], T, g4[:, t0:NT, :])
                link(V.tensor_scalar(d, d, 0.5, None, ALU.is_lt))
                cn = chosen[:, 0:4 * T, :]
                rank(s4, 4 * T, cn)
                link(V.tensor_scalar(cn, cn, 1.5, None, ALU.is_lt))
                after(V.tensor_tensor(cn, cn, spread(d, 4), ALU.mult), "chosen_dve", l, 1)
                ga = gates[:, t0:NT, :]
                link(V.tensor_tensor(ga, af, cn.rearrange("p (t g) e -> p t (g e)", t=T), ALU.mult))
                link(V.tensor_reduce(rsum[:, t0:NT], ga, AX.X, ALU.add))
                link(V.reciprocal(rsum[:, t0:NT], rsum[:, t0:NT]))
                link(V.tensor_tensor(ga, ga, spread(rsum[:, t0:NT], NE), ALU.mult))

            def assign(l):
                ts = tiles(l)
                T, t0 = len(ts), ts[0]
                ch = chosen[:, 0:4 * T, :].rearrange("p (t g) e -> p t (g e)", t=T)
                pl, pk, tm = place[:, t0:NT, :], pick[:, t0:NT, :], tmp16[:, t0:NT, :]
                dve.wait_ge(S("pos_pe"), upto("pos_pe", l, 1))
                link(V.tensor_copy(count, ps[:, 2, 0:NE]))
                link(V.tensor_reduce(few[:, 0:1], count, AX.X, ALU.max))
                link(V.tensor_scalar(few[:, 1:2], few[:, 0:1], float(CAP), 1.0, ALU.is_gt, ALU.add))
                for n in range(2, T):
                    link(V.tensor_scalar(few[:, 2:3], few[:, 0:1], float(n * CAP), None, ALU.is_gt))
                    link(V.tensor_tensor(few[:, 1:2], few[:, 1:2], few[:, 2:3], ALU.add))
                link(V.tensor_scalar(pl, heads(ps[:, 1, NE * t0:NE * NT], T), float(CAP + 4096), None, ALU.add))
                link(V.tensor_tensor(pl, pl, ch, ALU.mult))
                link(V.tensor_scalar(pl, pl, -4096.0, None, ALU.add))
                V.tensor_copy(rounds[:, l:l + 1], few[:, 1:2]).then_inc(S("rounds_dve"), 1)
                dve.wait_ge(S("rounds_dve"), upto("rounds_dve", l, 1))

            def choices(l):
                ts = tiles(l)
                T, t0 = len(ts), ts[0]
                ch = chosen[:, 0:4 * T, :].rearrange("p (t g) e -> p t (g e)", t=T)
                pl, pk, tm = place[:, t0:NT, :], pick[:, t0:NT, :], tmp16[:, t0:NT, :]
                ex = repeat(const[:, C_EXP:C_EXP + NE], T)
                link(V.tensor_tensor(tm, ch, ex, ALU.mult))
                link(V.tensor_reduce(first2[:, 0, t0:NT], tm, AX.X, ALU.max))
                link(V.tensor_tensor(pk, spread(first2[:, 0, t0:NT], NE), ex, ALU.is_equal))
                for n in range(2):
                    if n == 1:
                        link(V.tensor_tensor(pk, ch, pk, ALU.subtract))
                        link(V.tensor_tensor(tm, pk, ex, ALU.mult))
                        link(V.tensor_reduce(first2[:, 1, t0:NT], tm, AX.X, ALU.add))
                    link(V.tensor_tensor(tm, pk, pl, ALU.mult))
                    link(V.tensor_reduce(pos2[:, n, t0:NT], tm, AX.X, ALU.add))
                    link(V.tensor_tensor(tm, pk, gates[:, t0:NT, :], ALU.mult))
                    link(V.tensor_reduce(gate2[:, n, t0:NT], tm, AX.X, ALU.add))

            def experts(l):
                ts = tiles(l)
                T, t0 = len(ts), ts[0]
                dve.wait_ge(S("acc_zero"), upto("acc_zero", l, 1))
                first, R = load_rounds(dve, l)

                def slots_of(r, i, c):
                    e = i * 2 + c
                    if not (isinstance(i, int) and e < 2):
                        dve.wait_ge(S("who_pe"), job(r, i, c) - 1)
                    col = place[:, t0:NT, e:e + 1] if isinstance(e, int) else place[:, t0:NT, bass.ds(e, 1)]
                    V.tensor_tensor(onehot[:, c % 2, 0:T, :], repeat(const[:, C_IOTA:C_IOTA + P], T),
                                    col.to_broadcast([P, T, P]), ALU.is_equal).then_inc(S("onehot_dve"), 1)

                def who(r, i, c):
                    dve.wait_ge(S("who_pe"), job(r, i, c) + 1)
                    if not (isinstance(i, int) and 2 * i + c < 2):
                        dve.wait_ge(S(f"gathered{c % 2}"), (r * (NE // 2) + (i + c // 2)) * 16)
                    V.tensor_copy(slot_i[:, c % 2:c % 2 + 1], ps[:, 7, 0:1]).then_inc(S("who_dve"), 1)

                def product(r, i, c):
                    dve.wait_ge(S("hs_act"), job(r, i, c) + 1)
                    dve.wait_ge(S("up_pe"), job(r, i, c) + 1)
                    if not (isinstance(i, int) and 2 * i + c == 0):
                        dve.wait_ge(S("hT_pe"), job(r, i, c))
                    V.tensor_tensor(hp, hs, ps[:, 1, :], ALU.mult).then_inc(S("hp_dve"), 1)

                def result(r, i, c):
                    dve.wait_ge(S("dn_pe"), job(r, i, c) + 1)
                    if not (isinstance(i, int) and 2 * i + c < 2):
                        dve.wait_ge(S(f"stored{c % 2}"), (r * (NE // 2) + i) * 16)
                    V.tensor_copy(Yb[:, c, :], flat(3, 1024)).then_inc(S("y_dve"), 1)

                def pair(r, i, last):
                    for c in range(2):
                        if not last:
                            slots_of(r, i, c + 2)
                        product(r, i, c)
                        if not last:
                            who(r, i, c + 2)
                        result(r, i, c)

                def rows_of_round(r):
                    p, f, w, m = (v[:, :, t0:NT] for v in (pos2, first2, row2, inround))
                    V.tensor_scalar(p, p, -float(CAP), None, ALU.add).then_inc(S("row_steps"), 1)
                    dve.wait_ge(S("row_steps"), r * 6 + 1)
                    V.tensor_scalar(w, p, float(CAP), None, ALU.is_lt)
                    V.tensor_scalar(m, p, 0.0, None, ALU.is_ge).then_inc(S("row_steps"), 1)
                    dve.wait_ge(S("row_steps"), r * 6 + 2)
                    V.tensor_tensor(m, m, w, ALU.mult).then_inc(S("row_steps"), 1)
                    dve.wait_ge(S("row_steps"), r * 6 + 3)
                    V.scalar_tensor_tensor(w, p, -float(NO_ROW), f, ALU.add, ALU.add).then_inc(S("row_steps"), 1)
                    dve.wait_ge(S("row_steps"), r * 6 + 4)
                    V.tensor_tensor(w, w, m, ALU.mult).then_inc(S("row_steps"), 1)
                    dve.wait_ge(S("row_steps"), r * 6 + 5)
                    V.tensor_scalar(w, w, float(NO_ROW), None, ALU.add).then_inc(S("row_steps"), 1)
                    dve.wait_ge(S("row_steps"), r * 6 + 6)
                    V.tensor_copy(row_i[:, :, t0:NT], w).then_inc(S("row_dve"), 1)

                with dve.Fori(0, R) as n_round:
                    r = n_round + first
                    pl = place[:, t0:NT, :]
                    V.tensor_scalar(pl, pl, -float(CAP), None, ALU.add).then_inc(S("round_dve"), 1)
                    dve.wait_ge(S("round_dve"), r + 1)
                    slots_of(r, 0, 0)
                    slots_of(r, 0, 1)
                    who(r, 0, 0)
                    who(r, 0, 1)
                    rows_of_round(r)
                    pair(r, 0, False)
                    with dve.Fori(1, NE // 2 - 1) as i:
                        pair(r, i, False)
                    pair(r, NE // 2 - 1, True)
                    for q in range(2 * T):
                        n, t = divmod(q, T)
                        dve.wait_ge(X(f"back{q % 4}", l), (n_round * (2 * T // 4) + (q // 4 + 1)) * 16)
                        if q >= T:
                            dve.wait_ge(X("acc_dve", l), n_round * (2 * T) + (q - T + 1))
                        V.scalar_tensor_tensor(tokA[:, t0 + t, :], back[q % 4], gate2[:, n, t0 + t:t0 + t + 1],
                                               tokA[:, t0 + t, :], ALU.mult, ALU.add).then_inc(X("acc_dve", l), 1)
                    dve.wait_ge(X("acc_dve", l), n_round * (2 * T) + 2 * T)
                dve.wait_ge(S("row1"), upto("row1", l, len(segs(l))))
                for t in ts:
                    link(V.tensor_tensor(tokA[:, t, :], tokA[:, t, :], grow[:, t // 2, :], ALU.mult))
                    V.tensor_tensor(h[:, t, :], h[:, t, :], tokA[:, t, :], ALU.add).then_inc(S("h_end"), 1)

            dve.wait_ge(S("ld_const"), 16)
            for l in range(DEPTH):
                if l == 0:
                    modulation(0)
                norm_rows(l, "a", range(NT))
                project(l)
                na_norm(l)
                log_decays(l)
                scan(l)
                attention(l)
                gate_diag(l, 0)
                if l + 1 < DEPTH:
                    modulation(l + 1)
                residual(l)
                norm_rows(l, "f", tiles(l))
                gate_diag(l, 1)
                route(l)
                assign(l)
                choices(l)
                experts(l)

        @block.gpsimd
        def _(pool):
            G = nc.gpsimd
            chain = [0]

            def link(ins):
                chain[0] += 1
                ins.then_inc(S("pool_chain"), 1)
                pool.wait_ge(S("pool_chain"), chain[0])

            def rsqrt(v, n):
                return G.tensor_tensor(v, v, pw[:, 0:n], ALU.pow)

            def rope(l):
                for n, t in enumerate((2, 3)):
                    pool.wait_ge(S("in_dve"), upto("in_dve", l, dve_jobs_done(l, "ret_qk", t)))
                    v = heads(qk[:, t, :], 8)
                    a = heads(y.rearrange("p a b -> p (a b)")[:, 0:512], 8)
                    b = heads(y2.rearrange("p a b -> p (a b)")[:, 0:512], 8)
                    cos = const[:, C_COS + 64 * n:C_COS + 64 * n + 64]
                    sin = heads(const[:, C_SIN + 64 * n:C_SIN + 64 * n + 64], 2)
                    link(G.tensor_tensor(a, v, repeat(cos, 8), ALU.mult))
                    for half in range(2):
                        o, s = slice(16 * half, 16 * half + 16), slice(16 - 16 * half, 32 - 16 * half)
                        parts = lambda w, c: w.rearrange("p a (b c) -> p a b c", b=2)[:, :, :, c]
                        link(G.tensor_tensor(parts(b, o), parts(v, s),
                                             sin[:, :, o].unsqueeze(1).to_broadcast([P, 8, 2, 16]), ALU.mult))
                    G.tensor_tensor(v, a, b, ALU.add).then_inc(S("rope"), 1)
                    pool.wait_ge(S("rope"), upto("rope", l, n + 1))

            def triangle(l, n):
                if n < 0:
                    pool.wait_ge(S("loga"), upto("loga", l, 1))
                    pool.wait_ge(S("x_evac"), upto("x_evac", l, 5))
                    G.tensor_tensor(*triangle_rows(rbk[:, 0:RET_H, :], ret(Aall[:, 1, :]), 2, GE), ALU.mult
                                    ).then_inc(S("rb_pool"), 1)
                    return
                t = tiles(l)[n]
                pool.wait_ge(S("seg_pe"), upto("seg_pe", l, n + 1))
                G.tensor_tensor(*triangle_rows(rbk, ssd(Aall[:, 2 * t + 1, :]), 4, GE), ALU.mult
                                ).then_inc(S("rb_pool"), 1)

            def scan_head(l, n):
                t = tiles(l)[n]
                if n > 0:
                    pool.wait_ge(S("diag_pe"), upto("diag_pe", l, 2 * n))
                v = ssd(XV[:, t, :], HD).rearrange("p g (h c) -> p g h c", h=4)
                by_group = lambda w: w.rearrange("p (g h) c -> p g h c", g=2)
                G.tensor_tensor(by_group(Vf), v, spread2(ssd(DTX[:, 2 * t, :]), HD), ALU.mult)
                G.tensor_tensor(by_group(Vb), v, spread2(ssd(DTX[:, 2 * t + 1, :]), HD), ALU.mult
                                ).then_inc(S("v_pool"), 1)
                pool.wait_ge(S("sl_dve"), upto("sl_dve", l, n + 1))
                pool.wait_ge(S("e_act"), upto("e_act", l, n + 2))
                for g in range(2):
                    G.tensor_tensor(Mb[:, g, :, :], E[:, 4 * g:4 * g + 4, :], repeat(sL[:, g, :], 4), ALU.mult
                                    ).then_inc(S("mb_pool"), 1)
                if n + 1 < len(tiles(l)):
                    triangle(l, n + 1)

            def scan_tail(l, n):
                t = tiles(l)[n]
                if n > 0:
                    pool.wait_ge(S("yz_dve"), upto("yz_dve", l, n))
                G.tensor_tensor(dx.rearrange("p (g h) c -> p g h c", g=2),
                                ssd(XV[:, t, :], HD).rearrange("p g (h c) -> p g h c", h=4),
                                spread2(heads(rowp[:, R_D:R_D + SSD_H], 2), HD), ALU.mult).then_inc(S("dx_pool"), 1)
                pool.wait_ge(S("gn_ms"), upto("gn_ms", l, n + 1))
                rsqrt(stat2[:, 16:21], 5).then_inc(S("gn_rs"), 1)

            def experts(l):
                ts = tiles(l)
                T, t0 = len(ts), ts[0]
                first, R = load_rounds(pool, l)

                def step_on():
                    pool.sem_inc(S("pool_steps"), 1)

                def gather(r, i, c):
                    pool.wait_ge(S("who_dve"), job(r, i, c) + 1)
                    if not isinstance(i, int):
                        pool.wait_ge(S("xT_pe"), job(r, i, c) - 1)
                    step_on()
                    G.indirect_dma_start(gathered[c], None, rows_in[l], bass.IndirectOffsetOnAxis(slot_i[:, c:c + 1], 0)
                                         ).then_inc(S(f"gathered{c}"), 16)

                pool.wait_ge(S("row1_pe"), upto("row1_pe", l, 1))
                with pool.Fori(0, R) as n_round:
                    r = n_round + first
                    pool.wait_ge(S("round_dve"), r + 1)
                    for c in range(2):
                        gather(r, 0, c)
                    with pool.Fori(1, NE // 2) as i:
                        for c in range(2):
                            gather(r, i, c)
                    pool.wait_ge(S("row_dve"), r + 1)
                    pool.wait_ge(S("xT_pe"), job(r, NE // 2))
                    for c in range(2):
                        pool.wait_ge(S(f"stored{c}"), (r + 1) * (NE // 2) * 16)
                    step_on()
                    pool.wait_ge(X("no_row", l), 16)
                    for q in range(2 * T):
                        n, t = divmod(q, T)
                        if q >= 4:
                            pool.wait_ge(X("acc_dve", l), n_round * (2 * T) + (q - 3))
                            step_on()
                        G.indirect_dma_start(back[q % 4], None, rows_out[l],
                                             bass.IndirectOffsetOnAxis(row_i[:, n, t0 + t:t0 + t + 1], 0)
                                             ).then_inc(X(f"back{q % 4}", l), 16)

            G.memset(zero8[:, :], 0.0).then_inc(S("zero_pool"), 1)
            link(G.memset(pw[:, :], -0.5))
            pool.wait_ge(S("ld_const"), 16)
            for l in range(DEPTH):
                ts = tiles(l)
                if l > 0:
                    pool.wait_ge(S("h_end"), upto("h_end", l - 1, len(tiles(l - 1))))
                for c in (0, CTX + 1):
                    i = G.memset(xpad[:, :, :, c:c + 1], 0.0)
                i.then_inc(S("pad_zero"), 1)
                pool.wait_ge(S("a_ms"), upto("a_ms", l, 1))
                rsqrt(stat2[:, 0:NT], NT).then_inc(S("a_rs"), 1)
                rope(l)
                pool.wait_ge(S("na_ms"), upto("na_ms", l, 1))
                G.tensor_tensor(rs[:, :, 4:8], rs[:, :, 4:8], pw[:, 0:16].rearrange("p (a b) -> p a b", a=NT), ALU.pow)
                G.tensor_tensor(rs[:, ts[0]:NT, 0:4], rs[:, ts[0]:NT, 0:4],
                                pw[:, 0:4 * len(ts)].rearrange("p (a b) -> p a b", b=4), ALU.pow
                                ).then_inc(S("na_rs"), 1)
                triangle(l, -1)
                triangle(l, 0)
                pool.wait_ge(S("ld_rowp"), upto("ld_rowp", l, 16))
                scan_head(l, 0)
                for n in range(len(ts)):
                    if n + 1 < len(ts):
                        scan_head(l, n + 1)
                    scan_tail(l, n)
                pool.wait_ge(S("f_ms"), upto("f_ms", l, 1))
                rsqrt(stat2[:, ts[0]:NT], len(ts)).then_inc(S("f_rs"), 1)
                pool.wait_ge(S("f_stored"), upto("f_stored", l, 16))
                G.memset(tokA[:, ts[0]:NT, :], 0.0).then_inc(S("acc_zero"), 1)
                experts(l)


_RAW = ["x", "ctx", "w_mod", "w_in", "w_out", "na_rpb", "router_w", "router_b", "w_gate", "w_up", "w_down"]


def _layout(i):
    a = {k: np.ascontiguousarray(np.asarray(i[k])) for k in _RAW}
    a["x"], a["ctx"] = a["x"][0], a["ctx"][0]
    a["consts"] = shape_constants()
    col = lambda v: v.reshape(v.shape[0], -1, P).transpose(0, 2, 1)
    c = np.stack([np.asarray(i["c"])[0], np.asarray(i["c_ctx"])])[::-1]
    a["condT"] = np.ascontiguousarray(c.reshape(2, KD, P).transpose(2, 1, 0))
    cw = np.asarray(i["ssd_conv_w"])
    cw = cw.reshape(DEPTH, 3, 6, P).transpose(0, 3, 2, 1).reshape(DEPTH, P, 18)
    a["colp"] = np.ascontiguousarray(np.concatenate(
        [col(np.asarray(i["b_mod"])), col(np.asarray(i["norm_mix"])), col(np.asarray(i["norm_ffn"])), cw,
         col(np.asarray(i["ssd_conv_b"]))], axis=2))
    g = lambda k: np.asarray(i[k])
    qn = np.broadcast_to(g("na_q_norm")[:, None], (DEPTH, NA_H, HD)).reshape(DEPTH, -1)
    kn = np.broadcast_to(g("na_k_norm")[:, None], (DEPTH, NA_H, HD)).reshape(DEPTH, -1)

    def placed(d):
        s, r = g("ssd_a_log_" + d), g("ret_decay_" + d)
        return np.concatenate([s[:, 0:4], r[:, 0::2], s[:, 4:8], r[:, 1::2]], axis=1)

    a["rowp"] = np.ascontiguousarray(np.concatenate(
        [g("ssd_dt_bias_f"), g("ssd_dt_bias_b"), placed("f"), placed("b"), g("ssd_d"), qn, kn, g("ssd_norm")], axis=1))
    return a


def kernel(**inputs):
    import concourse.bacc as _bacc
    from concourse.bass_utils import run_bass_kernel_spmd as _run

    nc = _bacc.Bacc("TRN2", target_bir_lowering=False, num_devices=1)
    arrays = {f"in_{k}": v for k, v in _layout(inputs).items()}
    ins = {k[3:]: nc.dram_tensor(k, v.shape, mybir.dt.from_np(v.dtype), kind="ExternalInput").ap()
           for k, v in arrays.items()}
    out = nc.dram_tensor("out_0", (SEQ, D), F32, kind="ExternalOutput").ap()
    trunk(nc, ins, out)
    r = _run(nc, [arrays], core_ids=[0])
    return r.results[0]["out_0"].reshape(1, SEQ, D)
```

```python
from contextlib import ExitStack
import math

import numpy as np
import concourse.bass as bass
from concourse import mybir

F32 = mybir.dt.float32
U32 = mybir.dt.uint32
I32 = mybir.dt.int32
ALU = mybir.AluOpType
ACT = mybir.ActivationFunctionType
AX = mybir.AxisListType

P = 128
D = 1024
KD = D // P
DEPTH = 2
GRID = 64
CTX = 256
SEQ = 256
TOK = CTX + SEQ
NT = TOK // P
HD = 64
RET_H, SSD_H, NA_H = 4, 8, 4
NH = SSD_H + RET_H
STATE = 64
NE = 16
FE = 512
EPS = 1e-6
SCALE = HD ** -0.5
NEG = -1e30

IN_PIECES = (("bc_dt", 2048, 272), ("x", 1536, 512), ("ret_qk", 0, 512), ("ret_vg", 512, 512),
             ("z", 1024, 512), ("na_qk", 2320, 512), ("na_v", 2832, 256))
CAP = P
NO_ROW = NE * CAP
N_MOD = 12
N_OUT = 2
SLOT = 4096

C_ID, C_LE, C_GT, C_GE, C_LT, C_ONE, C_DRET, C_FLIP = (P * i for i in range(8))
C_MASK = 8 * P
C_COS = C_MASK + 64
C_SIN = C_COS + 128
C_TRI = C_SIN + 128
C_IOTA = C_TRI + 16
C_TOK = C_IOTA + P
C_EXP = C_TOK + 4
N_CONST = C_EXP + NE
L_BMOD, L_NMIX, L_NFFN, L_CW, L_CB = 0, 48, 56, 64, 82
N_COLP = 88
R_DTB, R_DEC, R_D, R_NQK, R_NORM = 0, 16, 40, 48, 560
N_ROWP = 1072


def shape_constants():
    c = np.zeros((P, N_CONST), np.float32)
    u = np.arange(P)[:, None]
    v = np.arange(P)[None, :]
    c[:, C_ID:C_ID + P] = u == v
    c[:, C_LE:C_LE + P] = u <= v
    c[:, C_GT:C_GT + P] = u > v
    c[:, C_GE:C_GE + P] = u >= v
    c[:, C_LT:C_LT + P] = u < v
    c[:, C_ONE:C_ONE + P] = 1.0
    c[:, C_DRET:C_DRET + P] = SCALE * (1.0 + (u == v))
    q = GRID - 1 - np.arange(P)[:, None] % GRID
    c[:, C_FLIP:C_FLIP + P] = (v // GRID == u // GRID) & (v % GRID == q)
    k = np.arange(GRID)[None, :]
    first = np.clip(q - 8, 0, GRID - 16)
    c[:, C_MASK:C_MASK + GRID] = np.where((k >= first) & (k < first + 16), 0.0, NEG)
    inv = (1.0 / (10000.0 ** (np.arange(16, dtype=np.float32) / 16))).astype(np.float32)
    for n in range(2):
        t = np.arange(P) + n * P
        for axis, pos in enumerate((t // GRID, t % GRID)):
            ang = pos[:, None].astype(np.float32) * inv
            for half in range(2):
                at = n * 64 + axis * 32 + half * 16
                c[:, C_COS + at:C_COS + at + 16] = np.cos(ang)
                c[:, C_SIN + at:C_SIN + at + 16] = np.sin(ang) * (1 if half else -1)
    i = np.arange(4)
    c[:, C_TRI:C_TRI + 16] = (i[None, :] < i[:, None]).reshape(1, 16)
    c[:, C_IOTA:C_IOTA + P] = v
    c[:, C_TOK:C_TOK + 4] = u + P * i[None, :]
    c[:, C_EXP:C_EXP + NE] = CAP * np.arange(NE)
    return c


def trunk(nc, ins, out):
    x, ctx_in = ins["x"], ins["ctx"]
    es = ExitStack()
    with es:
        sems = {}

        def S(name):
            if name not in sems:
                sems[name] = es.enter_context(nc.semaphore(name))
            return sems[name]

        def per_layer(name, l):
            T = len(tiles(l))
            jobs = in_jobs(l)
            a, d = emptied(jobs, len(jobs))
            table = {
                "mod_pe": mod_units(l), "mod_row": mod_units(l), "in_pe": len(jobs), "in_act": a, "in_dve": d, "out_pe": N_OUT * T, "res_dve": N_OUT * T,
                "a_sq": NT, "a_hn": NT, "a_tr": KD, "a_evac": KD // 2, "a_evac_dve": KD // 2, "f_sq": T, "f_hn": T, "f_tr": KD, "f_evac": KD // 2, "f_evac_dve": KD // 2,
                "conv_dve": 6, "conv_act": 6, "x_tr": 5, "x_evac": 5, "ret_tr": NT, "ret_evac": NT, "rope": 2,
                "na_sq": NT, "na_ss": NT, "na_norm": NT, "naT_tr": NT, "naT_evac": NT,
                "rf_dve": T + 1, "rb_pool": T + 1, "seg_pe": T + 1, "e_act": T + 1,
                "vw_dve": 6, "st_pe": 6, "h_dve": 6, "mix_tr": KD, "mixT": KD,
                "diag0": len(segs(l)), "row0": len(segs(l)), "diag1": len(segs(l)), "row1": len(segs(l)),
                "ld_rowp": 16, "ld_bias": 16 * 2 * NA_H,
            }
            table.update(dict.fromkeys(("sc_pe", "sl_dve", "mret_dve", "v_pool", "y_pe", "comb_dve", "dx_pool", "yz_dve",
                                        "yss_act", "gn_ms", "gn_rs", "na_out", "ffn_dve"), T))
            table.update({"h_end0": T // 2, "h_end1": T // 2})
            table.update(dict.fromkeys(("mf_dve", "mb_pool", "diag_pe"), 2 * T))
            table.update(dict.fromkeys(("s_pe", "mx_dve", "p_act", "pt_pe", "pt_dve", "pv_pe"), NA_H * T))
            table.update({"turn_pe": KD, "turn_act": KD, "f_stored": 16, "chosen_dve": 1, "pos_pe": 1, "rounds_dve": 1})
            table.update(dict.fromkeys(("mod_turned", "mod_evac", "modA", "a_ms", "a_rs", "f_ms", "f_rs", "pad_zero", "na_ms", "na_rs",
                                        "dt_abs", "dt_ln", "nA_act", "loga", "cum_pe", "ex_act", "bias_dve", "row0_pe",
                                        "row1_pe", "rt_pe", "rt_act", "rt_tr", "acc_zero"), 1))
            return table[name]

        def upto(name, l, n):
            return n + sum(per_layer(name, m) for m in range(l))

        def sb(name, *shape):
            return es.enter_context(nc.sbuf_tensor(name, [P, *shape], F32))

        h = sb("h", NT, D)
        featT = sb("featT", KD, TOK)
        tokA = sb("tokA", NT, D)
        ring = sb("ring", 2, SLOT)
        const = sb("const", N_CONST)
        colp = sb("colp", DEPTH, N_COLP)
        condT = sb("condT", KD, 2)
        silT = sb("silT", KD, 2)
        mod = sb("mod", DEPTH, 48, 2)
        modA = sb("modA", DEPTH, 2, KD, 2)
        rw = sb("rw", KD, NE)
        rb = sb("rb", NE)
        stat = sb("stat", 64)
        stat2 = sb("stat2", 64)
        pw = sb("pw", 64)
        zero8 = sb("zero8", KD)
        slot_i = es.enter_context(nc.sbuf_tensor("slot_i", [P, 2], U32))
        rounds = es.enter_context(nc.sbuf_tensor("rounds", [P, DEPTH], I32))
        ARENA = 30368
        arena = sb("arena", ARENA)
        cursor = [0]

        def carve(*shape):
            n = int(np.prod(shape))
            at = cursor[0]
            cursor[0] += n
            assert cursor[0] <= ARENA
            v = arena[:, at:at + n]
            if len(shape) == 2:
                v = v.rearrange("p (a b) -> p a b", a=shape[0])
            elif len(shape) == 3:
                v = v.rearrange("p (a b c) -> p a b c", a=shape[0], b=shape[1])
            elif len(shape) == 4:
                v = v.rearrange("p (a b c d) -> p a b c d", a=shape[0], b=shape[1], c=shape[2])
            return v

        qk = carve(NT, 512)
        XV = carve(NT, NH * HD)
        at = cursor[0]
        nqk = carve(NT, 512)
        cursor[0] = at
        Mf = carve(2, 4, P)
        Mb = carve(2, 4, P)
        nav = carve(NT, 256)
        BCT = carve(2, TOK)
        Bt = carve(NT, P)
        retT = carve(4, TOK)
        naT = carve(4, TOK)
        at = cursor[0]
        xT = carve(4, TOK)
        cursor[0] = at
        rf = carve(SSD_H, P)
        rbk = carve(SSD_H, P)
        at = cursor[0]
        Hs = carve(2, NT, 384)
        cursor[0] = at
        xpad = carve(6, 2, CTX + 2)
        y = carve(NH, HD)
        y2 = carve(NH, HD)
        Pm = carve(2, 512)
        sq = Pm[:, 0, :]
        at_gate = cursor[0]
        E = carve(SSD_H, P)
        Eret = carve(RET_H, P)
        Mret = carve(RET_H, P)
        sU = carve(2, P)
        sL = carve(2, P)
        VW = carve(NH, HD)
        Vf = carve(SSD_H, HD)
        Vb = carve(SSD_H, HD)
        at = cursor[0]
        cursor[0] = at_gate
        diag = carve(2, D)
        grow = carve(2, D)
        assert cursor[0] <= at
        cursor[0] = at
        at = cursor[0]
        dx = carve(SSD_H, HD)
        cursor[0] = at
        PT = carve(2, 4, P)
        bias = carve(NA_H, 6, GRID)
        rowp = carve(N_ROWP)
        nA = carve(2, NH)
        dtr = carve(NT * 2, SSD_H)
        dta = carve(NT * 2, SSD_H)
        DTX = carve(NT * 2, NH)
        Aall = carve(NT * 2, NH)
        EX = carve(288)
        Wt = carve(2, NT, NH)
        Dec = carve(NT * 2, 6)
        rs = carve(NT, 8)
        nmx = carve(16)
        nsum = carve(16)
        nrec = carve(16)
        cursor[0] = 0
        slots = [ring[:, 0, :], ring[:, 1, :]] + [carve(SLOT) for _ in range(4)]
        hs = carve(FE)
        hp = carve(FE)
        hT = carve(4, P)
        onehot = carve(NT, P)
        owner = carve(2, P)
        Xg = carve(1, D)
        assert cursor[0] <= at_gate
        cursor[0] = at_gate + 4 * D
        XT = carve(2, KD, P)
        Yb = carve(2, D)
        gates = carve(NT, NE)
        aff = carve(NT, NE)
        sel = carve(NT * 4, 4)
        g1, g2, g3, g4 = (carve(NT, 4) for _ in range(4))
        cmp1 = XT[:, 0, 0:2, :].rearrange("p a (b c) -> p (a b) c", c=16)
        cmp2 = XT[:, 0, 2:4, :].rearrange("p a (b c) -> p (a b) c", c=16)
        chosen = carve(NT * 4, 4)
        rsum = carve(NT)
        place = carve(NT, NE)
        pick = carve(NT, NE)
        tmp16 = carve(NT, NE)
        pos2 = carve(2, NT)
        first2 = carve(2, NT)
        gate2 = carve(2, NT)
        row2 = carve(2, NT)
        inround = carve(2, NT)
        row_i = carve(2, NT).bitcast(U32)
        few = carve(4)
        gathered = [Xg[:, 0, :], diag[:, 0, :]]
        back = [gathered[0], diag[:, 1, :], Yb[:, 0, :], XT[:, 0, :, :].rearrange("p k c -> p (k c)")]

        affT = hs[0:NE, :]

        ps = es.enter_context(nc.psum_tensor("ps", [P, 8, 512], F32))
        ident = const[:, C_ID:C_ID + P]
        LE, GT, GE, LT, ONE = (const[:, c:c + P] for c in (C_LE, C_GT, C_GE, C_LT, C_ONE))

        def flat(bank, n):
            return ps[:, bank:bank + (n + 511) // 512, :].rearrange("p a b -> p (a b)")[:, 0:n]

        def scan_out(k, g, place, n=1):
            half = NH * HD // 2
            bank, c = divmod((half * g if k == 0 else 2 * half * (1 + g) + half * (k - 1)) + HD * place, 512)
            assert c + HD * n <= 512
            return ps[:, bank, c:c + HD * n]

        def scan_outs(k):
            all_ = flat(0, 3 * NH * HD)
            if k == 0:
                return all_[:, 0:NH * HD].rearrange("p (g h c) -> p g h c", g=2, h=6)
            return all_[:, NH * HD:].rearrange("p (g k h c) -> p g k h c", g=2, k=2, h=6)[:, :, k - 1, :, :]

        def heads(ap, n):
            return ap.rearrange("p (a b) -> p a b", a=n)

        def ssd(ap, n=1):
            return ap.rearrange("p (g c) -> p g c", g=2)[:, :, 0:4 * n]

        def ret(ap, n=1):
            return ap.rearrange("p (g c) -> p g c", g=2)[:, :, 4 * n:6 * n]

        def line(ap):
            return ap.rearrange("p a b -> p (a b)")

        def spread2(ap, n):
            return ap.unsqueeze(3).to_broadcast([P, 2, ap.shape[2], n])

        def triangle_rows(dst, a, m, tri):
            return (dst.rearrange("p (g h) c -> p g h c", g=2), spread2(a, P),
                    tri.unsqueeze(1).unsqueeze(1).to_broadcast([P, 2, m, P]))

        def spread(ap, n):
            return ap.unsqueeze(2).to_broadcast([P, ap.shape[1], n])

        def repeat(ap, n):
            return ap.unsqueeze(1).to_broadcast([P, n, ap.shape[1]])

        def tiles(l):
            return list(range(NT)) if l < DEPTH - 1 else [2, 3]

        def in_jobs(l):
            jobs = [("bc_dt", "f", 4, "A"), ("bc_dt", "f", 5, "A"), ("bc_dt", "dt", 0, "D")]
            jobs += [("x", "f", f, "A") for f in range(4)]
            jobs += [("ret_qk", "t", t, "D") for t in range(NT)]
            jobs += [("ret_vg", "t", t, "A") for t in range(NT)]
            jobs += [("z", "t", t, "A") for t in tiles(l)]
            jobs += [("na_qk", "t", t, "D") for t in range(NT)]
            jobs += [("na_v", "t", t, "D") for t in range(NT)]
            return jobs

        def emptied(jobs, upto):
            a = sum(j[3] == "A" for j in jobs[:upto])
            return a, upto - a

        def cols_needed(l, piece, t):
            full = l < DEPTH - 1 or t >= 2
            return {"ret_qk": (0 if full else 256, 512), "ret_vg": (0, 512 if full else 256),
                    "z": (0, 512), "na_qk": (0 if full else 256, 512), "na_v": (0, 256)}[piece]

        STATE_STEPS = ((0, 0), (1, 1), (0, 1), (1, 0), (0, 2), (1, 3))
        STATE_NEXT = {(0, 0): 1, (0, 1): 2, (0, 2): 3, (1, 1): 0, (1, 0): 3, (1, 3): 2}

        def dirs_of(t):
            return [d for d in (0, 1) if (d, t) not in ((0, 0), (1, 1))]

        def att_units(l):
            return [(t, hd) for t in tiles(l) for hd in range(NA_H)]

        def segs(l):
            return [0, 1] if l < DEPTH - 1 else [1]

        def dve_jobs_done(l, name, i):
            jobs = in_jobs(l)
            n = next(n for n, q in enumerate(jobs) if q[0] == name and q[2] == i and q[3] == "D")
            return emptied(jobs, n + 1)[1]

        N_FIRST = 4
        STREAMS = [[(0, n) for n in range(N_FIRST)]]
        for l in range(DEPTH):
            STREAMS.append([(l, n) for n in range(N_FIRST, N_MOD)]
                           + [(l + 1, n) for n in range(N_FIRST) if l + 1 < DEPTH])

        def mod_width(l):
            return 512 if l == 0 else P

        def mod_units(l):
            return len(STREAMS[l]) * 512 // mod_width(l)

        def mod_row(l, u):
            return ps[0:2, 6 + u % 2, :] if l == 0 else ps[0:2, 5, 0:P]

        def mod_lag(l):
            return 2 if l == 0 else 1

        def mod_copy(l, u):
            at = 512 * (u % 4)
            return featT.rearrange("p k c -> p (k c)")[0:2, at:at + mod_width(l)]

        def mod_columns(l):
            return ps[:, 5, 384:480]

        def mod_at(l, step, n, point=0):
            ns, na = len(STATE_STEPS) - 2, len(att_units(l - 1))
            per_point = 2
            first_att = ns + per_point * 3 * len(tiles(l - 1))
            if step == "state":
                return range(n - 2, n - 1) if n >= 2 else range(0)
            if step == "tile":
                at = ns + per_point * (3 * n + point)
                return range(at, at + per_point)
            left = mod_units(l) - first_att
            return range(first_att + left * n // na, first_att + left * (n + 1) // na)

        def static_pieces():
            p = []
            for l in range(DEPTH):
                if l == 0:
                    p += [("mod", *q) for q in STREAMS[0]]
                p += [("in", l, n) for n in range(len(IN_PIECES))]
                p += [("mod", *q) for q in STREAMS[l + 1]]
                p += [("out", l, n) for n in range(N_OUT)]
            return p

        def slot_of(piece):
            g = static_pieces().index(piece)
            return (2, 3, 4, 1)[g] if g < len(STREAMS[0]) else g % 2

        def stream_of(piece):
            return next(n for n, q in enumerate(STREAMS) if piece[1:] in q)

        def landed(piece):
            ps_ = static_pieces()
            return 16 * sum(slot_of(q) == slot_of(piece) for q in ps_[:ps_.index(piece) + 1])

        def use_of(piece):
            kind, l, n = piece
            if kind == "mod":
                st = stream_of(piece)
                return "mod_pe", st, (STREAMS[st].index((l, n)) + 1) * 512 // mod_width(st)
            if kind == "in":
                return "in_pe", l, 1 + max(i for i, j in enumerate(in_jobs(l)) if j[0] == IN_PIECES[n][0])
            return "out_pe", l, N_OUT * (len(tiles(l)) - 1) + n + 1

        def before(piece):
            ps_ = static_pieces()
            same = [q for q in ps_[:ps_.index(piece)] if slot_of(q) == slot_of(piece)]
            return same[-1] if same else None

        def sum_order(l):
            T = len(tiles(l))
            return [(n, t) for n in (1, 0) for t in range(T)]

        def backs(l, q, n_round):
            T = len(tiles(l))
            return (n_round * (2 * T // 4) + (q // 4 + 1)) * 16

        def X(name, l):
            return S(f"{name}_{l}")

        def job(r, i, c=0):
            return r * NE + (i * 2 + c)

        def load_rounds(eng, l):
            eng.wait_ge(S("rounds_dve"), upto("rounds_dve", l, 1))
            first = 0
            for m in range(l):
                first = first + eng.value_load(rounds[0:1, m:m + 1], min_val=1, max_val=len(tiles(m)))
            return first, eng.value_load(rounds[0:1, l:l + 1], min_val=1, max_val=len(tiles(l)))

        rows_in = [nc.dram_tensor(f"ffn_rows{l}", (P * len(tiles(l)), D), F32, kind="Internal").ap() for l in range(DEPTH)]
        rows_out = [nc.dram_tensor(f"expert_rows{l}", (NO_ROW + 1, D), F32, kind="Internal").ap() for l in range(DEPTH)]

        block = es.enter_context(nc.Block())

        @block.sync
        def _(sp):
            sp.dma_start(const[:, :], ins["consts"]).then_inc(S("ld_const"), 16)
            sp.dma_start(condT[:, :, :], ins["condT"]).then_inc(S("ld_cond"), 16)

            def load_tokens():
                sp.dma_start(h[:, 0:2, :], ctx_in.rearrange("(t p) d -> p t d", p=P)).then_inc(S("ld_h0"), 16)
                sp.dma_start(h[:, 2:4, :], x.rearrange("(t p) d -> p t d", p=P)).then_inc(S("ld_h1"), 16)

            def load_rest():
                sp.dma_start(rw[:, :, :], ins["router_w"].rearrange("(k p) e -> p k e", p=P)).then_inc(S("ld_rw"), 16)
                rbt = ins["router_b"]
                sp.dma_start(rb[:, :], bass.AP(rbt.tensor, 0, [[0, P], [1, NE]])).then_inc(S("ld_rb"), 16)

                for l in range(DEPTH):
                    sp.dma_start(colp[:, l, :], ins["colp"][l]).then_inc(S("ld_colp"), 16)

            def load_static(piece):
                kind, l, n = piece
                if kind == "mod":
                    src = ins["w_mod"][l, :, 512 * n:512 * (n + 1)]
                elif kind == "in":
                    _, c, w = IN_PIECES[n]
                    src = ins["w_in"][l, :, c:c + w]
                else:
                    src = ins["w_out"][l, :, 512 * n:512 * (n + 1)]
                k = slot_of(piece)
                dst = slots[k][:, 0:KD * src.shape[1]].rearrange("p (k c) -> p k c", k=KD)
                sp.dma_start(dst, src.rearrange("(k p) c -> p k c", p=P)).then_inc(S(f"piece{k}"), 16)

            def small(l):
                rp = ins["rowp"]
                sp.dma_start(rowp, bass.AP(rp.tensor, l * N_ROWP, [[0, P], [1, N_ROWP]])).then_inc(S("ld_rowp"), 16)
                rpb = ins["na_rpb"]
                for half, dr0 in ((0, 5), (1, 4)):
                    for hd in range(NA_H):
                        base = ((l * NA_H + hd) * 15 + dr0) * 31 + 15 - (GRID - 1)
                        sp.dma_start(bias[64 * half:64 * half + 64, hd, :, :],
                                     bass.AP(rpb.tensor, base, [[1, 64], [31, 6], [1, 64]])
                                     ).then_inc(S("ld_bias"), 16)

            for l in range(DEPTH):
                nt = len(tiles(l))
                mine = [q for q in static_pieces() if l == (max(stream_of(q) - 1, 0) if q[0] == "mod" else q[1])]
                if l > 0:
                    sp.wait_ge(S("up_pe"), (first + R) * NE)
                for m, piece in enumerate(mine):
                    if l > 0 and m == 2:
                        for w in ("h_end0", "h_end1"):
                            sp.wait_ge(S(w), upto(w, l - 1, len(tiles(l - 1)) // 2))
                        small(l)
                    if before(piece) is not None and not (l > 0 and m < 2):
                        name, ll, value = use_of(before(piece))
                        sp.wait_ge(S(name), upto(name, ll, value))
                    load_static(piece)
                    if l == 0 and m == 0:
                        load_tokens()
                    if l == 0 and m == len(STREAMS[0]) - 1:
                        load_rest()
                        small(l)

                def load_expert(e, c, j):
                    slot = 3 * c + j
                    src = (ins["w_gate"], ins["w_up"], ins["w_down"])[j]
                    k = 8 if j < 2 else 4
                    dst = slots[slot].rearrange("p (k c) -> p k c", k=k)
                    w = src[l, e] if isinstance(e, int) else src[l, bass.ds(e, 1)].rearrange("o r c -> (o r) c")
                    sp.dma_start(dst, w.rearrange("(k p) c -> p k c", p=P)).then_inc(S(f"slot{slot}"), 16)

                for n in range(N_OUT):
                    name, ll, value = use_of(("out", l, n))
                    sp.wait_ge(S(name), upto(name, ll, value))
                load_expert(0, 0, 0)
                load_expert(0, 0, 1)
                sp.wait_ge(S("na_out"), upto("na_out", l, nt))
                load_expert(0, 0, 2)
                sp.wait_ge(S("zero_pool"), 1)
                sp.dma_start(rows_out[l][NO_ROW:NO_ROW + 1, :].rearrange("o (p c) -> (o p) c", p=P), zero8[:, :]
                             ).then_inc(X("no_row", l), 16)
                first, R = load_rounds(sp, l)
                for c in range(2):
                    sp.wait_ge(S(f"gathered{c}"), first * (NE // 2 * 16) + 16)
                for j in range(3):
                    load_expert(1, 1, j)
                with sp.Fori(first * (NE // 2) + 1, (first + R) * (NE // 2)) as i:
                    for c in range(2):
                        sp.wait_ge(S("up_pe"), job(0, i, c - 1))
                        load_expert((i % (NE // 2)) * 2 + c, c, 0)
                        load_expert((i % (NE // 2)) * 2 + c, c, 1)
                        sp.wait_ge(S("dn_pe"), job(0, i, c - 1))
                        load_expert((i % (NE // 2)) * 2 + c, c, 2)
            for l in range(DEPTH):
                sp.wait_ge(X("no_row", l), 16)
            for t in range(2):
                w = ("h_end0", "h_end1")[t]
                sp.wait_ge(S(w), upto(w, DEPTH - 1, 1))
                sp.dma_start(out[P * t:P * t + P, :], h[:, 2 + t, :]).then_inc(S("stored"), 16)
            sp.wait_ge(S("stored"), 32)

        @block.tensor
        def _(pe):
            mm = nc.tensor.matmul
            tr = nc.tensor.transpose
            pe.wait_ge(S("ld_const"), 16)

            def piece(q, w=512):
                return slots[slot_of(q)][:, 0:KD * w].rearrange("p (k c) -> p k c", k=KD)

            def turn_mod(l, u):
                w = mod_width(l)
                for f in range(w // P):
                    c = 2 * (u * w // P + f)
                    i = tr(mod_columns(l)[:, c:c + 2], mod_copy(l, u)[:, P * f:P * f + P], ident[0:2, 0:2])
                return i

            def mod_unit(l, u):
                n, c = divmod(u * mod_width(l), 512)
                q = ("mod", *STREAMS[l][n])
                if c == 0:
                    pe.wait_ge(S(f"piece{slot_of(q)}"), landed(q))
                if u >= mod_lag(l):
                    pe.wait_ge(S("mod_row"), upto("mod_row", l, u - mod_lag(l) + 1))
                    turn_mod(l, u - mod_lag(l))
                for k in range(KD):
                    i = mm(mod_row(l, u), silT[:, k, :], piece(q)[:, k, c:c + mod_width(l)],
                           start=k == 0, stop=k == KD - 1)
                i.then_inc(S("mod_pe"), 1)

            def mod_end(l):
                n = mod_units(l)
                pe.wait_ge(S("mod_row"), upto("mod_row", l, n))
                for u in range(n - mod_lag(l), n):
                    i = turn_mod(l, u)
                i.then_inc(S("mod_turned"), 1)

            def modulation(l):
                pe.wait_ge(S("sil"), 1)
                for u in range(mod_units(l)):
                    mod_unit(l, u)
                    if u == 1:
                        norm_transpose(l, "a", range(NT), range(4))
                mod_end(l)

            def norm_transpose(l, which, ts, blocks=range(KD)):
                pe.wait_ge(S(which + "_hn"), upto(which + "_hn", l, len(ts)))
                if which == "f":
                    pe.wait_ge(S("row1"), upto("row1", l, len(segs(l))))
                for k in blocks:
                    if k >= 4:
                        name = which + ("_evac" if k % 2 == 0 else "_evac_dve")
                        pe.wait_ge(S(name), upto(name, l, (k - 4) // 2 + 1))
                    for j, t in enumerate(ts):
                        i = tr(ps[:, 1 + k % 4, P * t:P * t + P], tokA[:, t, P * k:P * k + P], ident)
                    i.then_inc(S(which + "_tr"), 1)

            def project(l):
                jobs = in_jobs(l)
                pe.wait_ge(S("a_evac"), upto("a_evac", l, KD // 2))
                pe.wait_ge(S("a_evac_dve"), upto("a_evac_dve", l, KD // 2))
                for n, (name, kind, i, _) in enumerate(jobs):
                    p = [q[0] for q in IN_PIECES].index(name)
                    w = IN_PIECES[p][2]
                    W = piece(("in", l, p), w)
                    if n == 0 or jobs[n - 1][0] != name:
                        pe.wait_ge(S(f"piece{slot_of(('in', l, p))}"), landed(("in", l, p)))
                    if n >= 4:
                        a, d = emptied(jobs, n - 3)
                        pe.wait_ge(S("in_act"), upto("in_act", l, a))
                        if d:
                            pe.wait_ge(S("in_dve"), upto("in_dve", l, d))
                    bank = ps[:, n % 4, :]
                    if kind == "f":
                        c = P * (i % 4)
                        lo = 0 if (l < DEPTH - 1 or i != 5) else CTX
                        for k in range(KD):
                            o = mm(bank[:, lo:TOK], W[:, k, c:c + P], featT[:, k, lo:TOK],
                                   start=k == 0, stop=k == KD - 1)
                    elif kind == "dt":
                        for t in range(NT):
                            for k in range(KD):
                                o = mm(bank[:, 16 * t:16 * t + 16], featT[:, k, P * t:P * t + P], W[:, k, 256:272],
                                       start=k == 0, stop=k == KD - 1)
                    else:
                        lo, hi = cols_needed(l, name, i)
                        for k in range(KD):
                            o = mm(bank[:, lo:hi], featT[:, k, P * i:P * i + P], W[:, k, lo:hi],
                                   start=k == 0, stop=k == KD - 1)
                    o.then_inc(S("in_pe"), 1)
                    if (name, i) == ("na_qk", 1):
                        turn_scan_operands(l)
                    if (name, i) == ("na_v", 0):
                        decay_sums(l)

            def turn_scan_operands(l):
                pe.wait_ge(S("in_dve"), upto("in_dve", l, dve_jobs_done(l, "ret_qk", NT - 1)))
                for n, f in enumerate((4, 0, 1, 2, 3)):
                    pe.wait_ge(S("conv_act"), upto("conv_act", l, {4: 1, 5: 2}.get(f, f + 3)))
                    if n >= 2:
                        pe.wait_ge(S("x_evac"), upto("x_evac", l, n - 1))
                    src = BCT[:, 0, :] if f == 4 else xT[:, f, :]
                    for t in range(NT):
                        i = tr(ps[:, 4 + n % 2, P * t:P * t + P], src[:, P * t:P * t + P], ident)
                    i.then_inc(S("x_tr"), 1)
                for t in range(NT):
                    full = t in tiles(l)
                    if t >= 2:
                        pe.wait_ge(S("rope"), upto("rope", l, t - 1))
                        pe.wait_ge(S("ret_evac"), upto("ret_evac", l, t - 1))
                    for b in range(0 if full else 2, 4):
                        i = tr(ps[:, 6 + t % 2, P * b:P * b + P], qk[:, t, P * b:P * b + P], ident)
                    i.then_inc(S("ret_tr"), 1)

            def turn_na_operands(l):
                jobs = in_jobs(l)
                pe.wait_ge(S("in_dve"), upto("in_dve", l, emptied(jobs, len(jobs))[1]))
                for t in range(NT):
                    full = t in tiles(l)
                    pe.wait_ge(S("na_norm"), upto("na_norm", l, t + 1))
                    if t >= 2:
                        pe.wait_ge(S("naT_evac"), upto("naT_evac", l, t - 1))
                    for b in range(0 if full else 2, 4):
                        i = tr(ps[:, t % 2, P * b:P * b + P], nqk[:, t, P * b:P * b + P], ident)
                    i.then_inc(S("naT_tr"), 1)

            def decay_sums(l):
                pe.wait_ge(S("loga"), upto("loga", l, 1))
                f, b = Aall[:, 0:NT * 2:2, :], Aall[:, 1:NT * 2:2, :]
                pe.wait_ge(S("x_evac"), upto("x_evac", l, 5))
                for n, (tri, a) in enumerate(((LE, f), (GE, b), (GT, f), (LT, b))):
                    mm(ps[:, 4, 48 * n:48 * n + 48], tri, a, start=True, stop=True)
                mm(ps[:, 4, 192:288], ONE, Aall[:, :, :], start=True, stop=True).then_inc(S("cum_pe"), 1)

            def states(l):
                pe.wait_ge(S("x_evac"), upto("x_evac", l, 5))
                pe.wait_ge(S("ret_evac"), upto("ret_evac", l, NT))
                for n, (d, t) in enumerate(STATE_STEPS):
                    pe.wait_ge(S("vw_dve"), upto("vw_dve", l, n + 1))
                    if n >= 2:
                        pe.wait_ge(S("h_dve"), upto("h_dve", l, n - 1))
                    bank = ps[:, 3 + n % 2, :]
                    for g in range(2):
                        mm(bank[64 * g:64 * g + 64, 0:256], Bt[:, t, 64 * g:64 * g + 64],
                           VW[:, 6 * g:6 * g + 4, :], start=True, stop=True)
                    for r in range(RET_H):
                        i = mm(bank[64 * (r % 2):64 * (r % 2) + 64, 256 + 64 * (r // 2):320 + 64 * (r // 2)],
                               qk[:, t, 256 + 64 * r:320 + 64 * r], VW[:, 6 * (r % 2) + 4 + r // 2, :],
                               start=True, stop=True)
                    i.then_inc(S("st_pe"), 1)
                    for u in mod_at(l + 1, "state", n):
                        mod_unit(l + 1, u)

            def scan_tile(l, n, t):
                pe.wait_ge(S("rf_dve"), upto("rf_dve", l, n + 2))
                pe.wait_ge(S("rb_pool"), upto("rb_pool", l, n + 2))
                if n > 0:
                    pe.wait_ge(S("mret_dve"), upto("mret_dve", l, n))
                else:
                    pe.wait_ge(S("e_act"), upto("e_act", l, 1))
                for hf in range(2):
                    mm(ps[:, 6 + hf, :], GT, rf[:, 4 * hf:4 * hf + 4, :], start=True, stop=False)
                    i = mm(ps[:, 6 + hf, :], LT, rbk[:, 4 * hf:4 * hf + 4, :], start=False, stop=True)
                i.then_inc(S("seg_pe"), 1)
                for u in mod_at(l + 1, "tile", n, 0):
                    mod_unit(l + 1, u)
                pe.wait_ge(S("e_act"), upto("e_act", l, n + 2))
                c = slice(P * t, P * t + P)
                for g in range(2):
                    s = slice(64 * g, 64 * g + 64)
                    mm(ps[:, 6 + g, 0:P], BCT[s, 0, c], BCT[s, 1, c], start=True, stop=True)
                for r in range(RET_H):
                    s = slice(64 * (r % 2), 64 * (r % 2) + 64)
                    o = P * (1 + r // 2)
                    i = mm(ps[:, 6 + r % 2, o:o + P], retT[s, 2 + r // 2, c], retT[s, r // 2, c],
                           start=True, stop=True)
                i.then_inc(S("sc_pe"), 1)
                if n > 0:
                    pe.wait_ge(S("comb_dve"), upto("comb_dve", l, n))
                else:
                    pe.wait_ge(S("naT_evac"), upto("naT_evac", l, NT))
                for d in dirs_of(t):
                    pe.wait_ge(S("h_dve"), upto("h_dve", l, 6))
                    for g in range(2):
                        s = slice(64 * g, 64 * g + 64)
                        for place in (0, 2):
                            mm(scan_out(1 + d, g, place, 2), BCT[s, 1, c], Hs[s, d, t, HD * place:HD * (place + 2)],
                               start=True, stop=True)
                    for r in range(RET_H):
                        s = slice(64 * (r % 2), 64 * (r % 2) + 64)
                        mm(scan_out(1 + d, r % 2, 4 + r // 2), retT[s, r // 2, c],
                           Hs[s, d, t, 256 + 64 * (r // 2):320 + 64 * (r // 2)], start=True, stop=True)
                for u in mod_at(l + 1, "tile", n, 1):
                    mod_unit(l + 1, u)
                pe.wait_ge(S("v_pool"), upto("v_pool", l, n + 1))
                for g in range(2):
                    pe.wait_ge(S("mf_dve"), upto("mf_dve", l, 2 * n + g + 1))
                    pe.wait_ge(S("mb_pool"), upto("mb_pool", l, 2 * n + g + 1))
                    for j in range(4):
                        hd = 4 * g + j
                        o = scan_out(0, g, j)
                        mm(o, Mf[:, g, j, :], Vf[:, hd, :], start=True, stop=False)
                        i = mm(o, Mb[:, g, j, :], Vb[:, hd, :], start=False, stop=True)
                    i.then_inc(S("diag_pe"), 1)
                pe.wait_ge(S("mret_dve"), upto("mret_dve", l, n + 1))
                for r in range(RET_H):
                    g, o = r // 2, 256 + 64 * (r % 2)
                    i = mm(scan_out(0, g, 4 + r % 2), Mret[:, r, :], XV[:, t, 384 * g + o:384 * g + o + 64],
                           start=True, stop=True)
                i.then_inc(S("y_pe"), 1)
                for u in mod_at(l + 1, "tile", n, 2):
                    mod_unit(l + 1, u)

            def scan(l):
                pe.wait_ge(S("ret_evac"), upto("ret_evac", l, NT))
                pe.wait_ge(S("rf_dve"), upto("rf_dve", l, 1))
                pe.wait_ge(S("rb_pool"), upto("rb_pool", l, 1))
                mm(ps[:, 6, :], GT, rf[:, 0:4, :], start=True, stop=False)
                mm(ps[:, 6, :], LT, rbk[:, 0:4, :], start=False, stop=True).then_inc(S("seg_pe"), 1)
                states(l)
                for n, t in enumerate(tiles(l)):
                    scan_tile(l, n, t)

            def attention(l):
                un = att_units(l)
                pe.wait_ge(S("comb_dve"), upto("comb_dve", l, len(tiles(l))))

                def scores(n):
                    t, hd = un[n]
                    s = slice(64 * (hd % 2), 64 * (hd % 2) + 64)
                    keys = TOK if t >= 2 else CTX
                    if n >= 2:
                        pe.wait_ge(S("p_act"), upto("p_act", l, n - 1))
                    lat = t >= 2
                    i = mm(ps[:, n % 2, 0:keys], naT[s, hd // 2, P * t:P * t + P], naT[s, 2 + hd // 2, 0:keys],
                           start=True, stop=not lat)
                    if lat:
                        j = 2 - 2 * (t - 2)
                        pe.wait_ge(S("bias_dve"), upto("bias_dve", l, 1))
                        i = mm(ps[:, n % 2, CTX:TOK], const[:, C_FLIP:C_FLIP + P], bias[:, hd, j:j + 4, :], start=False, stop=True)
                    i.then_inc(S("s_pe"), 1)

                def turn(n):
                    t, hd = un[n]
                    nk = NT if t >= 2 else 2
                    pe.wait_ge(S("p_act"), upto("p_act", l, n + 1))
                    if n >= 2:
                        pe.wait_ge(S("pt_dve"), upto("pt_dve", l, n - 1))
                    for b in range(nk):
                        i = tr(ps[:, 2 + n % 2, P * b:P * b + P], Pm[:, n % 2, P * b:P * b + P], ident)
                    i.then_inc(S("pt_pe"), 1)

                def values(n):
                    t, hd = un[n]
                    nk = NT if t >= 2 else 2
                    pe.wait_ge(S("pt_dve"), upto("pt_dve", l, n + 1))
                    tile = n // NA_H
                    if n % NA_H == 0 and tile >= 2:
                        pe.wait_ge(S("na_out"), upto("na_out", l, tile - 1))
                    for b in range(nk):
                        i = mm(ps[:, 4 + 2 * (tile % 2), 64 * hd:64 * hd + 64], PT[:, n % 2, b, :],
                               nav[:, b, 64 * hd:64 * hd + 64], start=b == 0, stop=b == nk - 1)
                    i.then_inc(S("pv_pe"), 1)

                N = len(un)
                scores(0)
                for n in range(N):
                    if n + 1 < N:
                        scores(n + 1)
                    if n >= 1:
                        values(n - 1)
                    for u in mod_at(l + 1, "unit", n):
                        mod_unit(l + 1, u)
                    turn(n)
                values(N - 1)
                mod_end(l + 1)

            def output(l):
                ts = tiles(l)
                pe.wait_ge(S("na_out"), upto("na_out", l, len(ts)))
                for k in range(KD):
                    if k >= 2:
                        pe.wait_ge(S("mixT"), upto("mixT", l, k - 1))
                    for t in ts:
                        i = tr(ps[:, 6 + k % 2, P * t:P * t + P], tokA[:, t, P * k:P * k + P], ident)
                    i.then_inc(S("mix_tr"), 1)
                gate_rows(l, 0)
                pe.wait_ge(S("mixT"), upto("mixT", l, KD))
                pe.wait_ge(S("mod_evac"), upto("mod_evac", l + 1, 1))
                n = 0
                for half in range(N_OUT):
                    p = ("out", l, half)
                    pe.wait_ge(S(f"piece{slot_of(p)}"), landed(p))
                for t in ts:
                    for half in range(N_OUT):
                        p = ("out", l, half)
                        if n >= 2:
                            pe.wait_ge(S("res_dve"), upto("res_dve", l, n - 1))
                        for k in range(KD):
                            i = mm(ps[:, 4 + n % 2, :], featT[:, k, P * t:P * t + P], piece(p)[:, k, :],
                                   start=k == 0, stop=k == KD - 1)
                        i.then_inc(S("out_pe"), 1)
                        n += 1

            def gate_rows(l, which):
                pe.wait_ge(S(f"diag{which}"), upto(f"diag{which}", l, len(segs(l))))
                if which == 1:
                    pe.wait_ge(S("row0"), upto("row0", l, len(segs(l))))
                for seg in segs(l):
                    for hf in range(2):
                        i = mm(ps[:, 2 * seg + hf, :], ONE, diag[:, seg, 512 * hf:512 * hf + 512],
                               start=True, stop=True)
                i.then_inc(S(f"row{which}_pe"), 1)

            def router(l):
                ts = tiles(l)
                pe.wait_ge(S("f_evac"), upto("f_evac", l, KD // 2))
                pe.wait_ge(S("f_evac_dve"), upto("f_evac_dve", l, KD // 2))
                pe.wait_ge(S("ld_rw"), 16)
                pe.wait_ge(S("row1"), upto("row1", l, len(segs(l))))
                for k in range(KD):
                    i = mm(ps[0:NE, 0, P * ts[0]:TOK], rw[:, k, :], featT[:, k, P * ts[0]:TOK],
                           start=k == 0, stop=k == KD - 1)
                i.then_inc(S("rt_pe"), 1)

            def turn_affinities(l):
                pe.wait_ge(S("rt_act"), upto("rt_act", l, 1))
                for t in tiles(l):
                    i = tr(ps[:, 1, NE * t:NE * t + NE], affT[:, P * t:P * t + P], ident[0:NE, 0:NE])
                i.then_inc(S("rt_tr"), 1)

            def turn_back(l):
                for k in range(KD):
                    if k == 4:
                        turn_affinities(l)
                    if k >= 4:
                        pe.wait_ge(S("turn_act"), upto("turn_act", l, k - 3))
                    for t in tiles(l):
                        i = tr(ps[:, 4 + k % 4, P * t:P * t + P], featT[:, k, P * t:P * t + P], ident)
                    i.then_inc(S("turn_pe"), 1)

            def places(l):
                pe.wait_ge(S("chosen_dve"), upto("chosen_dve", l, 1))
                n = NE * len(tiles(l))
                mm(ps[:, 3, 0:n], LT, chosen[:, 0:4 * len(tiles(l)), :], start=True, stop=True)
                mm(ps[:, 2, 0:n], ONE, chosen[:, 0:4 * len(tiles(l)), :], start=True, stop=True).then_inc(S("pos_pe"), 1)

            def experts(l):
                ts = tiles(l)
                T = len(ts)
                first, R = load_rounds(pe, l)

                def who(r, i, c):
                    pe.wait_ge(S("onehot_dve"), job(r, i, c) + 1)
                    if not (isinstance(i, int) and 2 * i + c == 0):
                        pe.wait_ge(S("who_dve"), job(r, i, c))
                    o = mm(ps[:, 7, 0:1], owner[:, c % 2, :], ONE[:, 0:1], start=True, stop=True)
                    o.then_inc(S("who_pe"), 1)

                def turn_x(r, i, c):
                    pe.wait_ge(S(f"gathered{c % 2}"), (r * (NE // 2) + (i + c // 2) + 1) * 16)
                    if not (isinstance(i, int) and 2 * i + c == 0):
                        pe.wait_ge(S("xT_act"), job(r, i, c))
                    for k in range(KD):
                        o = tr(ps[:, 5 + k // 4, P * (k % 4):P * (k % 4) + P], gathered[c % 2][:, P * k:P * k + P], ident)
                    o.then_inc(S("xT_pe"), 1)

                def wide(r, i, c, m):
                    pe.wait_ge(S("xT_act"), job(r, i, c) + 1)
                    if not (isinstance(i, int) and 2 * i + c == 0):
                        pe.wait_ge(S(("hs_act", "hp_dve")[m]), job(r, i, c))
                    pe.wait_ge(S(f"slot{3 * c + m}"), (r * (NE // 2) + i + 1) * 16)
                    W = slots[3 * c + m].rearrange("p (k c) -> p k c", k=KD)
                    for k in range(KD):
                        o = mm(ps[:, m, :], XT[:, c, k, :], W[:, k, :], start=k == 0, stop=k == KD - 1)
                    o.then_inc(S(("gate_pe", "up_pe")[m]), 1)

                def turn_h(r, i, c):
                    pe.wait_ge(S("hp_dve"), job(r, i, c) + 1)
                    if not (isinstance(i, int) and 2 * i + c == 0):
                        pe.wait_ge(S("hT_act"), job(r, i, c))
                    for b in range(4):
                        o = tr(ps[:, 2, P * b:P * b + P], hp[:, P * b:P * b + P], ident)
                    o.then_inc(S("hT_pe"), 1)

                def down(r, i, c):
                    pe.wait_ge(S("hT_act"), job(r, i, c) + 1)
                    pe.wait_ge(S(f"slot{3 * (c % 2) + 2}"), (r * (NE // 2) + (i + 1 - (c < 0))) * 16)
                    if not (isinstance(i, int) and 2 * i + c == 0):
                        pe.wait_ge(S("y_dve"), job(r, i, c))
                    W = slots[3 * (c % 2) + 2].rearrange("p (k c) -> p k c", k=4)
                    for hf in range(2):
                        for k in range(4):
                            o = mm(ps[:, 3 + hf, :], hT[:, k, :], W[:, k, 512 * hf:512 * hf + 512],
                                   start=k == 0, stop=k == 3)
                    o.then_inc(S("dn_pe"), 1)

                def pair(r, i, first, last):
                    for c in range(2):
                        wide(r, i, c, 0)
                        if not (first and c == 0):
                            turn_h(r, i, c - 1)
                        wide(r, i, c, 1)
                        if not (last and c == 1):
                            turn_x(r, i, c + 1)
                        if not last:
                            who(r, i, c + 2)
                        if not (first and c == 0):
                            down(r, i, c - 1)

                pe.wait_ge(S("row1"), upto("row1", l, len(segs(l))))
                pe.wait_ge(S("turn_act"), upto("turn_act", l, KD))
                with pe.Fori(0, R) as n_round:
                    r = n_round + first
                    pe.wait_ge(S("round_dve"), r + 1)
                    who(r, 0, 0)
                    who(r, 0, 1)
                    turn_x(r, 0, 0)
                    pair(r, 0, True, False)
                    with pe.Fori(1, NE // 2 - 1) as i:
                        pair(r, i, False, False)
                    pair(r, NE // 2 - 1, False, True)
                    turn_h(r, NE // 2 - 1, 1)
                    down(r, NE // 2 - 1, 1)

            modulation(0)
            for l in range(DEPTH):
                norm_transpose(l, "a", range(NT), range(4 if l == 0 else 0, KD))
                project(l)
                turn_na_operands(l)
                scan(l)
                attention(l)
                output(l)
                gate_rows(l, 1)
                norm_transpose(l, "f", tiles(l))
                router(l)
                turn_back(l)
                places(l)
                experts(l)

        @block.scalar
        def _(act):
            A = nc.scalar.activation
            chain = [0]

            def link(ins):
                chain[0] += 1
                ins.then_inc(S("act_chain"), 1)
                act.wait_ge(S("act_chain"), chain[0])

            act.wait_ge(S("ld_cond"), 16)
            A(silT[:, :, :], condT[:, :, :], ACT.Silu).then_inc(S("sil"), 1)

            def mod_rows(l, units):
                for u in units:
                    act.wait_ge(S("mod_pe"), upto("mod_pe", l, u + 1))
                    A(mod_copy(l, u), mod_row(l, u), ACT.Identity).then_inc(S("mod_row"), 1)

            def square_rows(l, which, ts):
                for t in ts:
                    if which == "a" and l > 0:
                        w = ("h_end0", "h_end1")[t % 2]
                        act.wait_ge(S(w), upto(w, l - 1, t // 2 + 1))
                    elif which == "f":
                        act.wait_ge(S("res_dve"), upto("res_dve", l, N_OUT * (t - ts[0] + 1)))
                    A(tokA[:, t, :], h[:, t, :], ACT.Square, accum_out=stat[:, t:t + 1]).then_inc(S(which + "_sq"), 1)

            def norm_evac(l, which, ts):
                m = 0 if which == "a" else 1
                act.wait_ge(S("modA"), upto("modA", l + m, 1))
                for k in range(0, KD, 2):
                    act.wait_ge(S(which + "_tr"), upto(which + "_tr", l, k + 1))
                    for seg in (segs(l) if which == 'f' else [0, 1]):
                        c = slice(CTX * seg, CTX * seg + CTX)
                        i = A(featT[:, k, c], ps[:, 1 + k % 4, c], ACT.Identity,
                              scale=modA[:, l, m, k, seg:seg + 1], bias=mod[:, l, 24 * m + k, seg:seg + 1])
                    i.then_inc(S(which + "_evac"), 1)

            def project(l):
                jobs = in_jobs(l)
                act.wait_ge(S("pad_zero"), upto("pad_zero", l, 1))
                for n, (name, kind, i, eng) in enumerate(jobs):
                    if eng != "A":
                        continue
                    act.wait_ge(S("in_pe"), upto("in_pe", l, n + 1))
                    bank = ps[:, n % 4, :]
                    if kind == "f":
                        if l < DEPTH - 1 or i != 5:
                            A(xpad[:, i, :, 1:CTX + 1], heads(bank, 2), ACT.Identity).then_inc(S("in_act"), 1)
                        else:
                            A(xpad[:, i, 1, 1:CTX + 1], bank[:, CTX:TOK], ACT.Identity).then_inc(S("in_act"), 1)
                    elif name == "ret_vg":
                        o = A(ret(XV[:, i, :], HD).rearrange("p g (j c) -> p j g c", j=2),
                              bank[:, 0:256].rearrange("p (j g c) -> p j g c", j=2, g=2), ACT.Identity)
                        if i in tiles(l):
                            o = A(tokA[:, i, 0:256], bank[:, 256:512], ACT.Silu)
                        o.then_inc(S("in_act"), 1)
                    else:
                        A(tokA[:, i, 256:768], bank, ACT.Silu).then_inc(S("in_act"), 1)
                for n, f in enumerate((4, 5, 0, 1, 2, 3)):
                    act.wait_ge(S("conv_dve"), upto("conv_dve", l, n + 1))
                    dst = xT[:, f, :] if f < 4 else BCT[:, f - 4, :]
                    if f == 5 and l == DEPTH - 1:
                        dst = dst[:, CTX:TOK]
                    A(dst, dst, ACT.Silu).then_inc(S("conv_act"), 1)

            def na_norm(l):
                for t in range(NT):
                    lo = 0 if t in tiles(l) else 256
                    act.wait_ge(S("in_dve"), upto("in_dve", l, dve_jobs_done(l, "na_qk", t)))
                    if t > 0:
                        act.wait_ge(S("na_ss"), upto("na_ss", l, t))
                    A(sq[:, lo:512], nqk[:, t, lo:512], ACT.Square).then_inc(S("na_sq"), 1)

            def turn_scan_operands(l):
                for n, f in enumerate((4, 0, 1, 2, 3)):
                    act.wait_ge(S("x_tr"), upto("x_tr", l, n + 1))
                    src = heads(ps[:, 4 + n % 2, :], NT)
                    c = P * f + P * (f // 2)
                    dst = Bt[:, :, :] if f == 4 else XV[:, :, c:c + P]
                    A(dst, src, ACT.Identity).then_inc(S("x_evac"), 1)
                for t in range(NT):
                    lo = 0 if t in tiles(l) else 2
                    act.wait_ge(S("ret_tr"), upto("ret_tr", l, t + 1))
                    A(retT[:, lo:4, P * t:P * t + P], heads(ps[:, 6 + t % 2, :], 4)[:, lo:4, :],
                      ACT.Identity).then_inc(S("ret_evac"), 1)

            def turn_na_operands(l):
                for t in range(NT):
                    lo = 0 if t in tiles(l) else 2
                    act.wait_ge(S("naT_tr"), upto("naT_tr", l, t + 1))
                    A(naT[:, lo:4, P * t:P * t + P], heads(ps[:, t % 2, :], 4)[:, lo:4, :],
                      ACT.Identity).then_inc(S("naT_evac"), 1)

            def softplus(l):
                act.wait_ge(S("ld_rowp"), upto("ld_rowp", l, 16))
                A(nA[:, :, :], heads(rowp[:, R_DEC:R_DEC + 24], 2), ACT.Exp).then_inc(S("nA_act"), 1)
                act.wait_ge(S("dt_abs"), upto("dt_abs", l, 1))
                link(A(dta[:, :, :], dta[:, :, :], ACT.Exp, scale=-1.0))
                A(dta[:, :, :], dta[:, :, :], ACT.Ln, bias=1.0).then_inc(S("dt_ln"), 1)

            def scan(l):
                act.wait_ge(S("cum_pe"), upto("cum_pe", l, 1))
                A(EX, ps[:, 4, 0:288], ACT.Exp).then_inc(S("ex_act"), 1)
                turn_na_operands(l)
                act.wait_ge(S("seg_pe"), upto("seg_pe", l, 1))
                A(Eret[:, :, :], heads(ps[:, 6, :], 4), ACT.Exp).then_inc(S("e_act"), 1)
                for n in range(len(STATE_STEPS)):
                    mod_rows(l + 1, mod_at(l + 1, "state", n))

                def decays(n):
                    act.wait_ge(S("seg_pe"), upto("seg_pe", l, n + 2))
                    if n > 0:
                        act.wait_ge(S("mf_dve"), upto("mf_dve", l, 2 * n))
                        act.wait_ge(S("mb_pool"), upto("mb_pool", l, 2 * n))
                    A(E[:, :, :], heads(flat(6, 1024), SSD_H), ACT.Exp).then_inc(S("e_act"), 1)

                ts = tiles(l)
                decays(0)
                for point in range(3):
                    mod_rows(l + 1, mod_at(l + 1, "tile", 0, point))
                for n in range(len(ts)):
                    if n + 1 < len(ts):
                        decays(n + 1)
                        mod_rows(l + 1, mod_at(l + 1, "tile", n + 1, 0))
                    act.wait_ge(S("yz_dve"), upto("yz_dve", l, n + 1))
                    A(heads(sq, 2), ssd(line(y2), HD), ACT.Square,
                      accum_out=stat[:, 8 + n:9 + n]).then_inc(S("yss_act"), 1)
                    if n + 1 < len(ts):
                        for point in (1, 2):
                            mod_rows(l + 1, mod_at(l + 1, "tile", n + 1, point))

            def attention(l):
                for n, (t, hd) in enumerate(att_units(l)):
                    keys = TOK if t >= 2 else CTX
                    act.wait_ge(S("mx_dve"), upto("mx_dve", l, n + 1))
                    if n >= 2:
                        act.wait_ge(S("pt_pe"), upto("pt_pe", l, n - 1))
                    A(Pm[:, n % 2, 0:keys], ps[:, n % 2, 0:keys], ACT.Exp, bias=nmx[:, n:n + 1],
                      accum_out=nsum[:, n:n + 1]).then_inc(S("p_act"), 1)
                    mod_rows(l + 1, mod_at(l + 1, "unit", n))

            def mixT(l):
                ts = tiles(l)
                lo, hi = P * ts[0], P * ts[-1] + P
                for k in range(KD):
                    act.wait_ge(S("mix_tr"), upto("mix_tr", l, k + 1))
                    A(featT[:, k, lo:hi], ps[:, 6 + k % 2, lo:hi], ACT.Identity).then_inc(S("mixT"), 1)

            def gate_rows(l, which):
                act.wait_ge(S(f"row{which}_pe"), upto(f"row{which}_pe", l, 1))
                for seg in segs(l):
                    A(grow[:, seg, :], flat(2 * seg, 1024), ACT.Identity).then_inc(S(f"row{which}"), 1)

            def affinities(l):
                ts = tiles(l)
                act.wait_ge(S("rt_pe"), upto("rt_pe", l, 1))
                A(affT[:, P * ts[0]:TOK], ps[0:NE, 0, P * ts[0]:TOK], ACT.Sigmoid).then_inc(S("rt_act"), 1)

            def turn_back(l):
                ts = tiles(l)
                act.wait_ge(S("f_tr"), upto("f_tr", l, KD))
                for k in range(KD):
                    act.wait_ge(S("turn_pe"), upto("turn_pe", l, k + 1))
                    A(tokA[:, ts[0]:NT, P * k:P * k + P], heads(ps[:, 4 + k % 4, :], NT)[:, ts[0]:NT, :],
                      ACT.Identity).then_inc(S("turn_act"), 1)
                act.wait_ge(S("turn_act"), upto("turn_act", l, KD))
                act.dma_start(rows_in[l].rearrange("(t p) d -> p t d", p=P), tokA[:, ts[0]:NT, :]
                              ).then_inc(S("f_stored"), 16)

            def experts(l):
                first, R = load_rounds(act, l)

                def turned_x(r, i, c):
                    act.wait_ge(S("xT_pe"), job(r, i, c) + 1)
                    if not (isinstance(i, int) and 2 * i + c < 2):
                        act.wait_ge(S("up_pe"), job(r, i, c) - 1)
                    A(XT[:, c % 2, :, :], heads(flat(5, 1024), KD), ACT.Identity).then_inc(S("xT_act"), 1)

                def silu(r, i, c):
                    act.wait_ge(S("gate_pe"), job(r, i, c) + 1)
                    if not (isinstance(i, int) and 2 * i + c == 0):
                        act.wait_ge(S("hp_dve"), job(r, i, c))
                    A(hs, ps[:, 0, :], ACT.Silu).then_inc(S("hs_act"), 1)

                def turned_h(r, i, c):
                    act.wait_ge(S("hT_pe"), job(r, i, c) + 1)
                    if not (isinstance(i, int) and 2 * i + c == 0):
                        act.wait_ge(S("dn_pe"), job(r, i, c))
                    A(hT[:, :, :], heads(ps[:, 2, :], 4), ACT.Identity).then_inc(S("hT_act"), 1)

                def store(r, i, c):
                    act.wait_ge(S("y_dve"), job(r, i, c) + 1)
                    e = i * 2 + c
                    dst = (rows_out[l][CAP * e:CAP * e + CAP, :] if isinstance(e, int)
                           else rows_out[l][bass.ds(e * CAP, CAP), :])
                    act.dma_start(dst, Yb[:, c % 2, :]).then_inc(S(f"stored{c % 2}"), 16)

                def pair(r, i, first, last):
                    for c in range(2):
                        silu(r, i, c)
                        if not (first and c == 0):
                            turned_h(r, i, c - 1)
                        if not (last and c == 1):
                            turned_x(r, i, c + 1)
                        if not (first and c == 0):
                            store(r, i, c - 1)

                with act.Fori(0, R) as n_round:
                    r = n_round + first
                    act.wait_ge(S("round_dve"), r + 1)
                    turned_x(r, 0, 0)
                    pair(r, 0, True, False)
                    with act.Fori(1, NE // 2 - 1) as i:
                        pair(r, i, False, False)
                    pair(r, NE // 2 - 1, False, True)
                    turned_h(r, NE // 2 - 1, 1)
                    store(r, NE // 2 - 1, 1)

            for l in range(DEPTH):
                if l == 0:
                    act.wait_ge(S("ld_h0"), 16)
                    act.wait_ge(S("ld_h1"), 16)
                square_rows(l, "a", range(NT))
                if l == 0:
                    mod_rows(0, range(mod_units(0)))
                norm_evac(l, "a", range(NT))
                project(l)
                softplus(l)
                turn_scan_operands(l)
                na_norm(l)
                scan(l)
                attention(l)
                mixT(l)
                gate_rows(l, 0)
                square_rows(l, "f", tiles(l))
                gate_rows(l, 1)
                norm_evac(l, "f", tiles(l))
                affinities(l)
                turn_back(l)
                experts(l)

        @block.vector
        def _(dve):
            V = nc.vector
            chain = [0]

            def link(ins):
                chain[0] += 1
                ins.then_inc(S("dve_chain"), 1)
                dve.wait_ge(S("dve_chain"), chain[0])

            def after(ins, name, l, n):
                ins.then_inc(S(name), 1)
                dve.wait_ge(S(name), upto(name, l, n))

            def modulation(l):
                dve.wait_ge(S("ld_colp"), 16 * DEPTH)
                dve.wait_ge(S("mod_turned"), upto("mod_turned", l, 1))
                parts = []
                for m in sorted({m for m, _ in STREAMS[l]}):
                    mine = [n for n, q in enumerate(STREAMS[l]) if q[0] == m]
                    b = 4 * STREAMS[l][mine[0]][1]
                    parts.append((m, b, b + 4 * len(mine), 4 * mine[0]))
                cols = heads(mod_columns(l), 48)
                for m, lo, hi, at in parts:
                    i = V.tensor_tensor(mod[:, m, lo:hi, :], cols[:, at:at + hi - lo, :],
                                        spread(colp[:, m, L_BMOD + lo:L_BMOD + hi], 2), ALU.add)
                after(i, "mod_evac", l, 1)
                for m, lo, hi, at in parts:
                    for which, c in ((0, L_NMIX), (1, L_NFFN)):
                        b = 24 * which + 8
                        if lo <= b < hi:
                            i = V.scalar_tensor_tensor(modA[:, m, which, :, :], mod[:, m, b:b + 8, :], 1.0,
                                                       spread(colp[:, m, c:c + 8], 2), ALU.add, ALU.mult)
                i.then_inc(S("modA"), 1)

            def norm_rows(l, which, ts):
                n = len(ts)
                a = slice(ts[0], ts[0] + n)
                dve.wait_ge(S(which + "_sq"), upto(which + "_sq", l, n))
                V.tensor_scalar(stat2[:, a], stat[:, a], 1.0 / D, EPS, ALU.mult, ALU.add
                                ).then_inc(S(which + "_ms"), 1)
                dve.wait_ge(S(which + "_rs"), upto(which + "_rs", l, 1))
                for t in ts:
                    V.tensor_scalar(tokA[:, t, :], h[:, t, :], stat2[:, t:t + 1], None, ALU.mult
                                    ).then_inc(S(which + "_hn"), 1)

            def norm_evac(l, which):
                m = 0 if which == "a" else 1
                dve.wait_ge(S("modA"), upto("modA", l + m, 1))
                for k in range(1, KD, 2):
                    dve.wait_ge(S(which + "_tr"), upto(which + "_tr", l, k + 1))
                    for seg in (segs(l) if which == "f" else [0, 1]):
                        c = slice(CTX * seg, CTX * seg + CTX)
                        i = V.tensor_scalar(featT[:, k, c], ps[:, 1 + k % 4, c], modA[:, l, m, k, seg:seg + 1],
                                            mod[:, l, 24 * m + k, seg:seg + 1], ALU.mult, ALU.add)
                    i.then_inc(S(which + "_evac_dve"), 1)

            def project(l):
                jobs = in_jobs(l)
                for n, (name, kind, i, eng) in enumerate(jobs):
                    if eng != "D":
                        continue
                    dve.wait_ge(S("in_pe"), upto("in_pe", l, n + 1))
                    bank = ps[:, n % 4, :]
                    if kind == "dt":
                        dve.wait_ge(S("ld_rowp"), upto("ld_rowp", l, 16))
                        V.tensor_tensor(dtr.rearrange("p (t d) h -> p t (d h)", t=NT), heads(bank[:, 0:64], NT),
                                        repeat(rowp[:, R_DTB:R_DTB + 16], NT), ALU.add).then_inc(S("in_dve"), 1)
                        dve.wait_ge(S("in_dve"), upto("in_dve", l, 1))
                        V.scalar_tensor_tensor(dta[:, :, :], dtr[:, :, :], -1.0, dtr[:, :, :], ALU.mult, ALU.max
                                               ).then_inc(S("dt_abs"), 1)
                        convolve(l)
                        continue
                    lo, hi = cols_needed(l, name, i)
                    dst = {"ret_qk": qk, "na_qk": nqk, "na_v": nav}[name]
                    V.tensor_copy(dst[:, i, lo:hi], bank[:, lo:hi]).then_inc(S("in_dve"), 1)
                    if (name, i) == ("na_qk", NT - 1):
                        log_decays(l)
                        ret_triangle(l)
                        na_squares(l)
                        chunk_weights(l)
                        mask_bias(l)

            def convolve(l):
                for n, f in enumerate((4, 5, 0, 1, 2, 3)):
                    dve.wait_ge(S("in_act"), upto("in_act", l, n + 1))
                    full = l < DEPTH - 1 or f != 5
                    dst = heads(xT[:, f, :] if f < 4 else BCT[:, f - 4, :], 2)
                    sg = slice(0, 2) if full else slice(1, 2)
                    w = [colp[:, l, L_CW + 3 * f + j:L_CW + 3 * f + j + 1] for j in range(3)]
                    src = [xpad[:, f, sg, j:j + CTX] for j in range(3)]
                    link(V.tensor_scalar(dst[:, sg, :], src[0], w[0], colp[:, l, L_CB + f:L_CB + f + 1],
                                         ALU.mult, ALU.add))
                    link(V.scalar_tensor_tensor(dst[:, sg, :], src[1], w[1], dst[:, sg, :], ALU.mult, ALU.add))
                    V.scalar_tensor_tensor(dst[:, sg, :], src[2], w[2], dst[:, sg, :], ALU.mult, ALU.add
                                           ).then_inc(S("conv_dve"), 1)

            def na_squares(l):
                ts = tiles(l)
                for t in range(NT):
                    lo = 0 if t in ts else 4
                    dve.wait_ge(S("na_sq"), upto("na_sq", l, t + 1))
                    V.tensor_reduce(rs[:, t, lo:8], heads(sq, 8)[:, lo:8, :], AX.X, ALU.add
                                    ).then_inc(S("na_ss"), 1)
                dve.wait_ge(S("na_ss"), upto("na_ss", l, NT))
                V.tensor_scalar(rs[:, :, 4:8], rs[:, :, 4:8], 1.0 / HD, EPS, ALU.mult, ALU.add)
                V.tensor_scalar(rs[:, ts[0]:NT, 0:4], rs[:, ts[0]:NT, 0:4], 1.0, HD * EPS, ALU.mult, ALU.add
                                ).then_inc(S("na_ms"), 1)

            def na_scale(l):
                dve.wait_ge(S("na_rs"), upto("na_rs", l, 1))
                for t in range(NT):
                    lo = 0 if t in tiles(l) else 4
                    v = heads(nqk[:, t, :], 8)[:, lo:8, :]
                    link(V.tensor_tensor(v, v, spread(rs[:, t, lo:8], HD), ALU.mult))
                    V.tensor_tensor(v, v, heads(rowp[:, R_NQK:R_NQK + 512], 8)[:, lo:8, :], ALU.mult
                                    ).then_inc(S("na_norm"), 1)

            def log_decays(l):
                dve.wait_ge(S("nA_act"), upto("nA_act", l, 1))
                link(V.memset(DTX[:, :, :], SCALE))
                n6 = nA.rearrange("p d (g h) -> p (d g) h", g=2)
                V.tensor_scalar(n6[:, :, 0:4], n6[:, :, 0:4], -1.0, None, ALU.mult)
                link(V.tensor_scalar(n6[:, :, 4:6], n6[:, :, 4:6], -1.0 / SCALE, None, ALU.mult))
                dve.wait_ge(S("dt_ln"), upto("dt_ln", l, 1))
                by6 = DTX.rearrange("p a (g h) -> p (a g) h", g=2)[:, :, 0:4]
                by4 = [v.rearrange("p a (g h) -> p (a g) h", g=2) for v in (dtr, dta)]
                link(V.scalar_tensor_tensor(by6, by4[0], 0.0, by4[1], ALU.max, ALU.add))
                V.tensor_tensor(Aall.rearrange("p (t d) h -> p t (d h)", t=NT),
                                DTX.rearrange("p (t d) h -> p t (d h)", t=NT),
                                repeat(nA.rearrange("p d h -> p (d h)"), NT), ALU.mult).then_inc(S("loga"), 1)
                dve.wait_ge(S("loga"), upto("loga", l, 1))

            def ret_triangle(l):
                dve.wait_ge(S("x_evac"), upto("x_evac", l, 5))
                V.tensor_tensor(*triangle_rows(rf[:, 0:RET_H, :], ret(Aall[:, 0, :]), 2, LE), ALU.mult
                                ).then_inc(S("rf_dve"), 1)

            def triangle(l, n):
                t = tiles(l)[n]
                dve.wait_ge(S("seg_pe"), upto("seg_pe", l, n + 1))
                V.tensor_tensor(*triangle_rows(rf, ssd(Aall[:, 2 * t, :]), 4, LE), ALU.mult
                                ).then_inc(S("rf_dve"), 1)

            def chunk_weights(l):
                dve.wait_ge(S("ex_act"), upto("ex_act", l, 1))
                for d in range(2):
                    V.tensor_tensor(Wt[:, d, :, :], heads(EX[:, 96 + 48 * d:144 + 48 * d], NT),
                                    DTX[:, d:2 * NT:2, :], ALU.mult)
                T = heads(EX[:, 192:288], 2 * NT)
                V.tensor_copy(Dec[0:64, :, :], T[0:64, :, 0:6])
                link(V.tensor_copy(Dec[64:128, :, :], T[64:128, :, 6:12]))

            def ret_decays(l):
                dve.wait_ge(S("e_act"), upto("e_act", l, 1))
                link(V.tensor_tensor(Eret[:, :, :], Eret[:, :, :], repeat(const[:, C_DRET:C_DRET + P], RET_H), ALU.mult))

            def states(l):
                def weigh(n):
                    d, t = STATE_STEPS[n]
                    if n > 0:
                        dve.wait_ge(S("st_pe"), upto("st_pe", l, n))
                    V.tensor_tensor(VW[:, :, :], heads(XV[:, t, :], NH), spread(Wt[:, d, t, :], HD), ALU.mult
                                    ).then_inc(S("vw_dve"), 1)

                weigh(0)
                for n, (d, t) in enumerate(STATE_STEPS):
                    if n + 1 < len(STATE_STEPS):
                        weigh(n + 1)
                    else:
                        dve.wait_ge(S("st_pe"), upto("st_pe", l, n + 1))
                    bank = ps[:, 3 + n % 2, 0:384]
                    new = Hs[:, d, STATE_NEXT[d, t], :]
                    if n < 2:
                        V.tensor_copy(new, bank).then_inc(S("h_dve"), 1)
                    else:
                        if n == 2:
                            dve.wait_ge(S("h_dve"), upto("h_dve", l, 2))
                        else:
                            dve.wait_ge(S("h_dve"), upto("h_dve", l, n - 1))
                        link(V.tensor_tensor(heads(new, 6), heads(Hs[:, d, t, :], 6),
                                             spread(Dec[:, 2 * t + d, :], HD), ALU.mult))
                        V.tensor_tensor(new, new, bank, ALU.add).then_inc(S("h_dve"), 1)

            def scan_head(l, n):
                dve.wait_ge(S("sc_pe"), upto("sc_pe", l, n + 1))
                if n > 0:
                    dve.wait_ge(S("mb_pool"), upto("mb_pool", l, 2 * n))
                    dve.wait_ge(S("mf_dve"), upto("mf_dve", l, 2 * n))
                s = ps[:, 6:8, 0:P]
                V.tensor_tensor(sL[:, :, :], s, repeat(GE, 2), ALU.mult).then_inc(S("sl_dve"), 1)
                link(V.tensor_tensor(sU[:, :, :], s, repeat(LE, 2), ALU.mult))
                if n > 0:
                    dve.wait_ge(S("y_pe"), upto("y_pe", l, n))
                two = lambda v: v.rearrange("p (g h) c -> p g (h c)", g=2)
                V.tensor_tensor(two(Mret), two(Eret), ps[:, 6:8, P:3 * P], ALU.mult
                                ).then_inc(S("mret_dve"), 1)
                dve.wait_ge(S("e_act"), upto("e_act", l, n + 2))
                for g in range(2):
                    if n > 0:
                        dve.wait_ge(S("diag_pe"), upto("diag_pe", l, 2 * n - 1 + g))
                    V.tensor_tensor(Mf[:, g, :, :], E[:, 4 * g:4 * g + 4, :], repeat(sU[:, g, :], 4), ALU.mult
                                    ).then_inc(S("mf_dve"), 1)
                if n + 1 < len(tiles(l)):
                    triangle(l, n + 1)

            def scan_sum(l, n):
                t = tiles(l)[n]
                dve.wait_ge(S("y_pe"), upto("y_pe", l, n + 1))
                ds = dirs_of(t)
                places = lambda v: v.rearrange("p (g h) c -> p g h c", g=2)
                for k, d in enumerate(ds):
                    at = 48 * d + NH * t
                    link(V.tensor_tensor(places(y if k == 0 else y2), scan_outs(1 + d),
                                         spread2(heads(EX[:, at:at + NH], 2), HD), ALU.mult))
                after(V.tensor_tensor(places(y), places(y), scan_outs(0), ALU.add), "comb_dve", l, n + 1)
                if len(ds) == 2:
                    link(V.tensor_tensor(y[:, :, :], y[:, :, :], y2[:, :, :], ALU.add))

            def scan_tail(l, n):
                t = tiles(l)[n]
                ys, y2s = ssd(line(y), HD), ssd(line(y2), HD)
                dve.wait_ge(S("dx_pool"), upto("dx_pool", l, n + 1))
                link(V.tensor_tensor(ys, ys, heads(line(dx), 2), ALU.add))
                V.tensor_tensor(y2s, ys, heads(tokA[:, t, 256:768], 2), ALU.mult).then_inc(S("yz_dve"), 1)
                four = lambda v: v.rearrange("p g (h c) -> p g h c", h=2)
                yr, sqr = four(ret(line(y), HD)), four(ret(line(y2), HD))
                mu, var = heads(stat2[:, 8:12], 2), heads(stat2[:, 16:20], 2)
                link(V.tensor_reduce(mu, yr, AX.X, ALU.add))
                link(V.tensor_scalar(mu, mu, -1.0 / HD, None, ALU.mult))
                link(V.tensor_tensor(yr, yr, spread2(mu, HD), ALU.add))
                link(V.tensor_tensor(sqr, yr, yr, ALU.mult))
                link(V.tensor_reduce(var, sqr, AX.X, ALU.add))
                V.tensor_scalar(var, var, 1.0 / HD, EPS, ALU.mult, ALU.add)
                dve.wait_ge(S("yss_act"), upto("yss_act", l, n + 1))
                V.tensor_scalar(stat2[:, 20:21], stat[:, 8 + n:9 + n], 1.0 / (SSD_H * HD), EPS, ALU.mult, ALU.add
                                ).then_inc(S("gn_ms"), 1)
                dve.wait_ge(S("gn_rs"), upto("gn_rs", l, n + 1))
                V.scalar_tensor_tensor(heads(tokA[:, t, 256:768], 2), y2s, stat2[:, 20:21],
                                       heads(rowp[:, R_NORM:R_NORM + 512], 2), ALU.mult, ALU.mult)
                link(V.tensor_tensor(yr, yr, spread2(var, HD), ALU.mult))
                g = tokA[:, t, 0:256].rearrange("p (j g c) -> p g j c", j=2, g=2)
                link(V.tensor_tensor(g, yr, g, ALU.mult))

            def scan(l):
                states(l)
                triangle(l, 0)
                ret_decays(l)
                scan_head(l, 0)
                for n in range(len(tiles(l))):
                    scan_sum(l, n)
                    if n + 1 < len(tiles(l)):
                        scan_head(l, n + 1)
                    scan_tail(l, n)

            def mask_bias(l):
                dve.wait_ge(S("ld_bias"), upto("ld_bias", l, 16 * 2 * NA_H))
                b = bias.rearrange("p a b c -> p (a b) c")
                V.tensor_tensor(b, b, repeat(const[:, C_MASK:C_MASK + GRID], NA_H * 6), ALU.add
                                ).then_inc(S("bias_dve"), 1)

            def attention(l):
                un = att_units(l)

                def maximum(n):
                    keys = TOK if un[n][0] >= 2 else CTX
                    dve.wait_ge(S("s_pe"), upto("s_pe", l, n + 1))
                    V.tensor_reduce(nmx[:, n:n + 1], ps[:, n % 2, 0:keys], AX.X, ALU.max, negate=True
                                    ).then_inc(S("mx_dve"), 1)

                def turned(n):
                    nk = NT if un[n][0] >= 2 else 2
                    dve.wait_ge(S("pt_pe"), upto("pt_pe", l, n + 1))
                    if n >= 2:
                        dve.wait_ge(S("pv_pe"), upto("pv_pe", l, n - 1))
                    V.tensor_copy(PT[:, n % 2, 0:nk, :], heads(ps[:, 2 + n % 2, :], NT)[:, 0:nk, :]
                                  ).then_inc(S("pt_dve"), 1)

                def normalise(tile):
                    t = tiles(l)[tile]
                    c = slice(NA_H * tile, NA_H * tile + NA_H)
                    dve.wait_ge(S("pv_pe"), upto("pv_pe", l, NA_H * (tile + 1)))
                    link(V.reciprocal(nrec[:, c], nsum[:, c]))
                    o = V.tensor_tensor(heads(tokA[:, t, 768:1024], NA_H), heads(ps[:, 4 + 2 * (tile % 2), 0:256], NA_H),
                                        spread(nrec[:, c], HD), ALU.mult)
                    o.then_inc(S("na_out"), 1)

                N = len(un)
                maximum(0)
                for n in range(N):
                    if n + 1 < N:
                        maximum(n + 1)
                    if n >= 1 and n % NA_H == 0:
                        normalise(n // NA_H - 1)
                    turned(n)
                normalise(N // NA_H - 1)

            def gate_diag(l, which):
                for seg in segs(l):
                    c = 24 * which + 16
                    V.tensor_tensor(heads(diag[:, seg, :], KD), repeat(ident, KD),
                                    spread(mod[:, l, c:c + 8, seg], P), ALU.mult).then_inc(S(f"diag{which}"), 1)

            def residual(l):
                dve.wait_ge(S("row0"), upto("row0", l, len(segs(l))))
                gate_diag(l, 1)
                ts = tiles(l)
                n = 0
                for t in ts:
                    for half in range(N_OUT):
                        c = slice(512 * half, 512 * half + 512)
                        dve.wait_ge(S("out_pe"), upto("out_pe", l, n + 1))
                        link(V.tensor_tensor(Pm[:, n % 2, :], grow[:, t // 2, c], ps[:, 4 + n % 2, :], ALU.mult))
                        V.tensor_tensor(h[:, t, c], h[:, t, c], Pm[:, n % 2, :], ALU.add).then_inc(S("res_dve"), 1)
                        n += 1

            def route(l):
                ts = tiles(l)
                T = len(ts)
                t0 = ts[0]
                dve.wait_ge(S("ld_rb"), 16)
                dve.wait_ge(S("rt_tr"), upto("rt_tr", l, 1))
                se = sel.rearrange("p (t g) e -> p t (g e)", t=NT)[:, t0:NT, :]
                af = aff[:, t0:NT, :]
                link(V.tensor_copy(af, heads(ps[:, 1, NE * t0:NE * NT], T)))
                link(V.tensor_tensor(se, af, repeat(rb[:, :], T), ALU.add))
                s4 = sel[:, 4 * t0:4 * NT, :]
                fl = lambda v: v.rearrange("p t g -> p (t g)")[:, 4 * t0:4 * NT]
                a, b, c, d = fl(g1), fl(g2), fl(g3), fl(g4)
                e = [s4[:, :, j] for j in range(4)]
                link(V.tensor_tensor(a, e[0], e[1], ALU.add))
                link(V.tensor_tensor(b, e[2], e[3], ALU.add))
                link(V.tensor_tensor(a, a, b, ALU.max))
                link(V.tensor_tensor(b, e[0], e[1], ALU.max))
                link(V.tensor_tensor(c, e[2], e[3], ALU.max))
                link(V.tensor_tensor(b, b, c, ALU.add))
                link(V.tensor_tensor(a, a, b, ALU.max))

                def rank(v, n, out):
                    other = v.unsqueeze(2).to_broadcast([P, n, 4, 4])
                    own = v.unsqueeze(3).to_broadcast([P, n, 4, 4])
                    x1 = cmp1[:, 0:n, :].rearrange("p n (i j) -> p n i j", i=4)
                    x2 = cmp2[:, 0:n, :].rearrange("p n (i j) -> p n i j", i=4)
                    link(V.tensor_tensor(x1, other, own, ALU.is_gt))
                    link(V.tensor_tensor(x2, other, own, ALU.is_equal))
                    link(V.tensor_tensor(cmp2[:, 0:n, :], cmp2[:, 0:n, :],
                                         repeat(const[:, C_TRI:C_TRI + 16], n), ALU.mult))
                    link(V.tensor_tensor(cmp1[:, 0:n, :], cmp1[:, 0:n, :], cmp2[:, 0:n, :], ALU.add))
                    link(V.tensor_reduce(out, x1, AX.X, ALU.add))

                rank(g1[:, t0:NT, :], T, g4[:, t0:NT, :])
                link(V.tensor_scalar(d, d, 0.5, None, ALU.is_lt))
                cn = chosen[:, 0:4 * T, :]
                rank(s4, 4 * T, cn)
                link(V.tensor_scalar(cn, cn, 1.5, None, ALU.is_lt))
                after(V.tensor_tensor(cn, cn, spread(d, 4), ALU.mult), "chosen_dve", l, 1)
                ga = gates[:, t0:NT, :]
                link(V.tensor_tensor(ga, af, cn.rearrange("p (t g) e -> p t (g e)", t=T), ALU.mult))
                link(V.tensor_reduce(rsum[:, t0:NT], ga, AX.X, ALU.add))
                link(V.reciprocal(rsum[:, t0:NT], rsum[:, t0:NT]))
                link(V.tensor_tensor(ga, ga, spread(rsum[:, t0:NT], NE), ALU.mult))

            def assign(l):
                ts = tiles(l)
                T, t0 = len(ts), ts[0]
                ch = chosen[:, 0:4 * T, :].rearrange("p (t g) e -> p t (g e)", t=T)
                pl, pk, tm = place[:, t0:NT, :], pick[:, t0:NT, :], tmp16[:, t0:NT, :]
                dve.wait_ge(S("pos_pe"), upto("pos_pe", l, 1))
                sums = tmp16[:, 0:T, :]
                link(V.tensor_copy(sums, heads(ps[:, 2, 0:NE * T], T)))
                for n in range(1, T):
                    link(V.tensor_tensor(sums[:, n, :], sums[:, n, :], sums[:, n - 1, :], ALU.add))
                count = sums[:, T - 1, :]
                link(V.tensor_reduce(few[:, 0:1], count, AX.X, ALU.max))
                link(V.tensor_scalar(few[:, 1:2], few[:, 0:1], float(CAP), 1.0, ALU.is_gt, ALU.add))
                for n in range(2, T):
                    link(V.tensor_scalar(few[:, 2:3], few[:, 0:1], float(n * CAP), None, ALU.is_gt))
                    link(V.tensor_tensor(few[:, 1:2], few[:, 1:2], few[:, 2:3], ALU.add))
                link(V.tensor_scalar(pl, heads(ps[:, 3, 0:NE * T], T), float(CAP + 4096), None, ALU.add))
                link(V.tensor_tensor(pl[:, 1:T, :], pl[:, 1:T, :], sums[:, 0:T - 1, :], ALU.add))
                link(V.tensor_tensor(pl, pl, ch, ALU.mult))
                link(V.tensor_scalar(pl, pl, -4096.0, None, ALU.add))
                V.tensor_copy(rounds[:, l:l + 1], few[:, 1:2]).then_inc(S("rounds_dve"), 1)
                dve.wait_ge(S("rounds_dve"), upto("rounds_dve", l, 1))

            def experts(l):
                ts = tiles(l)
                T, t0 = len(ts), ts[0]
                first, R = load_rounds(dve, l)

                def slots_of(r, i, c):
                    e = i * 2 + c
                    if not (isinstance(i, int) and e < 2):
                        dve.wait_ge(S("who_pe"), job(r, i, c) - 1)
                    col = place[:, t0:NT, e:e + 1] if isinstance(e, int) else place[:, t0:NT, bass.ds(e, 1)]
                    hot = onehot[:, 0:T, :]
                    if not (isinstance(i, int) and e < 1):
                        dve.wait_ge(S("onehot_dve"), job(r, i, c))
                    V.tensor_tensor(hot, repeat(const[:, C_IOTA:C_IOTA + P], T),
                                    col.to_broadcast([P, T, P]), ALU.is_equal).then_inc(S("hot_steps"), 1)
                    dve.wait_ge(S("hot_steps"), job(r, i, c) * 2 + 1)
                    V.tensor_tensor(hot, hot, spread(const[:, C_TOK:C_TOK + T], P), ALU.mult
                                    ).then_inc(S("hot_steps"), 1)
                    dve.wait_ge(S("hot_steps"), job(r, i, c) * 2 + 2)
                    V.tensor_reduce(owner[:, c % 2, :], hot.rearrange("p t s -> p s t"), AX.X, ALU.add
                                    ).then_inc(S("onehot_dve"), 1)

                def who(r, i, c):
                    dve.wait_ge(S("who_pe"), job(r, i, c) + 1)
                    if not (isinstance(i, int) and 2 * i + c < 2):
                        dve.wait_ge(S(f"gathered{c % 2}"), (r * (NE // 2) + (i + c // 2)) * 16)
                    V.tensor_copy(slot_i[:, c % 2:c % 2 + 1], ps[:, 7, 0:1]).then_inc(S("who_dve"), 1)

                def product(r, i, c):
                    dve.wait_ge(S("hs_act"), job(r, i, c) + 1)
                    dve.wait_ge(S("up_pe"), job(r, i, c) + 1)
                    if not (isinstance(i, int) and 2 * i + c == 0):
                        dve.wait_ge(S("hT_pe"), job(r, i, c))
                    V.tensor_tensor(hp, hs, ps[:, 1, :], ALU.mult).then_inc(S("hp_dve"), 1)

                def result(r, i, c):
                    dve.wait_ge(S("dn_pe"), job(r, i, c) + 1)
                    if not (isinstance(i, int) and 2 * i + c < 2):
                        dve.wait_ge(S(f"stored{c % 2}"), (r * (NE // 2) + (i - (c < 0))) * 16)
                    V.tensor_copy(Yb[:, c % 2, :], flat(3, 1024)).then_inc(S("y_dve"), 1)

                def pair(r, i, first, last):
                    for c in range(2):
                        if not last:
                            slots_of(r, i, c + 2)
                        product(r, i, c)
                        if not last:
                            who(r, i, c + 2)
                        if not (first and c == 0):
                            result(r, i, c - 1)

                def rows_of_round(r):
                    STEPS = 20
                    counted = [0]

                    def step(ins):
                        counted[0] += 1
                        ins.then_inc(S("row_steps"), 1)
                        dve.wait_ge(S("row_steps"), r * STEPS + counted[0])

                    ch = chosen[:, 0:4 * T, :].rearrange("p (t g) e -> p t (g e)", t=T)
                    pl, pk, tm = place[:, t0:NT, :], pick[:, t0:NT, :], tmp16[:, t0:NT, :]
                    ex = repeat(const[:, C_EXP:C_EXP + NE], T)
                    step(V.tensor_tensor(tm, ch, ex, ALU.mult))
                    step(V.tensor_reduce(first2[:, 0, t0:NT], tm, AX.X, ALU.max))
                    step(V.tensor_tensor(pk, spread(first2[:, 0, t0:NT], NE), ex, ALU.is_equal))
                    for n in range(2):
                        if n == 1:
                            step(V.tensor_tensor(pk, ch, pk, ALU.subtract))
                            step(V.tensor_tensor(tm, pk, ex, ALU.mult))
                            step(V.tensor_reduce(first2[:, 1, t0:NT], tm, AX.X, ALU.add))
                        step(V.tensor_tensor(tm, pk, pl, ALU.mult))
                        step(V.tensor_reduce(pos2[:, n, t0:NT], tm, AX.X, ALU.add))
                        step(V.tensor_tensor(tm, pk, gates[:, t0:NT, :], ALU.mult))
                        step(V.tensor_reduce(gate2[:, n, t0:NT], tm, AX.X, ALU.add))
                    p, f, w, m = (v[:, :, t0:NT] for v in (pos2, first2, row2, inround))
                    step(V.tensor_scalar(w, p, float(CAP), None, ALU.is_lt))
                    step(V.tensor_scalar(m, p, 0.0, None, ALU.is_ge))
                    step(V.tensor_tensor(m, m, w, ALU.mult))
                    step(V.scalar_tensor_tensor(w, p, -float(NO_ROW), f, ALU.add, ALU.add))
                    step(V.tensor_tensor(w, w, m, ALU.mult))
                    step(V.tensor_scalar(w, w, float(NO_ROW), None, ALU.add))
                    assert counted[0] == STEPS
                    V.tensor_copy(row_i[:, :, t0:NT], w).then_inc(S("row_dve"), 1)

                def add_rows(n_round, lo, hi):
                    for q in range(lo, hi):
                        n, t = sum_order(l)[q]
                        dve.wait_ge(X(f"back{q % 4}", l), backs(l, q, n_round))
                        if q >= T:
                            dve.wait_ge(X("acc_dve", l), n_round * (2 * T) + (q - T + 1))
                        V.scalar_tensor_tensor(tokA[:, t0 + t, :], back[q % 4], gate2[:, n, t0 + t:t0 + t + 1],
                                               tokA[:, t0 + t, :], ALU.mult, ALU.add).then_inc(X("acc_dve", l), 1)

                dve.wait_ge(S("row1"), upto("row1", l, len(segs(l))))
                with dve.Fori(0, R) as n_round:
                    r = n_round + first
                    pl = place[:, t0:NT, :]
                    V.tensor_scalar(pl, pl, -float(CAP), None, ALU.add).then_inc(S("round_dve"), 1)
                    dve.wait_ge(S("round_dve"), r + 1)
                    for c in range(2):
                        slots_of(r, 0, c)
                        who(r, 0, c)
                    rows_of_round(r)
                    pair(r, 0, True, False)
                    with dve.Fori(1, NE // 2 - 1) as i:
                        pair(r, i, False, False)
                    pair(r, NE // 2 - 1, False, True)
                    result(r, NE // 2 - 1, 1)
                    dve.wait_ge(S("acc_zero"), upto("acc_zero", l, 1))
                    add_rows(n_round, 0, 2 * T)
                    dve.wait_ge(X("acc_dve", l), n_round * (2 * T) + 2 * T)
                for n, t in enumerate(ts):
                    V.tensor_tensor(tokA[:, t, :], tokA[:, t, :], grow[:, t // 2, :], ALU.mult
                                    ).then_inc(S("ffn_dve"), 1)
                    if n % 2 == 1:
                        dve.wait_ge(S("ffn_dve"), upto("ffn_dve", l, n + 1))
                        V.tensor_tensor(h[:, t, :], h[:, t, :], tokA[:, t, :], ALU.add).then_inc(S("h_end1"), 1)

            dve.wait_ge(S("ld_const"), 16)
            for l in range(DEPTH):
                norm_rows(l, "a", range(NT))
                if l == 0:
                    modulation(0)
                norm_evac(l, "a")
                project(l)
                na_scale(l)
                scan(l)
                attention(l)
                modulation(l + 1)
                gate_diag(l, 0)
                residual(l)
                norm_rows(l, "f", tiles(l))
                norm_evac(l, "f")
                route(l)
                assign(l)
                experts(l)

        @block.gpsimd
        def _(pool):
            G = nc.gpsimd
            chain = [0]

            def link(ins):
                chain[0] += 1
                ins.then_inc(S("pool_chain"), 1)
                pool.wait_ge(S("pool_chain"), chain[0])

            def rsqrt(v, n):
                return G.tensor_tensor(v, v, pw[:, 0:n], ALU.pow)

            def rope(l):
                for n, t in enumerate((2, 3)):
                    pool.wait_ge(S("in_dve"), upto("in_dve", l, dve_jobs_done(l, "ret_qk", t)))
                    v = heads(qk[:, t, :], 8)
                    a = heads(y.rearrange("p a b -> p (a b)")[:, 0:512], 8)
                    b = heads(y2.rearrange("p a b -> p (a b)")[:, 0:512], 8)
                    cos = const[:, C_COS + 64 * n:C_COS + 64 * n + 64]
                    sin = heads(const[:, C_SIN + 64 * n:C_SIN + 64 * n + 64], 2)
                    link(G.tensor_tensor(a, v, repeat(cos, 8), ALU.mult))
                    for half in range(2):
                        o, s = slice(16 * half, 16 * half + 16), slice(16 - 16 * half, 32 - 16 * half)
                        parts = lambda w, c: w.rearrange("p a (b c) -> p a b c", b=2)[:, :, :, c]
                        link(G.tensor_tensor(parts(b, o), parts(v, s),
                                             sin[:, :, o].unsqueeze(1).to_broadcast([P, 8, 2, 16]), ALU.mult))
                    G.tensor_tensor(v, a, b, ALU.add).then_inc(S("rope"), 1)
                    pool.wait_ge(S("rope"), upto("rope", l, n + 1))

            def triangle(l, n):
                if n < 0:
                    pool.wait_ge(S("loga"), upto("loga", l, 1))
                    pool.wait_ge(S("x_evac"), upto("x_evac", l, 5))
                    G.tensor_tensor(*triangle_rows(rbk[:, 0:RET_H, :], ret(Aall[:, 1, :]), 2, GE), ALU.mult
                                    ).then_inc(S("rb_pool"), 1)
                    return
                t = tiles(l)[n]
                pool.wait_ge(S("seg_pe"), upto("seg_pe", l, n + 1))
                G.tensor_tensor(*triangle_rows(rbk, ssd(Aall[:, 2 * t + 1, :]), 4, GE), ALU.mult
                                ).then_inc(S("rb_pool"), 1)

            def scan_head(l, n):
                t = tiles(l)[n]
                if n > 0:
                    pool.wait_ge(S("diag_pe"), upto("diag_pe", l, 2 * n))
                v = ssd(XV[:, t, :], HD).rearrange("p g (h c) -> p g h c", h=4)
                by_group = lambda w: w.rearrange("p (g h) c -> p g h c", g=2)
                G.tensor_tensor(by_group(Vf), v, spread2(ssd(DTX[:, 2 * t, :]), HD), ALU.mult)
                G.tensor_tensor(by_group(Vb), v, spread2(ssd(DTX[:, 2 * t + 1, :]), HD), ALU.mult
                                ).then_inc(S("v_pool"), 1)
                pool.wait_ge(S("sl_dve"), upto("sl_dve", l, n + 1))
                pool.wait_ge(S("e_act"), upto("e_act", l, n + 2))
                for g in range(2):
                    G.tensor_tensor(Mb[:, g, :, :], E[:, 4 * g:4 * g + 4, :], repeat(sL[:, g, :], 4), ALU.mult
                                    ).then_inc(S("mb_pool"), 1)
                if n + 1 < len(tiles(l)):
                    triangle(l, n + 1)

            def scan_tail(l, n):
                t = tiles(l)[n]
                if n > 0:
                    pool.wait_ge(S("yz_dve"), upto("yz_dve", l, n))
                G.tensor_tensor(dx.rearrange("p (g h) c -> p g h c", g=2),
                                ssd(XV[:, t, :], HD).rearrange("p g (h c) -> p g h c", h=4),
                                spread2(heads(rowp[:, R_D:R_D + SSD_H], 2), HD), ALU.mult).then_inc(S("dx_pool"), 1)
                pool.wait_ge(S("gn_ms"), upto("gn_ms", l, n + 1))
                rsqrt(stat2[:, 16:21], 5).then_inc(S("gn_rs"), 1)

            def experts(l):
                ts = tiles(l)
                T, t0 = len(ts), ts[0]
                first, R = load_rounds(pool, l)

                def step_on():
                    pool.sem_inc(S("pool_steps"), 1)

                def gather(r, i, c):
                    pool.wait_ge(S("who_dve"), job(r, i, c) + 1)
                    if not isinstance(i, int):
                        pool.wait_ge(S("xT_pe"), job(r, i, c) - 1)
                    step_on()
                    G.indirect_dma_start(gathered[c], None, rows_in[l], bass.IndirectOffsetOnAxis(slot_i[:, c:c + 1], 0)
                                         ).then_inc(S(f"gathered{c}"), 16)

                pool.wait_ge(S("f_stored"), upto("f_stored", l, 16))
                G.memset(tokA[:, t0:NT, :], 0.0).then_inc(S("acc_zero"), 1)
                pool.wait_ge(S("row1_pe"), upto("row1_pe", l, 1))
                with pool.Fori(0, R) as n_round:
                    r = n_round + first
                    pool.wait_ge(S("round_dve"), r + 1)
                    for c in range(2):
                        gather(r, 0, c)
                    with pool.Fori(1, NE // 2) as i:
                        for c in range(2):
                            gather(r, i, c)
                    pool.wait_ge(S("row_dve"), r + 1)
                    pool.wait_ge(S("up_pe"), job(r, NE // 2))
                    for c in range(2):
                        pool.wait_ge(S(f"stored{c}"), (r + 1) * (NE // 2) * 16)
                    step_on()
                    pool.wait_ge(X("no_row", l), 16)
                    for q, (n, t) in enumerate(sum_order(l)):
                        if q >= 4:
                            pool.wait_ge(X("acc_dve", l), n_round * (2 * T) + (q - 3))
                            step_on()
                        G.indirect_dma_start(back[q % 4], None, rows_out[l],
                                             bass.IndirectOffsetOnAxis(row_i[:, n, t0 + t:t0 + t + 1], 0)
                                             ).then_inc(X(f"back{q % 4}", l), 16)
                for n in range(0, T, 2):
                    pool.wait_ge(S("ffn_dve"), upto("ffn_dve", l, n + 1))
                    G.tensor_tensor(h[:, t0 + n, :], h[:, t0 + n, :], tokA[:, t0 + n, :], ALU.add
                                    ).then_inc(S("h_end0"), 1)

            G.memset(zero8[:, :], 0.0).then_inc(S("zero_pool"), 1)
            link(G.memset(pw[:, :], -0.5))
            pool.wait_ge(S("ld_const"), 16)
            for l in range(DEPTH):
                ts = tiles(l)
                if l > 0:
                    for w in ("h_end0", "h_end1"):
                        pool.wait_ge(S(w), upto(w, l - 1, len(tiles(l - 1)) // 2))
                for c in (0, CTX + 1):
                    i = G.memset(xpad[:, :, :, c:c + 1], 0.0)
                i.then_inc(S("pad_zero"), 1)
                pool.wait_ge(S("a_ms"), upto("a_ms", l, 1))
                rsqrt(stat2[:, 0:NT], NT).then_inc(S("a_rs"), 1)
                rope(l)
                pool.wait_ge(S("na_ms"), upto("na_ms", l, 1))
                G.tensor_tensor(rs[:, :, 4:8], rs[:, :, 4:8], pw[:, 0:16].rearrange("p (a b) -> p a b", a=NT), ALU.pow)
                G.tensor_tensor(rs[:, ts[0]:NT, 0:4], rs[:, ts[0]:NT, 0:4],
                                pw[:, 0:4 * len(ts)].rearrange("p (a b) -> p a b", b=4), ALU.pow
                                ).then_inc(S("na_rs"), 1)
                triangle(l, -1)
                triangle(l, 0)
                pool.wait_ge(S("ld_rowp"), upto("ld_rowp", l, 16))
                scan_head(l, 0)
                for n in range(len(ts)):
                    if n + 1 < len(ts):
                        scan_head(l, n + 1)
                    scan_tail(l, n)
                pool.wait_ge(S("f_ms"), upto("f_ms", l, 1))
                rsqrt(stat2[:, ts[0]:NT], len(ts)).then_inc(S("f_rs"), 1)
                experts(l)


_RAW = ["x", "ctx", "w_mod", "w_in", "w_out", "na_rpb", "router_w", "router_b", "w_gate", "w_up", "w_down"]


def _layout(i):
    a = {k: np.ascontiguousarray(np.asarray(i[k])) for k in _RAW}
    a["x"], a["ctx"] = a["x"][0], a["ctx"][0]
    a["consts"] = shape_constants()
    col = lambda v: v.reshape(v.shape[0], -1, P).transpose(0, 2, 1)
    c = np.stack([np.asarray(i["c"])[0], np.asarray(i["c_ctx"])])[::-1]
    a["condT"] = np.ascontiguousarray(c.reshape(2, KD, P).transpose(2, 1, 0))
    cw = np.asarray(i["ssd_conv_w"])
    cw = cw.reshape(DEPTH, 3, 6, P).transpose(0, 3, 2, 1).reshape(DEPTH, P, 18)
    a["colp"] = np.ascontiguousarray(np.concatenate(
        [col(np.asarray(i["b_mod"])), col(np.asarray(i["norm_mix"])), col(np.asarray(i["norm_ffn"])), cw,
         col(np.asarray(i["ssd_conv_b"]))], axis=2))
    g = lambda k: np.asarray(i[k])
    qn = np.broadcast_to(g("na_q_norm")[:, None], (DEPTH, NA_H, HD)).reshape(DEPTH, -1)
    kn = np.broadcast_to(g("na_k_norm")[:, None], (DEPTH, NA_H, HD)).reshape(DEPTH, -1)

    def placed(d):
        s, r = g("ssd_a_log_" + d), g("ret_decay_" + d)
        return np.concatenate([s[:, 0:4], r[:, 0::2], s[:, 4:8], r[:, 1::2]], axis=1)

    a["rowp"] = np.ascontiguousarray(np.concatenate(
        [g("ssd_dt_bias_f"), g("ssd_dt_bias_b"), placed("f"), placed("b"), g("ssd_d"), qn, kn, g("ssd_norm")], axis=1))
    return a


def kernel(**inputs):
    import concourse.bacc as _bacc
    from concourse.bass_utils import run_bass_kernel_spmd as _run

    nc = _bacc.Bacc("TRN2", target_bir_lowering=False, num_devices=1)
    arrays = {f"in_{k}": v for k, v in _layout(inputs).items()}
    ins = {k[3:]: nc.dram_tensor(k, v.shape, mybir.dt.from_np(v.dtype), kind="ExternalInput").ap()
           for k, v in arrays.items()}
    out = nc.dram_tensor("out_0", (SEQ, D), F32, kind="ExternalOutput").ap()
    trunk(nc, ins, out)
    r = _run(nc, [arrays], core_ids=[0])
    return r.results[0]["out_0"].reshape(1, SEQ, D)
```
